# Optimizing a Trainium2 kernel written in Bass

```python
import math
import jax, jax.numpy as jnp
from jax import lax
import numpy as np

D_MODEL = 1024
BATCH = 1
SEQ = 1024
DEPTH = 1
DEC_BATCH = 8
DEC_SEQ = 1
PAST_LEN = 8192
PAGE_SIZE = 128

D_MIX = D_MODEL
ATTN_WIDTH = D_MIX // 2
S5_WIDTH = D_MIX - ATTN_WIDTH
HEAD_DIM = 64
V_DIM = 2 * HEAD_DIM
N_HEADS = ATTN_WIDTH // V_DIM
ROT_DIM = HEAD_DIM // 4
ROPE_THETA = 500000.0
Q_BLOCK = 128
S5_GROUP = 16
S5_GROUPS = S5_WIDTH // S5_GROUP
S5_STATE = 64
N_GROUPS_MOE = 4
EXP_PER_GROUP = 8
N_EXPERTS = N_GROUPS_MOE * EXP_PER_GROUP
TOP_K_IN_GROUP = 2
D_EXPERT = D_MODEL // 4
PROJ_COLS = 2 * N_HEADS * HEAD_DIM * 2 + N_HEADS * V_DIM + S5_WIDTH
EPS = 1e-5
NEG_INF = -1e30

kernel_name = "hymba_diffattn_s5_hmoe_step"

def rmsnorm(x, g):
    xf = x.astype(jnp.float32)
    y = xf * lax.rsqrt(jnp.mean(xf * xf, axis=-1, keepdims=True) + EPS)
    return (y * g.astype(jnp.float32)).astype(x.dtype)

def rope_partial(x, pos):
    inv = ROPE_THETA ** (-jnp.arange(0, ROT_DIM, 2, dtype=jnp.float32) / ROT_DIM)
    ang = pos.astype(jnp.float32)[:, None] * inv[None, :]
    cos = jnp.cos(ang)[None, :, None, :]
    sin = jnp.sin(ang)[None, :, None, :]
    xf = x.astype(jnp.float32)
    x1 = xf[..., :ROT_DIM // 2]
    x2 = xf[..., ROT_DIM // 2:ROT_DIM]
    out = jnp.concatenate([x1 * cos - x2 * sin, x2 * cos + x1 * sin, xf[..., ROT_DIM:]], axis=-1)
    return out.astype(x.dtype)

def diff_attend(q, k, v, q_pos, k_pos, lam, subln_g, lambda_init):
    s = jnp.einsum('bqhcd,bkhcd->bhcqk', q, k).astype(jnp.float32)
    mask = k_pos[None, :] <= q_pos[:, None]
    s = jnp.where(mask, s, NEG_INF)
    p = jax.nn.softmax(s, axis=-1)
    a = p[:, :, 0] - lam * p[:, :, 1]
    o = jnp.einsum('bhqk,bkhe->bqhe', a, v.astype(jnp.float32))
    o = o * lax.rsqrt(jnp.mean(o * o, axis=-1, keepdims=True) + EPS)
    o = o * subln_g.astype(jnp.float32) * (1.0 - lambda_init)
    return o.astype(v.dtype)

def s5_mix(u, h0_re, h0_im, a_re, a_im, log_dt, b_re, b_im, c_re, c_im, d_skip, w_glu, b_glu):
    nb, ns, _ = u.shape
    uf = u.astype(jnp.float32).reshape(nb, ns, S5_GROUPS, S5_GROUP)
    lam = lax.complex(a_re.astype(jnp.float32), a_im.astype(jnp.float32))
    dt = jnp.exp(log_dt.astype(jnp.float32))[:, None]
    lam_bar = jnp.exp(lam * dt)
    b_c = lax.complex(b_re.astype(jnp.float32), b_im.astype(jnp.float32))
    b_bar = ((lam_bar - 1.0) / lam)[:, :, None] * b_c
    bu = jnp.einsum('gph,bsgh->bsgp', b_bar, uf.astype(jnp.complex64))
    a = jnp.broadcast_to(lam_bar, bu.shape)

    def combine(e1, e2):
        a1, x1 = e1
        a2, x2 = e2
        return a1 * a2, a2 * x1 + x2

    a_cum, h = lax.associative_scan(combine, (a, bu), axis=1)
    h0 = lax.complex(h0_re.astype(jnp.float32), h0_im.astype(jnp.float32))
    h = h + a_cum * h0[:, None]
    c_c = lax.complex(c_re.astype(jnp.float32), c_im.astype(jnp.float32))
    y = jnp.real(jnp.einsum('ghp,bsgp->bsgh', c_c, h))
    y = y + d_skip.astype(jnp.float32).reshape(S5_GROUPS, S5_GROUP) * uf
    y = jax.nn.gelu(y.reshape(nb, ns, S5_WIDTH))
    y = y * jax.nn.sigmoid(y @ w_glu.astype(jnp.float32) + b_glu.astype(jnp.float32))
    h_last = h[:, -1]
    return y.astype(u.dtype), jnp.real(h_last), jnp.imag(h_last)

def hier_moe(h, w_rg, b_rg, w_re, b_re, w_gate, w_up, w_down):
    nb, ns, dm = h.shape
    t = h.reshape(-1, dm)
    gl = (t @ w_rg + b_rg).astype(jnp.float32)
    gp = jax.nn.softmax(gl, axis=-1)
    g_idx = jnp.argmax(gl, axis=-1)
    g_w = jnp.take_along_axis(gp, g_idx[:, None], axis=1)
    el = (jnp.einsum('td,gde->tge', t, w_re) + b_re).astype(jnp.float32)
    el = jnp.take_along_axis(el, g_idx[:, None, None], axis=1)[:, 0]
    ep = jax.nn.softmax(el, axis=-1)
    w2, i2 = lax.top_k(ep, TOP_K_IN_GROUP)
    w2 = w2 / jnp.sum(w2, axis=-1, keepdims=True)
    gid = g_idx[:, None] * EXP_PER_GROUP + i2
    comb = jnp.sum(jax.nn.one_hot(gid, N_EXPERTS, dtype=jnp.float32) * (g_w * w2)[..., None], axis=1)
    out = jnp.zeros(t.shape, jnp.float32)
    for e in range(N_EXPERTS):
        he = jax.nn.silu(t @ w_gate[e]) * (t @ w_up[e])
        out = out + comb[:, e:e + 1] * (he @ w_down[e]).astype(jnp.float32)
    return out.astype(h.dtype).reshape(nb, ns, dm)

def decoder_layer(x, pos, past_k, past_v, h0_re, h0_im, lambda_init,
                  ln1_g, w_in, lambda_q1, lambda_k1, lambda_q2, lambda_k2, subln_g,
                  s5_a_re, s5_a_im, s5_log_dt, s5_b_re, s5_b_im, s5_c_re, s5_c_im, s5_d, w_glu, b_glu,
                  w_out, ln2_g, w_router_group, b_router_group, w_router_expert, b_router_expert,
                  w_gate, w_up, w_down):
    nb, ns, _ = x.shape
    hn = rmsnorm(x, ln1_g)
    proj = hn @ w_in
    qk_w = 2 * N_HEADS * HEAD_DIM
    q = proj[..., :qk_w]
    k = proj[..., qk_w:2 * qk_w]
    v = proj[..., 2 * qk_w:2 * qk_w + N_HEADS * V_DIM].reshape(nb, ns, N_HEADS, V_DIM)
    u = proj[..., 2 * qk_w + N_HEADS * V_DIM:]
    q = rope_partial(q.reshape(nb, ns, 2 * N_HEADS, HEAD_DIM), pos) * (HEAD_DIM ** -0.5)
    k = rope_partial(k.reshape(nb, ns, 2 * N_HEADS, HEAD_DIM), pos)
    lam = (jnp.exp(jnp.sum(lambda_q1.astype(jnp.float32) * lambda_k1.astype(jnp.float32)))
           - jnp.exp(jnp.sum(lambda_q2.astype(jnp.float32) * lambda_k2.astype(jnp.float32)))
           + lambda_init)
    q5 = q.reshape(nb, ns, N_HEADS, 2, HEAD_DIM)
    if past_k is None:
        k5 = k.reshape(nb, ns, N_HEADS, 2, HEAD_DIM)
        n_blk = ns // Q_BLOCK
        qb = q5.reshape(nb, n_blk, Q_BLOCK, N_HEADS, 2, HEAD_DIM).transpose(1, 0, 2, 3, 4, 5)
        pb = pos.reshape(n_blk, Q_BLOCK)
        ob = lax.map(lambda qp: diff_attend(qp[0], k5, v, qp[1], pos, lam, subln_g, lambda_init), (qb, pb))
        attn = ob.transpose(1, 0, 2, 3, 4).reshape(nb, ns, ATTN_WIDTH)
    else:
        k_all = jnp.concatenate([past_k, k], axis=1).reshape(nb, -1, N_HEADS, 2, HEAD_DIM)
        v_all = jnp.concatenate([past_v, v], axis=1)
        k_pos = jnp.arange(k_all.shape[1], dtype=jnp.int32)
        attn = diff_attend(q5, k_all, v_all, pos, k_pos, lam, subln_g, lambda_init).reshape(nb, ns, ATTN_WIDTH)
    s5_out, h_re, h_im = s5_mix(u, h0_re, h0_im, s5_a_re, s5_a_im, s5_log_dt, s5_b_re, s5_b_im,
                                s5_c_re, s5_c_im, s5_d, w_glu, b_glu)
    x = x + jnp.concatenate([attn, s5_out], axis=-1) @ w_out
    x = x + hier_moe(rmsnorm(x, ln2_g), w_router_group, b_router_group, w_router_expert,
                     b_router_expert, w_gate, w_up, w_down)
    return x, k, v, h_re, h_im

def setup_inputs(seed: int = 0) -> dict:
    key = jax.random.key(seed)
    ks = jax.random.split(key, 40)
    f32 = jnp.float32
    n_pages = PAST_LEN // PAGE_SIZE
    n_pool = (DEC_BATCH * n_pages * 5) // 4

    def nrm(k, shape, scale):
        return jax.random.normal(k, shape, f32) * scale

    x_prompt = nrm(ks[0], (BATCH, SEQ, D_MODEL), 1.0)
    x_sample = nrm(ks[1], (DEC_BATCH, DEC_SEQ, D_MODEL), 1.0)
    cache_k = nrm(ks[2], (DEPTH, n_pool, PAGE_SIZE, 2 * N_HEADS, HEAD_DIM), 1.0)
    cache_v = nrm(ks[3], (DEPTH, n_pool, PAGE_SIZE, N_HEADS, V_DIM), 1.0)
    state_s5_re = nrm(ks[4], (DEPTH, DEC_BATCH, S5_GROUPS, S5_STATE), 0.5)
    state_s5_im = nrm(ks[5], (DEPTH, DEC_BATCH, S5_GROUPS, S5_STATE), 0.5)
    page_table = jax.random.permutation(ks[6], n_pool)[:DEC_BATCH * n_pages].reshape(DEC_BATCH, n_pages).astype(jnp.int32)
    ln1_g = 1.0 + nrm(ks[7], (DEPTH, D_MODEL), 0.01)
    w_in = nrm(ks[8], (DEPTH, D_MODEL, PROJ_COLS), D_MODEL ** -0.5)
    lambda_q1 = nrm(ks[9], (DEPTH, HEAD_DIM), 0.1)
    lambda_k1 = nrm(ks[10], (DEPTH, HEAD_DIM), 0.1)
    lambda_q2 = nrm(ks[11], (DEPTH, HEAD_DIM), 0.1)
    lambda_k2 = nrm(ks[12], (DEPTH, HEAD_DIM), 0.1)
    subln_g = 1.0 + nrm(ks[13], (DEPTH, V_DIM), 0.01)
    s5_a_re = -0.5 + nrm(ks[14], (DEPTH, S5_GROUPS, S5_STATE), 0.01)
    s5_a_im = math.pi * jnp.arange(S5_STATE, dtype=f32)[None, None, :] + nrm(ks[15], (DEPTH, S5_GROUPS, S5_STATE), 0.01)
    s5_log_dt = jax.random.uniform(ks[16], (DEPTH, S5_GROUPS), f32, minval=math.log(1e-3), maxval=math.log(1e-1))
    s5_b_re = nrm(ks[17], (DEPTH, S5_GROUPS, S5_STATE, S5_GROUP), (2 * S5_GROUP) ** -0.5)
    s5_b_im = nrm(ks[18], (DEPTH, S5_GROUPS, S5_STATE, S5_GROUP), (2 * S5_GROUP) ** -0.5)
    s5_c_re = nrm(ks[19], (DEPTH, S5_GROUPS, S5_GROUP, S5_STATE), S5_STATE ** -0.5)
    s5_c_im = nrm(ks[20], (DEPTH, S5_GROUPS, S5_GROUP, S5_STATE), S5_STATE ** -0.5)
    s5_d = nrm(ks[21], (DEPTH, S5_WIDTH), 0.5)
    w_glu = nrm(ks[22], (DEPTH, S5_WIDTH, S5_WIDTH), S5_WIDTH ** -0.5)
    b_glu = nrm(ks[23], (DEPTH, S5_WIDTH), 0.01)
    w_out = nrm(ks[24], (DEPTH, D_MIX, D_MODEL), D_MIX ** -0.5)
    ln2_g = 1.0 + nrm(ks[25], (DEPTH, D_MODEL), 0.01)
    w_router_group = nrm(ks[26], (DEPTH, D_MODEL, N_GROUPS_MOE), D_MODEL ** -0.5)
    b_router_group = nrm(ks[27], (DEPTH, N_GROUPS_MOE), 0.01)
    w_router_expert = nrm(ks[28], (DEPTH, N_GROUPS_MOE, D_MODEL, EXP_PER_GROUP), D_MODEL ** -0.5)
    b_router_expert = nrm(ks[29], (DEPTH, N_GROUPS_MOE, EXP_PER_GROUP), 0.01)
    w_gate = nrm(ks[30], (DEPTH, N_EXPERTS, D_MODEL, D_EXPERT), D_MODEL ** -0.5)
    w_up = nrm(ks[31], (DEPTH, N_EXPERTS, D_MODEL, D_EXPERT), D_MODEL ** -0.5)
    w_down = nrm(ks[32], (DEPTH, N_EXPERTS, D_EXPERT, D_MODEL), D_EXPERT ** -0.5)
    ln_f_g = 1.0 + nrm(ks[33], (D_MODEL,), 0.01)
    return {"x_prompt": x_prompt, "x_sample": x_sample, "cache_k": cache_k, "cache_v": cache_v,
            "state_s5_re": state_s5_re, "state_s5_im": state_s5_im, "page_table": page_table,
            "ln1_g": ln1_g, "w_in": w_in, "lambda_q1": lambda_q1, "lambda_k1": lambda_k1,
            "lambda_q2": lambda_q2, "lambda_k2": lambda_k2, "subln_g": subln_g,
            "s5_a_re": s5_a_re, "s5_a_im": s5_a_im, "s5_log_dt": s5_log_dt,
            "s5_b_re": s5_b_re, "s5_b_im": s5_b_im, "s5_c_re": s5_c_re, "s5_c_im": s5_c_im,
            "s5_d": s5_d, "w_glu": w_glu, "b_glu": b_glu, "w_out": w_out, "ln2_g": ln2_g,
            "w_router_group": w_router_group, "b_router_group": b_router_group,
            "w_router_expert": w_router_expert, "b_router_expert": b_router_expert,
            "w_gate": w_gate, "w_up": w_up, "w_down": w_down, "ln_f_g": ln_f_g}

def reference(x_prompt, x_sample, cache_k, cache_v, state_s5_re, state_s5_im, page_table,
              ln1_g, w_in, lambda_q1, lambda_k1, lambda_q2, lambda_k2, subln_g,
              s5_a_re, s5_a_im, s5_log_dt, s5_b_re, s5_b_im, s5_c_re, s5_c_im, s5_d, w_glu, b_glu,
              w_out, ln2_g, w_router_group, b_router_group, w_router_expert, b_router_expert,
              w_gate, w_up, w_down, ln_f_g):
    n_prompt, seq, _ = x_prompt.shape
    n_dec, dec_seq, _ = x_sample.shape
    past_len = page_table.shape[1] * cache_k.shape[2]
    pos_p = jnp.arange(seq, dtype=jnp.int32)
    pos_s = past_len + jnp.arange(dec_seq, dtype=jnp.int32)
    zeros_state = jnp.zeros((n_prompt, S5_GROUPS, S5_STATE), jnp.float32)
    xp, xs = x_prompt, x_sample
    kp_l, vp_l, hrp_l, hip_l, ks_l, vs_l, hrs_l, his_l = [], [], [], [], [], [], [], []
    for l in range(DEPTH):
        lambda_init = 0.8 - 0.6 * math.exp(-0.3 * l)
        lw = (ln1_g[l], w_in[l], lambda_q1[l], lambda_k1[l], lambda_q2[l], lambda_k2[l], subln_g[l],
              s5_a_re[l], s5_a_im[l], s5_log_dt[l], s5_b_re[l], s5_b_im[l], s5_c_re[l], s5_c_im[l],
              s5_d[l], w_glu[l], b_glu[l], w_out[l], ln2_g[l], w_router_group[l], b_router_group[l],
              w_router_expert[l], b_router_expert[l], w_gate[l], w_up[l], w_down[l])
        xp, kp, vp, hrp, hip = decoder_layer(xp, pos_p, None, None, zeros_state, zeros_state, lambda_init, *lw)
        past_k = cache_k[l, page_table].reshape(n_dec, past_len, 2 * N_HEADS, HEAD_DIM)
        past_v = cache_v[l, page_table].reshape(n_dec, past_len, N_HEADS, V_DIM)
        xs, ksn, vsn, hrs, his = decoder_layer(xs, pos_s, past_k, past_v, state_s5_re[l], state_s5_im[l],
                                               lambda_init, *lw)
        kp_l.append(kp); vp_l.append(vp); hrp_l.append(hrp); hip_l.append(hip)
        ks_l.append(ksn); vs_l.append(vsn); hrs_l.append(hrs); his_l.append(his)
    y_prompt = rmsnorm(xp, ln_f_g)
    y_sample = rmsnorm(xs, ln_f_g)
    new_k_prompt = jnp.stack(kp_l, axis=0)
    new_v_prompt = jnp.stack(vp_l, axis=0)
    new_s5_re_prompt = jnp.stack(hrp_l, axis=0)
    new_s5_im_prompt = jnp.stack(hip_l, axis=0)
    new_k_sample = jnp.stack(ks_l, axis=0)
    new_v_sample = jnp.stack(vs_l, axis=0)
    new_s5_re_sample = jnp.stack(hrs_l, axis=0)
    new_s5_im_sample = jnp.stack(his_l, axis=0)
    return (y_prompt, y_sample, new_k_prompt, new_v_prompt, new_s5_re_prompt, new_s5_im_prompt,
            new_k_sample, new_v_sample, new_s5_re_sample, new_s5_im_sample)


_drawn_inputs = setup_inputs


def setup_inputs(seed=0):
    import zlib

    import numpy as np

    out = dict(_drawn_inputs(seed))
    spreads = {}
    factors = {'ln1_g': 3.607,
     'lambda_q1': 3.7,
     'lambda_k1': 8.0,
     'subln_g': 4.483,
     's5_a_re': 3.954,
     'b_glu': 8.0,
     'ln2_g': 2.881,
     'b_router_group': 4.38,
     'b_router_expert': 3.676,
     'ln_f_g': 5.685}
    for name, (base, spread) in spreads.items():
        noise = np.random.default_rng([zlib.crc32(name.encode()), seed]).standard_normal(out[name].shape)
        drawn = base * np.exp(spread * noise) if base else spread * noise
        out[name] = __import__('jax').numpy.asarray(drawn.astype(out[name].dtype))
    for name, factor in factors.items():
        out[name] = (out[name] * factor).astype(out[name].dtype)
    return out
```

```python
import numpy as np
import concourse.bass as bass
from concourse import mybir
from contextlib import ExitStack

SEQ, NB, D = 1024, 8, 1024
TT = SEQ + NB
KD = D // 128
NT = SEQ // 128
H, HD, VD = 4, 64, 128
QKW = 2 * H * HD
PROJ = 4 * QKW
NPAGE, PG = 64, 128
POOL = NB * NPAGE * 5 // 4
RING = 16
GRP = 8
TURNS = NPAGE // RING
NROT = 8
G5, W5, P5 = 32, 16, 64
NP5 = G5 // 2
CH = 8
NC = SEQ // CH
NE, EG, NG = 32, 8, 4
DE = D // 4
MAXT = 48
SLOTS = MAXT * 128
EPS = 1e-5
NEG = -1e30
LINIT = 0.8 - 0.6
MAGIC = 12582912.0
GELU_C = float(np.sqrt(2.0 / np.pi))

C_ID, C_ONE, C_UP, C_MASK = 0, 128, 256, 384
C_SUM = 512
C_NEG = 640
C_M0, C_M1 = 704, 708
C_I8, C_I32, C_THR, C_TOK, C_VAL, C_TI = 712, 720, 752, 761, 770, 779
C_NH = C_TI + 128
C_END = C_NH + 1



def make_plan():
    dec = []
    for b in range(NB):
        dec += [(1.0, ("K", b, t)) for t in range(TURNS)]
        dec += [(.3, ("m1", b)), (.3, ("m2", b)), (.4, ("m3", b)), (.3, ("pt", b))]
        dec += [(1.0, ("V", b, t)) for t in range(TURNS)] + [(.1, ("ov", b))]
    pro = [(6.8, ("u", s)) for s in range(NT)]
    pend = None
    for i in range(NT):
        pro += [(6.8, ("qk", i, 0)), (6.8, ("qk", i, 1)), (6.8, ("v", i))]
        if pend is not None:
            pro += [(1 + .3 * i, ("av",) + pend), (.3, ("ot", i - 1))]
            pend = None
        pro += [(.5, ("qt", i))]
        for h in range(H):
            pro += [(.45 * (i + 1), ("s", i, h))]
            if pend is not None:
                pro += [(.3 * (i + 1), ("av",) + pend)]
            pend = (i, h)
    pro += [(3, ("av",) + pend), (.3, ("ot", NT - 1))]
    pro += [(10, ("s5a",)), (2, ("s5pt",))] + [(.3, ("s5u", n)) for n in range(8)]
    pro += [(14, ("s5k",))] + [(2, ("s5x", n)) for n in range(8)] + [(30, ("s5h",))]
    pro += [(2, ("s5y", n)) for n in range(8)] + [(3, ("s5g", n)) for n in range(3)]
    pro += [(.5, ("s5t", n)) for n in range(5)] + [(6.8, ("glu", n)) for n in range(4)] + [(1, ("glu", 4))]
    pro += [(2, ("x1",))]
    for i in range(NT):
        pro += [(13.6, ("out", i)), (2, ("ht", i))]
    total, wsum = sum(c for c, _ in pro), sum(w for w, _ in dec)
    plan, t, n, due = [("stats",), ("dqkv",), ("dprep",)], 0.0, 0, 0.0
    for c, x in pro:
        plan.append(x)
        t += c
        while n < len(dec) and t * wsum > due * total:
            plan.append(dec[n][1])
            due += dec[n][0]
            n += 1
    plan += [x for _, x in dec[n:]]
    plan += [("dout",), ("out", NT), ("ht", NT), ("route",)]
    return plan


def psum_keys(unit):
    k, a = unit[0], unit[1:]
    return {
        "stats": [("ss",)], "dqkv": [("dp",)], "dprep": [("dqt",)],
        "pt": [("PT",) + a + (0,), ("PT",) + a + (1,), ("PTn",) + a],
        "u": [("u",) + a], "qk": [("qk",) + a[:1]] if a[1:] == (0,) else [], "v": [("v",) + a], "qt": [("qkT",) + a],
        "s": [("S",) + a + (0,), ("S",) + a + (1,)], "av": [("AT",) + a, ("O",) + a],
        "ot": [("oT",) + a], "dout": [("dss",)],
        "s5pt": [("pt", n) for n in range(4)], "s5k": [("k", n) for n in range(4)],
        "s5u": [("U",) + a], "s5x": [("X",) + a], "s5y": [("Y",) + a],
        "s5t": [("yT",) + a], "glu": [("z",) + a],
        "route": [("rank",), ("ids",)],
        "out": [("o",) + a], "ht": [("hT",) + a, ("r",) + a],
    }.get(k, [])


def hymba_step(nc, io):
    f32, i32, u32 = mybir.dt.float32, mybir.dt.int32, mybir.dt.uint32
    ALU, ACT, AX = mybir.AluOpType, mybir.ActivationFunctionType, mybir.AxisListType.X
    MUL, ADD, SUB, MAX, MIN = ALU.mult, ALU.add, ALU.subtract, ALU.max, ALU.min

    PLAN = make_plan()
    USE = {}
    for unit in PLAN:
        for key in psum_keys(unit):
            USE[key] = len(USE)
    POW = {}
    for unit in PLAN:
        if unit[0] in ("stats", "dout", "ht") or (unit[0] == "av" and unit[2] == H - 1):
            POW[unit] = len(POW)

    ctx = ExitStack()
    with ctx:
        def sb(name, shape, dt=f32):
            return ctx.enter_context(nc.sbuf_tensor(name, shape, dt))

        def sem(name):
            return ctx.enter_context(nc.semaphore(name))

        consts = sb("consts", [128, C_END])
        ident, ones = consts[:, C_ID:C_ID + 128], consts[:, C_ONE:C_ONE + 128]
        causal = consts[:, C_MASK:C_MASK + 128]
        rope = sb("rope", [128, NT + 1, 2 * NROT])
        ptab = sb("ptab", [1, NB * NPAGE], i32)
        colw = sb("colw", [128, 3 * KD])
        lamt = sb("lamt", [128, 8])
        rstd = sb("rstd", [128, 2 * NT + 1])
        xm = sb("xm", [128, KD, TT])
        ring = sb("ring", [128, RING, 512])
        dvu = sb("dvu", [NB, 2 * QKW])
        qpad = sb("qpad", [128, H, NB, 32])
        knT = sb("knT", [128, H, NB])
        sall = sb("sall", [128, TURNS, 512])
        snew = sb("snew", [128, NB])
        ptn = sb("ptn", [NB, 128])
        mrow = sb("mrow", [128, 8])
        mrep = sb("mrep", [1, 4, 32])
        wmap = sb("wmap", [128, 2, H])
        o4s = sb("o4s", [128, 512])
        aD = sb("aD", [128, H, NB])
        aD2 = sb("aD2", [128, H, NB])
        rt = sb("rt", [128, 16, NROT, 4])
        st = sb("st", [128, 32])
        arena = sb("arena", [128, 28112])
        rtf = rt[:, :, :, :].rearrange("p a b c -> p (a b c)")

        def region(base, size, pat=None, /, **kw):
            v = arena[:, base:base + size]
            return v if pat is None else v.rearrange(pat, **kw)

        w_qkv = region(0, KD * 3 * QKW, "p (k n) -> p k n", k=KD)
        w_u = region(12288, KD * QKW, "p (k n) -> p k n", k=KD)
        P = region(12288, 4096, "p (s c n) -> p s c n", s=2, c=2)
        kT = region(16384, H * SEQ, "p (h n) -> p h n", h=H)
        sq = region(16384, 2 * TT, "p (s n) -> p s n", s=2)
        V = region(20480, NT * QKW, "p (t n) -> p t n", t=NT)
        qk = region(24576, 1024)
        qT = region(25600, H * 128, "p (h n) -> p h n", h=H)
        att = region(26112, QKW)
        lamv = region(26112, 4 * HD, "p (a d) -> p a d", a=4)

        CLr = region(0, 2304, "p (j k h) -> p j k h", j=NP5, k=CH + 1)
        CLn = region(2304, 2304, "p (j k h) -> p j k h", j=NP5, k=CH + 1)
        PT5 = region(4608, 4096, "p (m j q) -> p m j q", m=2, j=NP5)
        PB = region(8704, 4096, "p (m j s h) -> p m j s h", m=2, j=NP5, s=CH)
        U = region(8704, 4608, "p (g c) -> p g c", g=G5)
        Hs = region(13312, 4640, "p (m j c) -> p m j c", m=2, j=NP5)
        Ksb = region(17952, 4096, "p (g q) -> p g q", g=G5)
        Z = region(17952, 4096, "p (g s h) -> p g s h", g=G5, s=CH)[0:2 * NB]
        Bt = region(13312, 4096, "p (m j s h) -> p m j s h", m=2, j=NP5, s=CH)
        yT = region(17952, 4 * TT, "p (k n) -> p k n", k=4)
        usb = region(22080, 4096, "p (s n) -> p s n", s=CH)
        par = region(26176, 48, "p (a j) -> p a j", a=3)
        bc = region(26224, 1024, "p (a m j h) -> p a m j h", a=2, m=2, j=NP5)
        Lp = region(27248, 288, "p (m k j) -> p m k j", m=2, k=CH + 1)
        LpR = region(27536, 256, "p (m j s) -> p m j s", m=2, j=NP5)
        sm5 = region(27792, 320, "p (a j) -> p a j", a=20)
        hs8 = rtf[:, 0:256].rearrange("p (m j b) -> p m j b", m=2, j=NP5)
        hp = rtf[:, 256:288].rearrange("p (m j) -> p m j", m=2)
        T5 = xm[:, 4:8, :].rearrange("p k n -> p (k n)")[:, 0:4096].rearrange("p (g q) -> p g q", g=G5)
        ug = T5.rearrange("p g (s h) -> p g s h", s=CH)
        tmp5 = region(4608, 4096)
        tmp5b = region(17952, 4096)
        wglu = region(0, 2048, "p (k n) -> p k n", k=4)
        x1 = region(0, (NT + 1) * D, "p (t n) -> p t n", t=NT + 1)
        wout = region(9216, KD * D, "p (k n) -> p k n", k=KD)
        h2 = region(17408, 2048, "p (s n) -> p s n", s=2)
        h2T = region(19456, 2048, "p (s k n) -> p s k n", s=2, k=KD)
        wr = sb("wr", [128, KD, 36])
        br = sb("br", [128, 36])
        logit = sb("logit", [128, NT + 1, 36])
        bglu = sb("bglu", [128, 4])
        dskip = sb("dskip", [128, QKW])
        ids = sb("ids", [128, MAXT], u32)
        idc = sb("idc", [128, 2], u32)
        rows = sb("rows", [128, 2, NT + 1], u32)
        wts = sb("wts", [128, 2, NT + 1])
        plan_t = sb("plan_t", [1, MAXT + 2], i32)
        R = [region(b, 9 * 128, "p (t n) -> p t n", t=9) for b in (19456, 15360)]
        TO = [region(b, 9 * MAXT, "p (t n) -> p t n", t=9) for b in (20608, 21040)]
        OH = [region(16512 + 288 * c, 288, "p (t e) -> p t e", t=9) for c in range(2)]
        OHs = region(17088, 320, "p (t e) -> p t e", t=10)
        xmf, ringf = xm[:, :, :].rearrange("p k n -> p (k n)"), ring[:, :, :].rearrange("p a n -> p (a n)")
        WX = [region(21504, 6144), xmf[:, 0:6144], ringf[:, 0:6144], region(9216, 6144)]
        Wgu = [w[:, 0:4096].rearrange("p (k n) -> p k n", k=KD) for w in WX]
        Wdn = [w[:, 4096:6144].rearrange("p (k n) -> p k n", k=2) for w in WX]
        hg = [ringf[:, 6144 + 1024 * s:7168 + 1024 * s] for s in range(2)]
        hgT = [xmf[:, 6144 + 1024 * s:7168 + 1024 * s].rearrange("p (k n) -> p k n", k=KD) for s in range(2)]
        yb = [region(15360 + 1024 * s, 1024) for s in range(2)]
        tg, he, heT_ = ([region(17408 + 512 * a + 256 * s, 256) for s in range(2)] for a in range(3))
        lnf = region(19456, D)
        yg = [[region(21504 + 2048 * s + 1024 * c, 1024) for c in range(2)] for s in range(2)]

        SC = ctx.enter_context(nc.psum_tensor("SC", [128, 512], f32))
        OD = ctx.enter_context(nc.psum_tensor("OD", [128, 512], f32))
        nkP, mxT, mbP, lP, aP = OD[0:32, 0:NB], OD[0:1, 128:256], OD[:, 256:257], OD[:, 257:258], OD[:, 260:264]
        W = [ctx.enter_context(nc.psum_tensor(f"W{i}", [128, 1024], f32)) for i in range(3)]

        ps_full = [sem(f"ps_full{i}") for i in range(3)]
        ps_free = [sem(f"ps_free{i}") for i in range(3)]
        s_cst, s_lamv, s_lam = sem("s_cst"), sem("s_lamv"), sem("s_lam")
        s_wk = [sem(f"s_wk{k}") for k in range(KD)]
        s_xk = [sem(f"s_xk{k}") for k in range(KD)]
        s_pg = [sem(f"s_pg{k}") for k in range(RING // GRP)]
        s_pgfree = sem("s_pgfree")
        s_tab = sem("s_tab")
        s_sq, s_sqread, s_xg, s_rstd = sem("s_sq"), sem("s_sqread"), sem("s_xg"), sem("s_rstd")
        s_dq, s_drope, s_dst, s_qbd = sem("s_dq"), sem("s_drope"), sem("s_dst"), sem("s_qbd")
        s_u = sem("s_u")
        s_qk, s_v, s_rope, s_kst, s_qkT = sem("s_qk"), sem("s_v"), sem("s_rope"), sem("s_kst"), sem("s_qkT")
        s_vst = sem("s_vst")
        s_mx, s_exp, s_comb, s_ATs, s_att = sem("s_mx"), sem("s_exp"), sem("s_comb"), sem("s_ATs"), sem("s_att")
        s_ms, s_rs = sem("s_ms"), sem("s_rs")
        s_mix = sem("s_mix")
        s_score, s_evac, s_nk, s_m1, s_mT, s_mrep, s_mb, s_nb, s_pexp = (sem(x) for x in (
            "s_score", "s_evac", "s_nk", "s_m1", "s_mT", "s_mrep", "s_mb", "s_nb", "s_pexp"))
        s_l, s_lP, s_ptw, s_pv, s_o4, s_aP, s_ad, s_ad2, s_dmix = (sem(x) for x in (
            "s_l", "s_lP", "s_ptw", "s_pv", "s_o4", "s_aP", "s_ad", "s_ad2", "s_dmix"))
        s_ust = [sem(f"s_ust{n}") for n in range(2)]
        s_dve5, s_act5, s_pool5, s_ld5, s_u5, s_x5, s_Td, s_Tz, s_h0 = (sem(x) for x in (
            "s_dve5", "s_act5", "s_pool5", "s_ld5", "s_u5", "s_x5", "s_Td", "s_Tz", "s_h0"))
        s_z, s_pt5, s_ks, s_Us, s_Xs, s_ks1, s_ks2, s_ks3, s_scan = (sem(x) for x in (
            "s_z", "s_pt5", "s_ks", "s_Us", "s_Xs", "s_ks1", "s_ks2", "s_ks3", "s_scan"))
        s_du, s_y, s_th, s_g5, s_yT, s_zt, s_mix2, s_wl, s_wo, s_x1 = (sem(x) for x in (
            "s_du", "s_y", "s_th", "s_g5", "s_yT", "s_zt", "s_mix2", "s_wl", "s_wo", "s_x1"))
        s_xo, s_sq2, s_h2, s_h2T, s_hst, s_logit = (sem(x) for x in (
            "s_xo", "s_sq2", "s_h2", "s_h2T", "s_hst0", "s_logit"))
        s_hst = [s_hst, sem("s_hst1")]
        s_fx, s_ug = sem("s_fx"), sem("s_ug")
        s_rexp, s_rex2, s_oh, s_lst, s_route = (sem(x) for x in ("s_rexp", "s_rex2", "s_oh", "s_lst", "s_route"))
        m_w = [sem(f"m_w{n}") for n in range(4)]
        m_hg = [sem(f"m_hg{n}") for n in range(2)]
        m_st = [sem(f"m_st{n}") for n in range(2)]
        m_T, m_hT, m_gu, m_th, m_he, m_heT, m_heS, m_y, m_ys = (sem(x) for x in (
            "m_T", "m_hT", "m_gu", "m_th", "m_he", "m_heT", "m_heS", "m_y", "m_ys"))
        s_stored = sem("s_stored")
        s_zero, s_zst = sem("s_zero"), sem("s_zst")
        f_g = [sem(f"f_g{n}") for n in range(2)]
        f_gf, f_x, f_sq, f_ms, f_rs, f_out, f_st = (sem(x) for x in (
            "f_gf", "f_x", "f_sq", "f_ms", "f_rs", "f_out", "f_st"))

        def slot(*key):
            return W[USE[key] % 3]

        def filled(*key):
            return ps_full[USE[key] % 3], USE[key] // 3 + 1

        def full_sem(*key):
            return ps_full[USE[key] % 3]

        def free_sem(*key):
            return ps_free[USE[key] % 3]

        def vacant(eng, *key):
            if USE[key] >= 3:
                eng.wait_ge(ps_free[USE[key] % 3], USE[key] // 3)

        block = ctx.enter_context(nc.Block())

        @block.sync
        def _(sp):
            sp.dma_start(ptab[:, :], io["page_table"]).then_inc(s_tab, 16)
            for k in range(KD):
                sp.dma_start(xm[:, k, :], io["xT"][k, :, :]).then_inc(s_xk[k], 16)
                sp.dma_start(w_qkv[:, k, :], io["w_qkv"][k, :, :]).then_inc(s_wk[k], 16)
                sp.dma_start(w_u[:, k, :], io["w_u"][k, :, :]).then_inc(s_wk[k], 16)
            sp.wait_ge(s_tab, 16)
            with sp.Fori(0, NB) as b:
                for kind, cache in enumerate((io["cacheK"], io["cacheV"])):
                    with sp.Fori(0, NPAGE // RING) as r:
                        for j in range(RING):
                            page = sp.value_load(ptab[0:1, bass.ds(b * NPAGE + r * RING + j, 1)],
                                                 min_val=0, max_val=POOL - 1)
                            if j % GRP == 0:
                                sp.wait_ge(s_pgfree, b * (2 * NPAGE // GRP) + r * 2
                                           + (kind * (NPAGE // GRP) + j // GRP + 1))
                            sp.dma_start(ring[:, j, :], cache[bass.ds(page, 1), :, :]
                                         .rearrange("a p n -> p (a n)")).then_inc(s_pg[j // GRP], 16)

            def weights(e, v):
                sp.dma_start(Wgu[v], io["w_gu"][e, :, :, :].rearrange("a p k n -> p (a k) n")).then_inc(m_w[v], 16)
                sp.dma_start(Wdn[v], io["w_dn"][e, :, :, :].rearrange("a p k n -> p (a k) n")).then_inc(m_w[v], 16)

            sp.wait_ge(s_mix2, 5)
            sp.wait_ge(s_fx, 32)
            weights(slice(0, 1), 0)
            sp.wait_ge(*filled("o", NT))
            weights(slice(1, 2), 1)
            weights(slice(3, 4), 3)
            sp.wait_ge(s_pgfree, RING // GRP + NB * 2 * NPAGE // GRP)
            weights(slice(2, 3), 2)
            sp.wait_ge(s_route, 1)
            n4 = sp.value_load(plan_t[0:1, MAXT:MAXT + 1], min_val=NE // 4, max_val=MAXT // 4)
            with sp.Fori(1, n4) as q:
                for v in range(4):
                    e = sp.value_load(plan_t[0:1, bass.ds(4 * q + v, 1)], min_val=0, max_val=NE - 1)
                    sp.wait_ge(m_y, 4 * q + (v - 3))
                    weights(bass.ds(e, 1), v)
            for i in range(NT + 1):
                sp.wait_ge(f_out, i + 1)
                if i < NT:
                    sp.dma_start(io["y_p"][i, :, :], x1[:, i, :]).then_inc(f_st, 16)
                else:
                    sp.dma_start(io["y_s"], x1[0:NB, NT, :]).then_inc(f_st, 16)
            sp.wait_ge(f_st, 16 * (NT + 1))

        @block.gpsimd
        def _(gp):
            gp.dma_start(consts[:, :], io["consts"]).then_inc(s_cst, 16)
            gp.dma_start(colw[:, :], io["colw"]).then_inc(s_cst, 16)
            gp.dma_start(rope[:, :, :], io["rope"]).then_inc(s_cst, 16)
            gp.dma_start(dskip[:, :], io["dskip"].partition_broadcast(128)).then_inc(s_cst, 16)
            gp.dma_start(br[:, :], io["b_r"].partition_broadcast(128)).then_inc(s_cst, 16)
            gp.dma_start(wr[:, :, :], io["w_r"]).then_inc(s_cst, 16)
            gp.dma_start(bglu[:, :], io["b_glu"]).then_inc(s_cst, 16)
            gp.dma_start(lamv[:, :, :], io["lamv"].partition_broadcast(128)).then_inc(s_lamv, 16)

            def stats():
                gp.memset(qpad[:, :, :, :], 0.0).then_inc(s_qbd, 1)
                gp.wait_ge(s_cst, 112)
                for k in range(KD):
                    gp.wait_ge(s_sq, k + 1)
                    gp.tensor_scalar(xm[:, k, :], xm[:, k, :], colw[:, k:k + 1], None, MUL).then_inc(s_xg, 1)

                gp.memset(sall[:, 0:2, :], 0.0).then_inc(s_zero, 1)
                root(rstd[:, :], ("stats",))
                gp.wait_ge(s_zero, 1)
                for t in range(NE, MAXT):
                    gp.dma_start(io["y_scratch"][128 * t:128 * t + 128, :],
                                 sall[:, 0:2, :].rearrange("p t n -> p (t n)")).then_inc(s_zst, 16)

            def root(x, key):
                gp.wait_ge(s_ms, POW[key] + 1)
                gp.tensor_tensor(x, x, consts[:, C_NH:C_NH + 1].to_broadcast(list(x.shape)), ALU.pow).then_inc(s_rs, 1)

            def av(i, h):
                if h == H - 1:
                    root(st[:, 24:28], ("av", i, h))

            def dout():
                root(aD2[:, :, :].rearrange("p h b -> p (h b)"), ("dout",))

            def dqkv():
                gp.wait_ge(s_drope, 1)
                gp.dma_start(io["v_s"], dvu[:, 0:QKW]).then_inc(s_dst, 16)
                gp.wait_ge(s_drope, 1)
                gp.dma_start(io["k_s"], qk[0:NB, QKW:2 * QKW]).then_inc(s_dst, 16)

            def u(s):
                gp.wait_ge(s_u, s + 1)
                gp.dma_start(io["u_scratch"][:, s, :], qk[:, QKW * (s % 2):QKW * (s % 2) + QKW]).then_inc(s_ust[s % 2], 16)

            def qt(i):
                gp.wait_ge(s_rope, i + 1)
                gp.dma_start(io["k_p"][i, :, :], qk[:, QKW:2 * QKW]).then_inc(s_kst, 16)
                gp.wait_ge(s_v, i + 1)
                gp.dma_start(io["v_p"][i, :, :], V[:, i, :]).then_inc(s_vst, 16)

            def s5a():
                gp.wait_ge(*filled("oT", NT - 1))
                gp.wait_ge(s_kst, 16 * NT)
                gp.wait_ge(s_vst, 16 * NT)
                for n in range(2):
                    gp.wait_ge(s_ust[n], 16 * (CH // 2))
                gp.dma_start(par, io["s5_par"]).then_inc(s_ld5, 16)
                gp.dma_start(bc, io["s5_bc"]).then_inc(s_ld5, 16)
                gp.dma_start(usb, io["u_scratch"]).then_inc(s_u5, 16)
                gp.memset(Z, 0.0).then_inc(s_z, 1)
                gp.wait_ge(s_z, 1)
                for a, s in ((0, 0), (1, CH - 1)):
                    gp.dma_start(Z[NB * a:NB * a + NB, :, s, :],
                                 dvu[:, QKW:2 * QKW].rearrange("p (g h) -> p g h", g=G5)).then_inc(s_u5, 16)

            def s5k():
                gp.wait_ge(*filled("U", 7))
                gp.memset(T5, 0.0).then_inc(s_Tz, 1)
                gp.wait_ge(*filled("k", 3))
                gp.memset(Hs[:, :, :, 0:1], 0.0).then_inc(s_Tz, 1)
                gp.wait_ge(s_ks, 4)
                gp.wait_ge(s_Tz, 2)
                for s in range(CH):
                    gp.dma_start(T5[16 * s:16 * s + 16, :, 16 * s:128], Ksb[16 * s:16 * s + 16, :, 0:128 - 16 * s])\
                        .then_inc(s_Td, 16)

            def s5x(n):
                if n == 7:
                    gp.wait_ge(s_Us, 8)
                    gp.wait_ge(s_cst, 112)
                    gp.tensor_tensor(usb, usb, dskip[:, :].unsqueeze(1).to_broadcast([128, CH, QKW]), MUL)
                    gp.tensor_tensor(dvu[:, QKW:2 * QKW], dvu[:, QKW:2 * QKW], dskip[0:NB, :], MUL)
                    gp.drain().then_inc(s_du, 1)
                    gp.wait_ge(s_Xs, 8)
                    for m in range(2):
                        gp.dma_start(Hs[:, m, :, NC + 1:NC + 1 + NB], io["s5_h0"][m, :, :, :]).then_inc(s_h0, 16)

            def s5h():
                gp.wait_ge(s_scan, 1)
                gp.dma_start(io["h_p"].rearrange("m p j -> p m j"), hp).then_inc(s_fx, 16)
                gp.dma_start(io["h_s"].rearrange("m p j b -> p m j b"), hs8).then_inc(s_fx, 16)

            def s5y(n):
                if n == 7:
                    gp.wait_ge(*filled("Y", 7))
                    gp.dma_start(wglu, io["w_glu"]).then_inc(s_wl, 16)
                    gp.dma_start(wout, io["w_out"]).then_inc(s_wo, 16)

            def x1_():
                gp.wait_ge(*filled("z", 4))
                gp.wait_ge(s_mix2, 5)
                for i in range(NT):
                    gp.dma_start(x1[:, i, :], io["x_p"][i, :, :]).then_inc(s_x1, 16)
                gp.dma_start(x1[0:NB, NT, :], io["x_s"]).then_inc(s_x1, 16)

            def ht(i):
                root(st[:, 28:29], ("ht", i))
                r = 128 if i < NT else NB
                gp.wait_ge(s_h2, i + 1)
                gp.dma_start(io["h2_scratch"][128 * i:128 * i + r, :], h2[0:r, i % 2, :]).then_inc(s_hst[i % 2], 16)

            later = {"s5a": s5a, "s5k": s5k, "s5x": s5x, "s5h": s5h, "s5y": s5y, "x1": x1_, "ht": ht}
            todo = {"stats": stats, "dqkv": dqkv, "qt": qt, "av": av, "dout": dout, "u": u, **later}
            for unit in PLAN:
                if unit[0] in todo:
                    todo[unit[0]](*unit[1:])

            def gather(q, v):
                gp.tensor_copy(idc[:, v % 2:v % 2 + 1], ids[:, bass.ds(4 * q + v, 1)])
                gp.drain()
                gp.indirect_dma_start(hg[v % 2], None, io["h2_scratch"],
                                      bass.IndirectOffsetOnAxis(ap=idc[:, v % 2:v % 2 + 1], axis=0))\
                    .then_inc(m_hg[v % 2], 16)

            gp.wait_ge(s_route, 1)
            gp.wait_ge(s_pgfree, RING // GRP + NB * 2 * NPAGE // GRP)
            for n in range(2):
                gp.wait_ge(s_hst[n], 16 * ((NT + 2 - n) // 2))
            gp.dma_start(lnf, io["ln_f_g"].partition_broadcast(128)).then_inc(f_gf, 16)
            for v in range(4):
                if v >= 2:
                    gp.wait_ge(m_T, v - 1)
                gather(0, v)
            n4 = gp.value_load(plan_t[0:1, MAXT:MAXT + 1], min_val=NE // 4, max_val=MAXT // 4)
            with gp.Fori(1, n4) as q:
                for v in range(4):
                    gp.wait_ge(m_T, 4 * q + (v - 1))
                    gather(q, v)

            def gather2(i):
                for c in range(2):
                    r = 128 if i < NT else NB
                    gp.indirect_dma_start(yg[i % 2][c][0:r, :], None, io["y_scratch"],
                                          bass.IndirectOffsetOnAxis(ap=rows[0:r, c, i:i + 1], axis=0))\
                        .then_inc(f_g[i % 2], 16)

            gp.wait_ge(s_stored, 1)
            gather2(0)
            gather2(1)
            for i in range(NT + 1):
                gp.wait_ge(f_ms, i + 1)
                x = st[:, i:i + 1]
                gp.tensor_tensor(x, x, consts[:, C_NH:C_NH + 1], ALU.pow).then_inc(f_rs, 1)
                if i + 2 <= NT:
                    gather2(i + 2)
            gp.wait_ge(s_dst, 32)
            gp.wait_ge(s_fx, 32)
            for n in range(2):
                gp.wait_ge(s_ust[n], 16 * (CH // 2))
                gp.wait_ge(s_hst[n], 16 * ((NT + 2 - n) // 2))
            gp.wait_ge(s_kst, 16 * NT)
            gp.wait_ge(s_vst, 16 * NT)

        @block.scalar
        def _(act):
            def stats():
                for k in range(KD):
                    act.wait_ge(s_xk[k], 16)
                    if k >= 2:
                        act.wait_ge(s_sqread, k - 1)
                    act.activation(sq[:, k % 2, :], xm[:, k, :], ACT.Square).then_inc(s_sq, 1)

            def dqkv():
                act.wait_ge(*filled("dp"))
                for n, out in enumerate((qk[0:NB, 0:QKW], qk[0:NB, QKW:2 * QKW], dvu[:, 0:QKW], dvu[:, QKW:2 * QKW])):
                    act.activation(out, slot("dp")[32 * n:32 * n + NB, 0:QKW], ACT.Copy)
                act.drain().then_inc(free_sem("dp"), 1)
                act.drain().then_inc(s_dq, 1)

            def u(s):
                act.wait_ge(s_rstd, 1)
                if s < 2:
                    act.wait_ge(*filled("dqt"))
                    act.wait_ge(s_dst, 32)
                else:
                    act.wait_ge(s_ust[s % 2], 16 * (s // 2))
                act.wait_ge(*filled("u", s))
                act.activation(qk[:, QKW * (s % 2):QKW * (s % 2) + QKW], slot("u", s)[:, 0:QKW], ACT.Copy,
                               scale=rstd[:, NT + s:NT + s + 1]).then_inc(s_u, 1)
                act.drain().then_inc(free_sem("u", s), 1)

            def qk_(i, n):
                if n == 0:
                    return
                if i >= 1:
                    act.wait_ge(*filled("qkT", i - 1))
                    act.wait_ge(s_kst, 16 * i)
                else:
                    for n in range(2):
                        act.wait_ge(s_ust[n], 16 * (CH // 2))
                act.wait_ge(*filled("qk", i))
                act.activation(qk, slot("qk", i)[:, :], ACT.Copy,
                               scale=rstd[:, i:i + 1]).then_inc(s_qk, 1)
                act.drain().then_inc(free_sem("qk", i), 1)

            def v(i):
                act.wait_ge(*filled("v", i))
                act.activation(V[:, i, :], slot("v", i)[:, 0:QKW], ACT.Copy,
                               scale=rstd[:, i:i + 1]).then_inc(s_v, 1)
                act.drain().then_inc(free_sem("v", i), 1)

            def qt(i):
                act.wait_ge(*filled("qkT", i))
                src = slot("qkT", i)[:, :].rearrange("p (a h n) -> p a h n", a=2, h=H)
                if i >= 1:
                    act.wait_ge(*filled("S", i - 1, H - 1, 1))
                act.activation(qT, src[:, 0, :, :], ACT.Copy)
                act.activation(kT[:, :, 128 * i:128 * i + 128], src[:, 1, :, :], ACT.Copy)
                act.drain().then_inc(free_sem("qkT", i), 1)
                act.drain().then_inc(s_qkT, 1)

            def s(i, h):
                n, w = H * i + h, 128 * (i + 1)
                if n >= 2:
                    act.wait_ge(*filled("O", (n - 2) // H, (n - 2) % H))
                for c in range(2):
                    act.wait_ge(s_mx, 2 * n + c + 1)
                    act.activation(P[:, n % 2, c, 0:w], slot("S", i, h, c)[:, 0:w], ACT.Exp,
                                   bias=st[:, 4 * (n % 2) + c:4 * (n % 2) + c + 1], scale=HD ** -0.5,
                                   accum_out=st[:, 4 * (n % 2) + 2 + c:4 * (n % 2) + 3 + c])
                    act.drain().then_inc(free_sem("S", i, h, c), 1)
                    act.drain().then_inc(s_exp, 1)

            def av(i, h):
                n, w = H * i + h, 128 * (i + 1)
                act.wait_ge(*filled("AT", i, h))
                act.activation(P[:, n % 2, 1, 0:w], slot("AT", i, h)[:, 0:w], ACT.Copy).then_inc(s_ATs, 1)
                act.drain().then_inc(free_sem("AT", i, h), 1)

            def ot(i):
                act.wait_ge(*filled("oT", i))
                for h in range(H):
                    act.activation(xm[:, h, 128 * i:128 * i + 128], slot("oT", i)[:, 128 * h:128 * h + 128],
                                   ACT.Copy, scale=colw[:, 2 * KD:2 * KD + 1])
                act.drain().then_inc(free_sem("oT", i), 1)
                act.drain().then_inc(s_mix, 1)

            def K(b, t):
                if t == 0 and b >= 1:
                    act.wait_ge(s_pv, b)
                if t == 0 and b == 0:
                    act.wait_ge(s_zst, 16 * (MAXT - NE))
                for g in range(2):
                    act.wait_ge(s_score, 2 * (TURNS * b + t) + g + 1)
                    act.activation(sall[:, t, 256 * g:256 * g + 256], (SC, OD)[g][:, 0:256],
                                   ACT.Copy).then_inc(s_evac, 1)

            def m3(b):
                act.wait_ge(s_nb, b + 1)
                act.activation(sall[:, :, :], sall[:, :, :], ACT.Exp, bias=mrow[:, 1:2], scale=HD ** -0.5,
                               accum_out=mrow[:, 2:3])
                act.activation(snew[:, :], snew[:, :], ACT.Exp, bias=mrow[:, 1:2], scale=HD ** -0.5,
                               accum_out=mrow[:, 3:4])
                act.drain().then_inc(s_pexp, 1)

            def pt(b):
                for n in range(2):
                    act.wait_ge(*filled("PT", b, n))
                    act.activation(sall[:, 2 * n:2 * n + 2, :].rearrange("p t n -> p (t n)"), slot("PT", b, n)[:, :],
                                   ACT.Copy)
                    act.drain().then_inc(free_sem("PT", b, n), 1)
                act.wait_ge(*filled("PTn", b))
                act.activation(ptn[:, :], slot("PTn", b)[0:NB, 0:128], ACT.Copy)
                act.drain().then_inc(free_sem("PTn", b), 1)
                act.drain().then_inc(s_ptw, 1)

            def s5a():
                act.wait_ge(s_ld5, 32)
                act.activation(sm5[:, 0, :], par[:, 2, :], ACT.Exp).then_inc(s_act5, 1)
                act.wait_ge(s_dve5, 1)
                act.activation(sm5[:, 3, :], sm5[:, 1, :], ACT.Exp).then_inc(s_act5, 1)
                act.activation(sm5[:, 6:8, :], sm5[:, 4:6, :], ACT.Sin).then_inc(s_act5, 1)

            def evac(key, n, out, src, sem_, scale=1.0):
                act.activation(out, src, ACT.Copy, scale=scale)
                act.drain().then_inc(free_sem(key, n), 1)
                act.drain().then_inc(sem_, 1)

            def s5pt():
                flat = PT5.rearrange("p m j q -> p (m j q)")
                act.wait_ge(s_u5, 48)
                act.activation(ug, usb.rearrange("p s (g h) -> p g s h", g=G5), ACT.Copy)
                act.drain().then_inc(s_ug, 1)
                for n in range(4):
                    act.wait_ge(*filled("pt", n))
                    evac("pt", n, flat[:, 1024 * n:1024 * n + 1024], slot("pt", n)[:, :], s_pt5)

            def s5k():
                act.wait_ge(*filled("U", 7))
                for n in range(4):
                    act.wait_ge(*filled("k", n))
                    evac("k", n, Ksb[:, 8 * n:8 * n + 8, :].rearrange("p (j e) q -> p e j q", e=2),
                         slot("k", n)[:, :].rearrange("p (e j q) -> p e j q", e=2, j=4), s_ks)

            def s5u(n):
                act.wait_ge(*filled("pt", 3))
                act.wait_ge(*filled("U", n))
                act.activation(U[:, 4 * n:4 * n + 4, 0:NC],
                               slot("U", n)[:, 0:512].rearrange("p (g c) -> p g c", g=4), ACT.Copy)
                evac("U", n, U[:, 4 * n:4 * n + 4, NC:NC + 16],
                     slot("U", n)[:, 512:576].rearrange("p (g c) -> p g c", g=4), s_Us)

            def s5x(n):
                act.wait_ge(*filled("X", n))
                if n == 0:
                    act.wait_ge(s_Tz, 2)
                for j in range(2):
                    act.activation(Hs[:, :, 2 * n + j, 1:145],
                                   slot("X", n)[:, 512 * j:512 * j + 288].rearrange("p (m c) -> p m c", m=2), ACT.Copy)
                act.drain().then_inc(free_sem("X", n), 1)
                act.drain().then_inc(s_Xs, 1)

            def s5g(n):
                act.wait_ge(s_th, 2 * n + 1)
                t = tmp5[0:NB, 0:512] if n == 2 else tmp5[:, 2048 * (n % 2):2048 * (n % 2) + 2048]
                act.activation(t, t, ACT.Tanh, scale=GELU_C).then_inc(s_g5, 1)

            def s5t(n):
                act.wait_ge(*filled("yT", n))
                if n == 0:
                    act.wait_ge(s_Td, 16 * CH)
                if n < 4:
                    for s in range(2):
                        act.activation(yT[:, :, 2 * n + s:SEQ:CH],
                                       slot("yT", n)[:, 512 * s:512 * s + 512].rearrange("p (k c) -> p k c", k=4),
                                       ACT.Copy, scale=0.5)
                else:
                    act.activation(yT[:, :, SEQ:TT], slot("yT", n)[:, 0:4 * NB].rearrange("p (k c) -> p k c", k=4),
                                   ACT.Copy, scale=0.5)
                act.drain().then_inc(free_sem("yT", n), 1)
                act.drain().then_inc(s_yT, 1)

            def glu(n):
                act.wait_ge(*filled("z", n))
                if n >= 2:
                    act.wait_ge(s_mix2, n - 1)
                t = tmp5[:, 1024 * (n % 2):1024 * (n % 2) + 1024]
                if n < 4:
                    act.activation(t, slot("z", n)[:, :], ACT.Tanh, bias=bglu[:, n:n + 1], scale=0.5)
                else:
                    for m in range(4):
                        act.activation(t[:, NB * m:NB * m + NB], slot("z", n)[:, NB * m:NB * m + NB], ACT.Tanh,
                                       bias=bglu[:, m:m + 1], scale=0.5)
                act.drain().then_inc(free_sem("z", n), 1)
                act.drain().then_inc(s_zt, 1)

            def ht(i):
                r = 128 if i < NT else NB
                act.wait_ge(s_xo, i + 1)
                if i >= 2:
                    act.wait_ge(s_hst[i % 2], 16 * (i // 2))
                    act.wait_ge(*filled("hT", i - 2))
                act.activation(h2[0:r, i % 2, :], x1[0:r, i, :], ACT.Square,
                               accum_out=st[0:r, 28:29]).then_inc(s_sq2, 1)

            def route():
                act.wait_ge(s_rexp, 1)
                e = rtf[:, 0:45]
                act.activation(e, e, ACT.Exp).then_inc(s_rex2, 1)

            later = {"s5a": s5a, "s5pt": s5pt, "s5k": s5k, "s5u": s5u, "s5x": s5x, "s5g": s5g, "s5t": s5t,
                     "glu": glu, "ht": ht, "route": route}
            act.wait_ge(s_lam, 1)
            act.activation(lamt[:, 2:4], lamt[:, 0:2], ACT.Exp).then_inc(s_lam, 1)
            todo = {"stats": stats, "dqkv": dqkv, "u": u, "qk": qk_, "v": v, "qt": qt, "s": s, "av": av,
                    "ot": ot, "m3": m3, "K": K, "pt": pt, **later}
            for unit in PLAN:
                if unit[0] in todo:
                    todo[unit[0]](*unit[1:])

            def tanh(q, v):
                act.wait_ge(m_gu, 4 * q + (v + 1))
                act.activation(tg[v % 2], W[2][:, 512 * (v % 2):512 * (v % 2) + 256], ACT.Tanh, scale=0.5)\
                    .then_inc(m_th, 1)

            def turned(q, v):
                act.wait_ge(m_heT, 4 * q + (v + 1))
                act.activation(heT_[v % 2], (SC, OD)[v % 2][:, 0:256], ACT.Copy, scale=0.5).then_inc(m_heS, 1)

            def store(q, v, first=False):
                act.wait_ge(m_y, 4 * q + (v + 1))
                if not (first and v < 2):
                    act.wait_ge(m_st[v % 2], 32 * q + 16 * (v // 2))
                act.activation(yb[v % 2], W[1][:, :], ACT.Copy).then_inc(m_ys, 1)
                act.wait_ge(m_ys, 4 * q + (v + 1))
                act.dma_start(io["y_scratch"][bass.ds(512 * q + 128 * v, 128), :], yb[v % 2]).then_inc(m_st[v % 2], 16)

            def step(q, v, first=False, last=False):
                turned(q, v)
                if not (last and v == 3):
                    tanh(q, v + 1)
                store(q, v, first)

            act.wait_ge(s_route, 1)
            n4 = act.value_load(plan_t[0:1, MAXT:MAXT + 1], min_val=NE // 4, max_val=MAXT // 4)
            n3 = act.value_load(plan_t[0:1, MAXT + 1:MAXT + 2], min_val=NE // 4 - 1, max_val=MAXT // 4 - 1)
            tanh(0, 0)
            for v in range(4):
                step(0, v, first=True)
            with act.Fori(1, n3) as q:
                for v in range(4):
                    step(q, v)
            for v in range(4):
                step(n3, v, last=True)
            for n in range(2):
                act.wait_ge(m_st[n], 32 * n4)
            act.nop().then_inc(s_stored, 1)
            for i in range(NT + 1):
                act.wait_ge(f_x, i + 1)
                r = 128 if i < NT else NB
                act.activation(yb[0][0:r, :], x1[0:r, i, :], ACT.Square, accum_out=st[0:r, i:i + 1]).then_inc(f_sq, 1)

        @block.vector
        def _(dve):
            def root(key):
                dve.drain().then_inc(s_ms, 1)
                dve.wait_ge(s_rs, POW[key] + 1)

            def mean_sq(out, in_, n):
                dve.tensor_scalar(out, in_, 1.0 / n, EPS, MUL, ADD)

            def rotate(x, rows, tile):
                v = x.rearrange("p (g d) -> p g d", d=HD)
                x1, x2 = v[:, :, 0:NROT], v[:, :, NROT:2 * NROT]
                cos = rope[0:rows, tile:tile + 1, 0:NROT].to_broadcast([rows, 16, NROT])
                sin = rope[0:rows, tile:tile + 1, NROT:].to_broadcast([rows, 16, NROT])
                t = [rt[0:rows, :, :, j] for j in range(4)]
                dve.tensor_tensor(t[0], x1, cos, MUL)
                dve.tensor_tensor(t[1], x2, sin, MUL)
                dve.tensor_tensor(t[2], x2, cos, MUL)
                dve.tensor_tensor(t[3], x1, sin, MUL)
                dve.drain()
                dve.tensor_tensor(x1, t[0], t[1], SUB)
                dve.tensor_tensor(x2, t[2], t[3], ADD)
                dve.drain()

            def lam():
                dve.wait_ge(s_lamv, 16)
                dve.tensor_tensor(lamv[:, 0, :], lamv[:, 0, :], lamv[:, 1, :], MUL)
                dve.tensor_tensor(lamv[:, 2, :], lamv[:, 2, :], lamv[:, 3, :], MUL)
                dve.drain()
                dve.reduce_sum(lamt[:, 0:1], lamv[:, 0, :], AX)
                dve.reduce_sum(lamt[:, 1:2], lamv[:, 2, :], AX)
                dve.drain().then_inc(s_lam, 1)
                dve.wait_ge(s_lam, 2)
                dve.tensor_tensor(lamt[:, 4:5], lamt[:, 3:4], lamt[:, 2:3], SUB)
                dve.drain()
                dve.tensor_scalar(lamt[:, 7:8], lamt[:, 4:5], -LINIT, None, ADD)
                dve.drain()

            def stats():
                lam()
                dve.wait_ge(s_cst, 112)
                dve.wait_ge(*filled("ss"))
                dve.memset(rstd[:, 2 * NT:2 * NT + 1], 1.0)
                dve.scalar_tensor_tensor(wmap[:, 0, :], consts[:, C_M1:C_M1 + H], lamt[:, 7:8],
                                         consts[:, C_M0:C_M0 + H], MUL, ADD)
                dve.drain()
                mean_sq(rstd[:, 0:2 * NT], slot("ss")[:, 0:2 * NT], D)
                mean_sq(rstd[0:NB, 2 * NT:2 * NT + 1], slot("ss")[0:NB, 2 * NT:2 * NT + 1], D)
                root(("stats",))
                dve.drain().then_inc(free_sem("ss"), 1)
                dve.tensor_scalar(bglu[:, :], bglu[:, :], 0.5, None, MUL)
                dve.memset(logit[:, NT, :], 0.0)
                dve.memset(st[:, :], 1.0)
                dve.tensor_scalar(colw[:, 2 * KD:2 * KD + 1], colw[:, 2 * KD:2 * KD + 1], 1.0 - LINIT, None, MUL)
                dve.drain().then_inc(s_rstd, 1)

            def dqkv():
                dve.wait_ge(s_dq, 1)
                r = rstd[0:NB, 2 * NT:2 * NT + 1]
                dve.tensor_scalar(qk[0:NB, :], qk[0:NB, :], r, None, MUL)
                dve.tensor_scalar(dvu[:, :], dvu[:, :], r, None, MUL)
                dve.drain()
                rotate(qk[0:NB, :], NB, NT)
                dve.drain().then_inc(s_drope, 1)

            def dprep():
                dve.wait_ge(s_qbd, 1)
                dve.wait_ge(*filled("dqt"))
                src = slot("dqt")[:, 0:2 * H * NB].rearrange("p (a h b) -> p a h b", a=2, h=H)
                for h in range(H):
                    for c in range(2):
                        dve.tensor_copy(qpad[64 * c:64 * c + 64, h, :, 2 * h + c], src[64 * c:64 * c + 64, 0, h, :])
                dve.tensor_copy(knT[:, :, :], src[:, 1, :, :])
                dve.drain().then_inc(free_sem("dqt"), 1)
                dve.drain().then_inc(s_qbd, 1)

            def v(i):
                dve.wait_ge(s_qk, i + 1)
                rotate(qk, 128, i)
                dve.drain().then_inc(s_rope, 1)

            def s(i, h):
                n, w = H * i + h, 128 * (i + 1)
                for c in range(2):
                    dve.wait_ge(*filled("S", i, h, c))
                    S = slot("S", i, h, c)
                    dve.tensor_tensor(S[:, 128 * i:w], S[:, 128 * i:w], causal, ADD)
                    dve.drain()
                    dve.reduce_max(st[:, 8 + c:9 + c], S[:, 0:w], AX)
                    dve.drain()
                    dve.tensor_scalar(st[:, 4 * (n % 2) + c:4 * (n % 2) + c + 1], st[:, 8 + c:9 + c],
                                      -HD ** -0.5, None, MUL)
                    dve.drain().then_inc(s_mx, 1)
                dve.wait_ge(s_exp, 2 * n + 2)
                l0, l1 = (st[:, 4 * (n % 2) + 2 + c:4 * (n % 2) + 3 + c] for c in range(2))
                r0, r1, cf = (st[:, 16 + 4 * (n % 2) + c:17 + 4 * (n % 2) + c] for c in range(3))
                dve.reciprocal(r0, l0)
                dve.reciprocal(r1, l1)
                dve.drain()
                dve.scalar_tensor_tensor(cf, l0, lamt[:, 7:8], r1, MUL, MUL)
                dve.drain()
                dve.scalar_tensor_tensor(P[:, n % 2, 0, 0:w], P[:, n % 2, 1, 0:w], cf,
                                         P[:, n % 2, 0, 0:w], MUL, ADD)
                dve.drain().then_inc(s_comb, 1)

            def av(i, h):
                n = H * i + h
                dve.wait_ge(*filled("O", i, h))
                if h == 0 and i >= 1:
                    dve.wait_ge(*filled("oT", i - 1))
                o = att[:, 128 * h:128 * h + 128]
                dve.tensor_scalar(o, slot("O", i, h)[:, 0:VD], st[:, 16 + 4 * (n % 2):17 + 4 * (n % 2)], None, MUL)
                dve.drain().then_inc(free_sem("O", i, h), 1)
                dve.tensor_tensor(rtf[:, 0:128], o, o, MUL)
                dve.drain()
                dve.reduce_sum(st[:, 24 + h:25 + h], rtf[:, 0:128], AX)
                dve.drain()
                if h == H - 1:
                    mean_sq(st[:, 24:28], st[:, 24:28], VD)
                    root(("av", i, h))
                    dve.tensor_tensor(att.rearrange("p (h d) -> p h d", h=H), att.rearrange("p (h d) -> p h d", h=H),
                                      st[:, 24:28].unsqueeze(2).to_broadcast([128, H, VD]), MUL)
                    dve.drain().then_inc(s_att, 1)

            def m1(b):
                if b >= 1:
                    dve.wait_ge(s_ptw, b)
                dve.memset(snew[:, :], NEG)
                dve.drain()
                dve.wait_ge(s_nk, b + 1)
                dve.tensor_tensor(snew[0:32, :], nkP, consts[0:32, C_NEG + 8 * b:C_NEG + 8 * b + 8], ADD)
                dve.wait_ge(s_evac, 2 * TURNS * (b + 1))
                dve.drain()
                dve.reduce_max(mrow[:, 0:1], sall[:, :, :].rearrange("p t n -> p (t n)"), AX)
                dve.reduce_max(mrow[:, 1:2], snew[:, :], AX)
                dve.drain()
                dve.tensor_tensor(mrow[:, 0:1], mrow[:, 0:1], mrow[:, 1:2], MAX)
                dve.drain().then_inc(s_m1, 1)

            def m2(b):
                dve.wait_ge(s_mT, b + 1)
                dve.reduce_max(mrep[:, 0, :], mxT.rearrange("a (j e) -> a e j", j=4), AX)
                dve.drain()
                dve.tensor_copy(mrep[:, 1:4, :], mrep[:, 0:1, :].to_broadcast([1, 3, 32]))
                dve.drain().then_inc(s_mrep, 1)

            def m3(b):
                dve.wait_ge(s_mb, b + 1)
                dve.tensor_scalar(mrow[:, 1:2], mbP, -HD ** -0.5, None, MUL)
                dve.drain().then_inc(s_nb, 1)

            def pt(b):
                dve.wait_ge(s_pexp, b + 1)
                dve.tensor_tensor(mrow[:, 2:3], mrow[:, 2:3], mrow[:, 3:4], ADD)
                dve.drain().then_inc(s_l, 1)

            def ov(b):
                dve.wait_ge(s_lP, b + 1)
                dve.wait_ge(s_pv, b + 1)
                dve.tensor_copy(o4s[:, :], SC[:, :])
                dve.reciprocal(mrow[:, 4:5], lP)
                dve.drain()
                dve.tensor_scalar(wmap[:, 1, :], wmap[:, 0, :], mrow[:, 4:5], None, MUL)
                dve.drain().then_inc(s_o4, 1)
                dve.wait_ge(s_aP, b + 1)
                dve.tensor_copy(aD[:, :, b], aP)
                dve.drain().then_inc(s_ad, 1)

            def dout():
                dve.tensor_tensor(aD2[:, :, :], aD[:, :, :], aD[:, :, :], MUL)
                dve.drain().then_inc(s_ad2, 1)
                dve.wait_ge(*filled("dss"))
                mean_sq(aD2[:, :, :], slot("dss")[:, 0:H * NB].rearrange("p (h b) -> p h b", h=H), VD)
                root(("dout",))
                dve.drain().then_inc(free_sem("dss"), 1)
                dve.tensor_tensor(aD2[:, :, :], aD2[:, :, :], aD[:, :, :], MUL)
                dve.drain()
                dve.tensor_scalar(xm[:, 0:H, SEQ:TT], aD2[:, :, :], colw[:, 2 * KD:2 * KD + 1], None, MUL)
                dve.drain().then_inc(s_dmix, 1)

            def cmul(out, a, b, t, neg_im=False):
                dve.tensor_tensor(out[0], a[0], b[0], MUL)
                dve.tensor_tensor(t[0], a[1], b[1], MUL)
                dve.tensor_tensor(out[1], a[0], b[1], MUL)
                dve.tensor_tensor(t[1], a[1], b[0], MUL)
                dve.drain()
                dve.tensor_tensor(out[0], out[0], t[0], SUB)
                if neg_im:
                    dve.scalar_tensor_tensor(out[1], out[1], -1.0, t[1], MUL, SUB)
                else:
                    dve.tensor_tensor(out[1], out[1], t[1], ADD)
                dve.drain()

            def s5a():
                dve.wait_ge(s_ld5, 32)
                dve.wait_ge(s_act5, 1)
                v = [sm5[:, a, :] for a in range(20)]
                dve.tensor_tensor(v[1], par[:, 0, :], v[0], MUL)
                dve.tensor_tensor(v[2], par[:, 1, :], v[0], MUL)
                dve.drain()
                dve.tensor_scalar(v[8], v[2], float(1 / (2 * np.pi)), None, MUL)
                dve.drain()
                dve.tensor_scalar(v[8], v[8], MAGIC, None, ADD)
                dve.drain()
                dve.tensor_scalar(v[8], v[8], MAGIC, None, SUB)
                for c in (6.28125, 0.001934051513671875, float(2 * np.pi - 6.28125 - 0.001934051513671875)):
                    dve.drain()
                    dve.scalar_tensor_tensor(v[2], v[8], -c, v[2], MUL, ADD)
                dve.drain()
                dve.tensor_scalar(v[4], v[2], 3.1415925, -3.1415925, MIN, MAX)
                dve.drain()
                dve.scalar_tensor_tensor(v[5], v[4], -1.0, v[4], MUL, MAX)
                dve.drain()
                dve.tensor_scalar(v[5], v[5], -1.0, float(np.pi / 2), MUL, ADD)
                dve.drain().then_inc(s_dve5, 1)
                dve.wait_ge(s_act5, 3)
                dve.memset(Lp[:, 0, 0, :], 1.0)
                dve.memset(Lp[:, 1, 0, :], 0.0)
                dve.tensor_tensor(Lp[:, 0, 1, :], v[3], v[7], MUL)
                dve.tensor_tensor(Lp[:, 1, 1, :], v[3], v[6], MUL)
                dve.drain()
                t = (v[16], v[17])
                L = [(Lp[:, 0, k, :], Lp[:, 1, k, :]) for k in range(CH + 1)]
                for k in range(2, CH + 1):
                    cmul(L[k], L[k - 1], L[1], t)
                for k in range(CH):
                    dve.tensor_copy(LpR[:, :, :, CH - 1 - k], Lp[:, :, k, :])
                dve.tensor_scalar(v[8], L[1][0], -1.0, None, ADD)
                dve.tensor_scalar(v[9], par[:, 1, :], -1.0, None, MUL)
                dve.tensor_tensor(v[10], par[:, 0, :], par[:, 0, :], MUL)
                dve.tensor_tensor(v[11], par[:, 1, :], par[:, 1, :], MUL)
                dve.drain()
                dve.tensor_tensor(v[10], v[10], v[11], ADD)
                dve.drain()
                dve.reciprocal(v[10], v[10])
                cmul((v[12], v[13]), (v[8], L[1][1]), (par[:, 0, :], v[9]), t)
                dve.tensor_tensor(v[12], v[12], v[10], MUL)
                dve.tensor_tensor(v[13], v[13], v[10], MUL)
                dve.drain()
                full = [128, NP5, W5]
                f = [v[12 + m].unsqueeze(2).to_broadcast(full) for m in range(2)]
                t0 = [tmp5[:, 256 * m:256 * m + 256].rearrange("p (j h) -> p j h", j=NP5) for m in range(4)]
                dve.tensor_copy(t0[2], bc[:, 0, 0, :, :])
                dve.tensor_copy(t0[3], bc[:, 0, 1, :, :])
                dve.drain()
                B = (bc[:, 0, 0, :, :], bc[:, 0, 1, :, :])
                cmul(B, (t0[2], t0[3]), f, t0[0:2])
                full = [128, NP5, CH, W5]
                t1 = [tmp5[:, 2048 * m:2048 * m + 2048].rearrange("p (j s h) -> p j s h", j=NP5, s=CH) for m in range(2)]
                cmul((PB[:, 0, :, :, :], PB[:, 1, :, :, :]),
                     [b.unsqueeze(2).to_broadcast(full) for b in B],
                     [LpR[:, m, :, :].unsqueeze(3).to_broadcast(full) for m in range(2)], t1)
                dve.drain().then_inc(s_dve5, 1)
                full = [128, NP5, CH + 1, W5]
                t2 = [region(13312 + 2304 * m, 2304, "p (j k h) -> p j k h", j=NP5, k=CH + 1) for m in range(2)]
                cmul((CLr, CLn), [bc[:, 1, m, :, :].unsqueeze(2).to_broadcast(full) for m in range(2)],
                     [Lp[:, m, :, :].rearrange("p k j -> p j k").unsqueeze(3).to_broadcast(full) for m in range(2)],
                     t2, neg_im=True)
                for m in range(2):
                    dve.tensor_copy(Bt[:, m, :, :, :], B[m].unsqueeze(2).to_broadcast([128, NP5, CH, W5]))
                dve.drain().then_inc(s_dve5, 1)

            def s5h():
                dve.wait_ge(s_Xs, 8)
                dve.wait_ge(s_h0, 32)
                t = [tmp5[:, 128 * a:128 * a + 128].rearrange("p (j b) -> p j b", j=NP5) for a in range(2)]
                full = [128, NP5, NB]
                cmul((hs8[:, 0, :, :], hs8[:, 1, :, :]), [Hs[:, m, :, NC + 1:NC + 1 + NB] for m in range(2)],
                     [Lp[:, m, 1, :].unsqueeze(2).to_broadcast(full) for m in range(2)], t)
                for m in range(2):
                    dve.tensor_tensor(hs8[:, m, :, :], hs8[:, m, :, :], Hs[:, m, :, NC + 1 + NB:NC + 1 + 2 * NB], ADD)
                dve.drain()
                A, nxt, t = (Lp[:, 0, CH, :], Lp[:, 1, CH, :]), 0, (sm5[:, 16, :], sm5[:, 17, :])
                dve.wait_ge(s_Td, 16 * CH)
                d = 1
                while d < NC:
                    n = NC - d
                    full = [128, NP5, n]
                    lo = [Hs[:, m, :, 1:1 + n] for m in range(2)]
                    hi = [Hs[:, m, :, 1 + d:1 + NC] for m in range(2)]
                    q = [(tmp5 if a < 2 else tmp5b)[:, 2048 * (a % 2):2048 * (a % 2) + NP5 * n]
                         .rearrange("p (j c) -> p j c", j=NP5) for a in range(4)]
                    Ab = [a.unsqueeze(2).to_broadcast(full) for a in A]
                    dve.tensor_tensor(q[0], lo[0], Ab[0], MUL)
                    dve.tensor_tensor(q[1], lo[1], Ab[1], MUL)
                    dve.tensor_tensor(q[2], lo[1], Ab[0], MUL)
                    dve.tensor_tensor(q[3], lo[0], Ab[1], MUL)
                    B = (sm5[:, nxt, :], sm5[:, nxt + 1, :])
                    cmul(B, A, A, t)
                    dve.tensor_tensor(hi[0], hi[0], q[0], ADD)
                    dve.tensor_tensor(hi[1], hi[1], q[2], ADD)
                    dve.drain()
                    dve.tensor_tensor(hi[0], hi[0], q[1], SUB)
                    dve.tensor_tensor(hi[1], hi[1], q[3], ADD)
                    dve.drain()
                    A, nxt, d = B, nxt + 2, 2 * d
                dve.tensor_copy(hp, Hs[:, :, :, NC])
                dve.drain().then_inc(s_scan, 1)

            def s5y(n):
                if n == 0:
                    dve.wait_ge(s_du, 1)
                dve.wait_ge(*filled("Y", n))
                out = usb[:, :, 64 * n:64 * n + 64].rearrange("p s (g h) -> p g s h", g=4)
                for g in range(4):
                    dve.tensor_tensor(out[:, g, :, :], out[:, g, :, :],
                                      slot("Y", n)[:, 512 * (g % 2) + 128 * (g // 2):512 * (g % 2) + 128 * (g // 2) + 128]
                                      .rearrange("p (s h) -> p s h", s=CH), ADD)
                o = dvu[:, QKW + 64 * n:QKW + 64 * n + 64].rearrange("p (j e h) -> p e j h", j=2, e=2)
                dve.tensor_tensor(o, o, slot("Y", n)[0:NB, :].rearrange("p (e c) -> p e c", e=2)[:, :, 256:288]
                                  .rearrange("p e (j h) -> p e j h", j=2), ADD)
                dve.drain().then_inc(free_sem("Y", n), 1)

            def s5g(n):
                if n == 2:
                    x, t = dvu[:, QKW:2 * QKW], tmp5[0:NB, 0:512]
                    dve.wait_ge(s_th, 2)
                else:
                    x = usb[:, 4 * n:4 * n + 4, :].rearrange("p s n -> p (s n)")
                    t = tmp5[:, 2048 * n:2048 * n + 2048]
                dve.tensor_tensor(t, x, x, MUL)
                dve.drain()
                dve.tensor_scalar(t, t, 0.044715, 1.0, MUL, ADD)
                dve.drain()
                dve.tensor_tensor(t, t, x, MUL)
                dve.drain().then_inc(s_th, 1)
                dve.wait_ge(s_g5, n + 1)
                dve.scalar_tensor_tensor(x, t, 1.0, x, ADD, MUL)
                dve.drain().then_inc(s_th, 1)

            def glu(n):
                if n == 0:
                    dve.wait_ge(*filled("Y", 7))
                dve.wait_ge(s_zt, n + 1)
                t = tmp5[:, 1024 * (n % 2):1024 * (n % 2) + 1024]
                if n < 4:
                    out, y = xm[:, 4 + n, 0:SEQ], yT[:, n, 0:SEQ]
                else:
                    t = t[:, 0:4 * NB]
                    out, y = xm[:, 4:8, SEQ:TT], yT[:, :, SEQ:TT]
                dve.tensor_scalar(t, t, 0.5, 0.5, MUL, ADD)
                dve.drain()
                dve.tensor_tensor(out, t if n < 4 else t.rearrange("p (k b) -> p k b", k=4), y, MUL)
                dve.drain().then_inc(s_mix2, 1)

            def out_(i):
                r = 128 if i < NT else NB
                dve.wait_ge(s_x1, 16 * (NT + 1))
                dve.wait_ge(*filled("o", i))
                dve.tensor_tensor(x1[0:r, i, :], x1[0:r, i, :], slot("o", i)[0:r, :], ADD)
                dve.drain().then_inc(free_sem("o", i), 1)
                dve.drain().then_inc(s_xo, 1)

            def ht(i):
                r = 128 if i < NT else NB
                dve.wait_ge(s_sq2, i + 1)
                mean_sq(st[:, 28:29], st[:, 28:29], D)
                root(("ht", i))
                dve.tensor_scalar(h2[0:r, i % 2, :], x1[0:r, i, :], st[0:r, 28:29], None, MUL)
                dve.drain().then_inc(s_h2, 1)
                dve.wait_ge(*filled("hT", i))
                if i >= 2:
                    dve.wait_ge(*filled("r", i - 2))
                dve.tensor_tensor(h2T[:, i % 2, :, 0:r], slot("hT", i)[:, :].rearrange("p (k n) -> p k n", k=KD)[:, :, 0:r],
                                  colw[:, KD:2 * KD].unsqueeze(2).to_broadcast([128, KD, r]), MUL)
                dve.drain().then_inc(free_sem("hT", i), 1)
                dve.drain().then_inc(s_h2T, 1)
                dve.wait_ge(*filled("r", i))
                dve.tensor_tensor(logit[0:r, i, :], slot("r", i)[0:r, 0:36], br[0:r, :], ADD)
                dve.drain().then_inc(free_sem("r", i), 1)

            def route():
                for n in range(2):
                    dve.wait_ge(s_hst[n], 16 * ((NT + 2 - n) // 2))
                dve.wait_ge(s_fx, 32)
                T9, EQ, used = NT + 1, ALU.is_equal, [27648]
                dve.drain()

                def small(*shape):
                    n = int(np.prod(shape))
                    v = region(used[0], n)
                    used[0] += n
                    return v if len(shape) == 1 else v.rearrange("p (a b) -> p a b", a=shape[0])

                def wide(x, n):
                    return x.unsqueeze(2).to_broadcast([128, T9, n])

                def row(c, n):
                    return consts[:, c:c + n].unsqueeze(1).to_broadcast([128, T9, n])

                def first_max(x, n, top, v, hot):
                    dve.reduce_max(top, x, AX)
                    dve.drain()
                    dve.tensor_tensor(v, x, wide(top, n), EQ)
                    dve.drain()
                    dve.scalar_tensor_tensor(v, v, -8.0, row(C_I8, n), MUL, ADD)
                    dve.drain()
                    dve.tensor_reduce(f9, v, AX, MIN)
                    dve.drain()
                    dve.tensor_tensor(hot, v, wide(f9, n), EQ)
                    dve.drain()

                rf = rtf
                ex, exg = rf[:, 0:45], rf[:, 0:36].rearrange("p (t n) -> p t n", t=T9)
                over, incl, B = rf[:, 64:96], rf[:, 96:128], rf[:, 128:160]
                zero = rf[:, 160:192]
                big = region(19456, 288)
                f9, gtop, gsum, t1, t2 = (small(T9) for _ in range(5))
                v4, ghot = small(T9, NG), small(T9, NG)
                el, v8, hot1, hot2 = (small(T9, EG) for _ in range(4))
                gl, els = logit[:, :, 0:NG], logit[:, :, NG:].rearrange("p t (g e) -> p t g e", g=NG)
                first_max(gl, NG, gtop, v4, ghot)
                dve.tensor_tensor(exg, gl, wide(gtop, NG), SUB)
                b4 = big.rearrange("p (t g e) -> p t g e", t=T9, g=NG)
                gh4 = ghot.unsqueeze(3).to_broadcast([128, T9, NG, EG])
                dve.tensor_tensor(b4, els, gh4, MUL)
                dve.drain()
                dve.reduce_sum(el, b4.rearrange("p t g e -> p t e g"), AX)
                dve.drain()
                first_max(el, EG, t1, v8, hot1)
                dve.scalar_tensor_tensor(el, hot1, NEG, el, MUL, ADD)
                dve.drain()
                first_max(el, EG, t2, v8, hot2)
                dve.tensor_tensor(ex[:, 36:45], t2, t1, SUB)
                dve.drain().then_inc(s_rexp, 1)
                valid = consts[:, C_VAL:C_VAL + T9]
                for c, hot in enumerate((hot1, hot2)):
                    dve.tensor_tensor(hot, hot, wide(valid, EG), MUL)
                dve.memset(OHs[:, T9, :], 0.0)
                dve.drain()
                for c, hot in enumerate((hot1, hot2)):
                    dve.tensor_tensor(OH[c].rearrange("p t (g e) -> p t g e", g=NG), gh4,
                                      hot.unsqueeze(2).to_broadcast([128, T9, NG, EG]), MUL)
                dve.drain()
                dve.tensor_tensor(OHs[:, 0:T9, :], OH[0], OH[1], ADD)
                dve.drain().then_inc(s_oh, 1)
                dve.wait_ge(s_rex2, 1)
                dve.reduce_sum(gsum, exg, AX)
                dve.tensor_scalar(t1, ex[:, 36:45], 1.0, None, ADD)
                dve.drain()
                dve.tensor_tensor(gsum, gsum, t1, MUL)
                dve.drain()
                dve.reciprocal(wts[:, 0, :], gsum)
                dve.drain()
                dve.tensor_tensor(wts[:, 1, :], wts[:, 0, :], ex[:, 36:45], MUL)
                dve.memset(zero, 0.0)
                dve.wait_ge(*filled("rank"))
                rank = slot("rank")[:, 0:288].rearrange("p (t e) -> p t e", t=T9)
                total = slot("rank")[:, 288:320]
                c8 = big[:, 0:256].rearrange("p (e m) -> p e m", m=EG)
                thr = consts[:, C_THR + 1:C_THR + 9].unsqueeze(1)
                dve.tensor_tensor(c8, total.unsqueeze(2).to_broadcast([128, NE, EG]), thr.to_broadcast([128, NE, EG]),
                                  ALU.is_gt)
                dve.drain()
                dve.reduce_sum(over, c8, AX)
                dve.drain()
                dve.tensor_tensor_scan(incl, zero, over, 0.0, ADD, ADD)
                dve.drain()
                dve.scalar_tensor_tensor(B, incl, float(NE - 1), over, ADD, SUB)
                dve.drain()
                dve.tensor_tensor(B, B, consts[:, C_I32:C_I32 + NE], SUB)
                dve.drain()
                r9, q9, e9, b9, g9 = f9, gtop, gsum, t1, t2
                c9 = v8
                big3 = big.rearrange("p (t e) -> p t e", t=T9)
                for c in range(2):
                    for src, out in ((rank, r9), (row(C_I32, NE), e9), (B.unsqueeze(1).to_broadcast([128, T9, NE]), b9)):
                        dve.tensor_tensor(big3, OH[c], src, MUL)
                        dve.drain()
                        dve.reduce_sum(out, big3, AX)
                        dve.drain()
                    dve.tensor_tensor(c9, wide(r9, EG), thr.to_broadcast([128, T9, EG]), ALU.is_ge)
                    dve.drain()
                    dve.reduce_sum(q9, c9, AX)
                    dve.drain()
                    dve.scalar_tensor_tensor(r9, q9, -128.0, r9, MUL, ADD)
                    dve.tensor_scalar(g9, q9, 0.0, None, ALU.is_gt)
                    dve.tensor_tensor(e9, e9, q9, ADD)
                    dve.drain()
                    dve.tensor_tensor(g9, g9, b9, MUL)
                    dve.drain()
                    dve.tensor_tensor(e9, e9, g9, ADD)
                    dve.drain()
                    dve.scalar_tensor_tensor(g9, e9, 128.0, r9, MUL, ADD)
                    dve.tensor_tensor(TO[c], row(C_TI, MAXT), wide(e9, MAXT), EQ)
                    dve.drain()
                    dve.tensor_copy(rows[:, c, :], g9)
                    dve.tensor_tensor(TO[c], TO[c], wide(consts[:, C_TOK:C_TOK + T9], MAXT), MUL)
                    if c == 1:
                        dve.tensor_tensor(R[1], row(C_TI, 128), wide(r9, 128), EQ)
                        dve.tensor_tensor(R[0], row(C_TI, 128), wide(v4[:, :, 0], 128), EQ)
                    else:
                        dve.tensor_copy(v4[:, :, 0], r9)
                    dve.drain()
                dve.drain().then_inc(s_lst, 1)
                dve.drain().then_inc(free_sem("rank"), 1)
                k16 = consts[0:1, C_TI:C_TI + 16].unsqueeze(2).to_broadcast([1, 16, NE])
                cm = region(16512, 512, "p (k e) -> p k e", k=16)[0:1]
                te = rf[0:1, 256:256 + MAXT + 2]
                dve.tensor_tensor(cm, incl[0:1, :].unsqueeze(1).to_broadcast([1, 16, NE]), k16, ALU.is_le)
                dve.tensor_copy(te[:, 0:NE], consts[0:1, C_I32:C_I32 + NE])
                dve.tensor_scalar(zero[0:1, 0:4], consts[0:1, C_I8:C_I8 + 4], 4.0, None, MUL)
                dve.drain()
                dve.reduce_sum(te[:, NE:MAXT], cm, AX)
                dve.tensor_tensor(zero[0:1, 4:8], incl[0:1, NE - 1:NE].to_broadcast([1, 4]), zero[0:1, 0:4], ALU.is_gt)
                dve.drain()
                dve.tensor_scalar(te[:, NE:MAXT], te[:, NE:MAXT], float(NE - 1), None, MIN)
                dve.reduce_sum(te[:, MAXT:MAXT + 1], zero[0:1, 4:8], AX)
                dve.drain()
                dve.tensor_scalar(te[:, MAXT + 1:], te[:, MAXT:MAXT + 1], float(NE // 4 - 1), None, ADD)
                dve.tensor_scalar(te[:, MAXT:MAXT + 1], te[:, MAXT:MAXT + 1], float(NE // 4), None, ADD)
                dve.drain()
                dve.tensor_copy(plan_t[:, :], te)
                dve.wait_ge(*filled("ids"))
                dve.tensor_copy(ids[:, :], slot("ids")[:, 0:MAXT])
                dve.drain().then_inc(free_sem("ids"), 1)
                dve.drain().then_inc(s_route, 1)

            later = {"s5a": s5a, "s5h": s5h, "s5y": s5y, "s5g": s5g, "glu": glu, "out": out_, "ht": ht,
                     "route": route}
            todo = {"stats": stats, "dqkv": dqkv, "dprep": dprep, "v": v, "s": s, "av": av,
                    "m1": m1, "m2": m2, "m3": m3, "pt": pt, "ov": ov, "dout": dout, **later}
            for unit in PLAN:
                if unit[0] in todo:
                    todo[unit[0]](*unit[1:])

            def scale(q, v):
                dve.wait_ge(m_T, 4 * q + (v + 1))
                dve.tensor_tensor(hgT[v % 2], W[0][:, :].rearrange("p (k n) -> p k n", k=KD),
                                  colw[:, KD:2 * KD].unsqueeze(2).to_broadcast([128, KD, 128]), MUL).then_inc(m_hT, 1)

            def silu(q, v):
                gu = W[2][:, 512 * (v % 2):512 * (v % 2) + 512]
                dve.wait_ge(m_th, 4 * q + (v + 1))
                dve.scalar_tensor_tensor(he[v % 2], tg[v % 2], 1.0, gu[:, 0:DE], ADD, MUL)
                dve.drain()
                dve.tensor_tensor(he[v % 2], he[v % 2], gu[:, DE:], MUL).then_inc(m_he, 1)

            n3 = dve.value_load(plan_t[0:1, MAXT + 1:MAXT + 2], min_val=NE // 4 - 1, max_val=MAXT // 4 - 1)
            scale(0, 0)
            for v in range(4):
                silu(0, v)
                scale(0, v + 1)
            with dve.Fori(1, n3) as q:
                for v in range(4):
                    silu(q, v)
                    scale(q, v + 1)
            for v in range(4):
                silu(n3, v)
                if v < 3:
                    scale(n3, v + 1)

            def combine(i):
                r = 128 if i < NT else NB
                dve.wait_ge(f_g[i % 2], 32 * (i // 2 + 1))
                for c in range(2):
                    dve.scalar_tensor_tensor(x1[0:r, i, :], yg[i % 2][c][0:r, :], wts[0:r, c, i:i + 1],
                                             x1[0:r, i, :], MUL, ADD)
                    dve.drain()
                dve.drain().then_inc(f_x, 1)

            def norm(i):
                r = 128 if i < NT else NB
                dve.wait_ge(f_rs, i + 1)
                dve.scalar_tensor_tensor(x1[0:r, i, :], x1[0:r, i, :], st[0:r, i:i + 1], lnf[0:r, :], MUL, MUL)\
                    .then_inc(f_out, 1)

            dve.wait_ge(f_gf, 16)
            for i in range(NT + 1):
                combine(i)
                if i >= 1:
                    norm(i - 1)
                dve.wait_ge(f_sq, i + 1)
                mean_sq(st[:, i:i + 1], st[:, i:i + 1], D)
                dve.drain().then_inc(f_ms, 1)
            norm(NT)

        @block.tensor
        def _(pe):
            def mm(out, lhsT, rhs, first=True, last=True, **kw):
                return pe.matmul(out, lhsT, rhs, start=first, stop=last, **kw)

            def stats():
                pe.nop().then_inc(s_pgfree, RING // GRP)
                pe.wait_ge(s_cst, 112)
                ss = slot("ss")
                for k in range(KD):
                    pe.wait_ge(s_sq, k + 1)
                    for t in range(2 * NT + 1):
                        cols = (sq[:, k % 2, 128 * t:128 * t + 128] if t < NT else
                                sq[:, k % 2, t - NT:SEQ:CH] if t < 2 * NT else sq[:, k % 2, SEQ:TT])
                        last = mm(ss[0:(NB if t == 2 * NT else 128), t:t + 1], cols, ones[:, 0:1],
                                  k == 0 and t == 0, k == KD - 1, skip_group_check=True)
                    last.then_inc(s_sqread, 1)
                pe.wait_ge(s_sqread, KD)
                pe.nop().then_inc(full_sem("ss"), 1)

            def dqkv():
                pe.wait_ge(s_xg, KD)
                vacant(pe, "dp")
                for k in range(KD):
                    pe.wait_ge(s_wk[k], 32)
                    for n in range(4):
                        w = w_qkv[:, k, 512 * n:512 * n + 512] if n < 3 else w_u[:, k, :]
                        last = mm(slot("dp")[32 * n:32 * n + NB, 0:512], xm[:, k, SEQ:TT], w, k == 0, k == KD - 1)
                last.then_inc(full_sem("dp"), 1)

            def dprep():
                pe.wait_ge(s_drope, 1)
                vacant(pe, "dqt")
                for j in range(2 * H):
                    last = pe.transpose(slot("dqt")[:, NB * j:NB * j + NB], qk[0:NB, 128 * j:128 * j + 128],
                                        ident[0:NB, 0:NB])
                last.then_inc(full_sem("dqt"), 1)

            def u(s):
                vacant(pe, "u", s)
                for k in range(KD):
                    last = mm(slot("u", s)[:, 0:QKW], xm[:, k, s:SEQ:CH], w_u[:, k, :], k == 0, k == KD - 1)
                last.then_inc(full_sem("u", s), 1)

            def product(out, i, n):
                for k in range(KD):
                    last = mm(out, xm[:, k, 128 * i:128 * i + 128], w_qkv[:, k, 512 * n:512 * n + 512],
                              k == 0, k == KD - 1)
                return last

            def qk_(i, n):
                if n == 0:
                    vacant(pe, "qk", i)
                last = product(slot("qk", i)[:, 512 * n:512 * n + 512], i, n)
                if n == 1:
                    last.then_inc(full_sem("qk", i), 1)

            def v(i):
                vacant(pe, "v", i)
                product(slot("v", i)[:, 0:512], i, 2).then_inc(full_sem("v", i), 1)

            def qt(i):
                pe.wait_ge(s_rope, i + 1)
                vacant(pe, "qkT", i)
                for j in range(2 * H):
                    last = pe.transpose(slot("qkT", i)[:, 128 * j:128 * j + 128], qk[:, 128 * j:128 * j + 128], ident)
                last.then_inc(full_sem("qkT", i), 1)

            def s(i, h):
                w = 128 * (i + 1)
                pe.wait_ge(s_qkT, i + 1)
                for c in range(2):
                    vacant(pe, "S", i, h, c)
                    for a in range(0, w, 512):
                        b = min(w, a + 512)
                        last = mm(slot("S", i, h, c)[:, a:b], qT[64 * c:64 * c + 64, h, :],
                                  kT[64 * c:64 * c + 64, h, a:b])
                    last.then_inc(full_sem("S", i, h, c), 1)

            def av(i, h):
                n = H * i + h
                pe.wait_ge(s_comb, n + 1)
                vacant(pe, "AT", i, h)
                for j in range(i + 1):
                    last = pe.transpose(slot("AT", i, h)[:, 128 * j:128 * j + 128],
                                        P[:, n % 2, 0, 128 * j:128 * j + 128], ident)
                last.then_inc(full_sem("AT", i, h), 1)
                vacant(pe, "O", i, h)
                pe.wait_ge(s_ATs, n + 1)
                pe.wait_ge(s_v, i + 1)
                for j in range(i + 1):
                    last = mm(slot("O", i, h)[:, 0:VD], P[:, n % 2, 1, 128 * j:128 * j + 128],
                              V[:, j, VD * h:VD * h + VD], j == 0, j == i)
                last.then_inc(full_sem("O", i, h), 1)

            def ot(i):
                pe.wait_ge(s_att, i + 1)
                vacant(pe, "oT", i)
                for h in range(H):
                    last = pe.transpose(slot("oT", i)[:, 128 * h:128 * h + 128], att[:, 128 * h:128 * h + 128], ident)
                last.then_inc(full_sem("oT", i), 1)

            def K(b, t):
                if t == 0:
                    pe.wait_ge(s_qbd, 2)
                    if b >= 1:
                        pe.wait_ge(s_ad, b)
                for g in range(2):
                    pe.wait_ge(s_pg[g], 16 * GRP * (2 * TURNS * b + t + 1))
                    if t:
                        pe.wait_ge(s_evac, 2 * (TURNS * b + t) + g - 1)
                    for h in range(H):
                        for c in range(4):
                            last = mm((SC, OD)[g][32 * c:32 * c + 32, 0:256], qpad[:, h, b, :],
                                      ring[:, GRP * g + 2 * c:GRP * g + 2 * c + 2, 128 * h:128 * h + 128],
                                      h == 0, h == H - 1, skip_group_check=True)
                    last.then_inc(s_score, 1)
                    pe.wait_ge(s_score, 2 * (TURNS * b + t) + g + 1)
                    pe.nop().then_inc(s_pgfree, 1)

            def m1(b):
                pe.wait_ge(s_evac, 2 * TURNS * (b + 1))
                for h in range(H):
                    last = mm(nkP, qpad[:, h, b, :], knT[:, h, :], h == 0, h == H - 1)
                last.then_inc(s_nk, 1)

            def m2(b):
                pe.wait_ge(s_m1, b + 1)
                pe.transpose(mxT, mrow[:, 0:1], ident).then_inc(s_mT, 1)

            def m3(b):
                pe.wait_ge(s_mrep, b + 1)
                mm(mbP, mrep[:, :, :].rearrange("a j e -> a (j e)"), ones[0:1, 0:1]).then_inc(s_mb, 1)

            def pt(b):
                pe.wait_ge(s_pexp, b + 1)
                for n in range(2):
                    vacant(pe, "PT", b, n)
                    for j in range(8):
                        last = pe.transpose(slot("PT", b, n)[:, 128 * j:128 * j + 128],
                                            sall[:, 2 * n + j // 4, 128 * (j % 4):128 * (j % 4) + 128], ident)
                    last.then_inc(full_sem("PT", b, n), 1)
                vacant(pe, "PTn", b)
                pe.transpose(slot("PTn", b)[0:NB, 0:128], snew[:, :], ident).then_inc(full_sem("PTn", b), 1)
                pe.wait_ge(s_l, b + 1)
                mm(lP, consts[:, C_SUM:C_SUM + 128], mrow[:, 2:3]).then_inc(s_lP, 1)

            def Vv(b, r):
                if r == 0:
                    pe.wait_ge(s_ptw, b + 1)
                for g in range(2):
                    pe.wait_ge(s_pg[g], 16 * GRP * (2 * TURNS * b + TURNS + r + 1))
                    for j in range(GRP):
                        t, q, c = j // 2, j % 2, j % 4
                        blk = sall[:, r, 256 * g + 128 * q:256 * g + 128 * q + 128]
                        last = mm(SC[32 * c:32 * c + 32, :], blk[:, 32 * t:32 * t + 32], ring[:, GRP * g + j, :],
                                  r == 0 and g == 0 and j < 4, r == TURNS - 1 and g == 1 and j >= 4 and c > 0,
                                  skip_group_check=True)
                    last.then_inc(s_pgfree, 1)
                if r == TURNS - 1:
                    mm(SC[0:32, :], ptn[:, 0:32], dvu[:, 0:QKW], False, True, skip_group_check=True).then_inc(s_pv, 1)

            def ov(b):
                pe.wait_ge(s_o4, b + 1)
                for h in range(H):
                    last = mm(aP[:, h:h + 1], o4s[:, 128 * h:128 * h + 128], wmap[:, 1, h:h + 1])
                last.then_inc(s_aP, 1)

            def dout():
                pe.wait_ge(s_ad2, 1)
                vacant(pe, "dss")
                mm(slot("dss")[:, 0:H * NB], ones, aD2[:, :, :].rearrange("p h b -> p (h b)"))\
                    .then_inc(full_sem("dss"), 1)

            def s5pt():
                pe.wait_ge(s_dve5, 2)
                for n in range(4):
                    vacant(pe, "pt", n)
                    for q in range(8):
                        m, j = divmod(8 * n + q, NP5)
                        last = pe.transpose(slot("pt", n)[:, 128 * q:128 * q + 128],
                                            PB[:, m, j, :, :].rearrange("p s h -> p (s h)"), ident)
                    last.then_inc(full_sem("pt", n), 1)

            def s5k():
                pe.wait_ge(s_dve5, 3)
                for n in range(4):
                    vacant(pe, "k", n)
                    for q in range(8):
                        j, e = divmod(8 * n + q, 2)
                        p = slice(64 * e, 64 * e + 64)
                        for m, C in enumerate((CLr, CLn)):
                            c = 512 * e + 128 * (q // 2)
                            last = mm(slot("k", n)[:, c:c + 128],
                                      Bt[p, m, j, :, :].rearrange("p s h -> p (s h)"),
                                      C[p, j, 0:CH, :].rearrange("p s h -> p (s h)"), m == 0, m == 1)
                    last.then_inc(full_sem("k", n), 1)

            def s5u(n):
                if n == 0:
                    pe.wait_ge(s_ug, 1)
                vacant(pe, "U", n)
                for q in range(4):
                    g = 4 * n + q
                    pe.transpose(slot("U", n)[:, 128 * q:128 * q + 128], ug[:, g, :, :].rearrange("p s h -> p (s h)"), ident)
                    last = pe.transpose(slot("U", n)[:, 512 + 16 * q:512 + 16 * q + 16],
                                        Z[:, g, :, :].rearrange("p s h -> p (s h)"), ident[0:16, 0:16])
                last.then_inc(full_sem("U", n), 1)

            def s5x(n):
                pe.wait_ge(s_pt5, 4)
                pe.wait_ge(s_Us, min(n + 1, 8))
                vacant(pe, "X", n)
                for q in range(2):
                    j = 2 * n + q
                    for m in range(2):
                        for e in range(2):
                            last = mm(slot("X", n)[64 * e:64 * e + 64, 512 * q + 144 * m:512 * q + 144 * m + 144],
                                      PT5[:, m, j, 64 * e:64 * e + 64], U[:, 2 * j + e, :], skip_group_check=True)
                last.then_inc(full_sem("X", n), 1)

            def s5y(n):
                if n == 0:
                    pe.wait_ge(s_scan, 1)
                    pe.wait_ge(s_Td, 16 * CH)
                vacant(pe, "Y", n)
                for q in range(4):
                    g = 4 * n + q
                    j, e = divmod(g, 2)
                    p = slice(64 * e, 64 * e + 64)
                    o, o2 = 512 * e + 128 * (q // 2), 512 * e + 256 + 16 * (q // 2)
                    for out, c0, c1, k0, k1 in ((slot("Y", n)[:, o:o + 128], 0, NC, 0, CH),
                                                (slot("Y", n)[0:NB, o2:o2 + 16], NC + 1, NC + 1 + NB, 0, 1)):
                        Uc = U[:, g, 0:NC] if c0 == 0 else U[:, g, NC:NC + NB]
                        mm(out, Uc, T5[:, g, 16 * k0:16 * k1], True, False, skip_group_check=True)
                        mm(out, Hs[p, 0, j, c0:c1], CLr[p, j, k0 + 1:k1 + 1, :].rearrange("p s h -> p (s h)"),
                           False, False, skip_group_check=True)
                        last = mm(out, Hs[p, 1, j, c0:c1], CLn[p, j, k0 + 1:k1 + 1, :].rearrange("p s h -> p (s h)"),
                                  False, True, skip_group_check=True)
                last.then_inc(full_sem("Y", n), 1)

            def s5t(n):
                pe.wait_ge(s_th, 2 * (n // 2 + 1))
                vacant(pe, "yT", n)
                if n < 4:
                    for q in range(8):
                        s, k = 2 * n + q // 4, q % 4
                        last = pe.transpose(slot("yT", n)[:, 128 * q:128 * q + 128], usb[:, s, 128 * k:128 * k + 128],
                                            ident)
                else:
                    for k in range(4):
                        last = pe.transpose(slot("yT", n)[:, NB * k:NB * k + NB],
                                            dvu[:, QKW + 128 * k:QKW + 128 * k + 128], ident[0:NB, 0:NB])
                last.then_inc(full_sem("yT", n), 1)

            def glu(n):
                pe.wait_ge(s_yT, 5)
                pe.wait_ge(s_wl, 16)
                vacant(pe, "z", n)
                if n < 4:
                    for a in range(2):
                        for k in range(4):
                            last = mm(slot("z", n)[:, 512 * a:512 * a + 512], wglu[:, k, 128 * n:128 * n + 128],
                                      yT[:, k, 512 * a:512 * a + 512], k == 0, k == 3)
                else:
                    for m in range(4):
                        for k in range(4):
                            last = mm(slot("z", n)[:, NB * m:NB * m + NB], wglu[:, k, 128 * m:128 * m + 128],
                                      yT[:, k, SEQ:TT], k == 0, k == 3)
                last.then_inc(full_sem("z", n), 1)

            def out_(i):
                pe.wait_ge(s_wo, 16)
                pe.wait_ge(s_mix, NT)
                pe.wait_ge(s_mix2, 5)
                if i == NT:
                    pe.wait_ge(s_dmix, 1)
                vacant(pe, "o", i)
                r = 128 if i < NT else NB
                for a in range(2):
                    for k in range(KD):
                        last = mm(slot("o", i)[0:r, 512 * a:512 * a + 512], xm[:, k, 128 * i:128 * i + r],
                                  wout[:, k, 512 * a:512 * a + 512], k == 0, k == KD - 1)
                last.then_inc(full_sem("o", i), 1)

            def ht(i):
                r = 128 if i < NT else NB
                pe.wait_ge(s_h2, i + 1)
                vacant(pe, "hT", i)
                for k in range(KD):
                    last = pe.transpose(slot("hT", i)[:, 128 * k:128 * k + r], h2[0:r, i % 2, 128 * k:128 * k + 128],
                                        ident[0:r, 0:r])
                last.then_inc(full_sem("hT", i), 1)
                pe.wait_ge(s_h2T, i + 1)
                vacant(pe, "r", i)
                for k in range(KD):
                    last = mm(slot("r", i)[0:r, 0:36], h2T[:, i % 2, k, 0:r], wr[:, k, :], k == 0, k == KD - 1)
                last.then_inc(full_sem("r", i), 1)

            def route():
                pe.wait_ge(s_oh, 1)
                vacant(pe, "rank")
                rank = slot("rank")[:, 0:320]
                mm(rank, consts[:, C_UP:C_UP + 128], OHs.rearrange("p t e -> p (t e)"), True, False,
                   skip_group_check=True)
                for i in range(NT + 1):
                    n = NT + 1 - i
                    last = mm(rank[:, 32 * (i + 1):320], ones, OHs[:, i:i + 1, :].to_broadcast([128, n, NE]),
                              False, i == NT, skip_group_check=True)
                last.then_inc(full_sem("rank"), 1)
                pe.wait_ge(s_lst, 1)
                vacant(pe, "ids")
                for c in range(2):
                    for i in range(NT + 1):
                        last = mm(slot("ids")[:, 0:MAXT], R[c][:, i, :], TO[c][:, i, :], c + i == 0,
                                  c == 1 and i == NT)
                last.then_inc(full_sem("ids"), 1)

            later = {"s5pt": s5pt, "s5k": s5k, "s5u": s5u, "s5x": s5x, "s5y": s5y, "s5t": s5t, "glu": glu,
                     "out": out_, "ht": ht, "route": route}
            todo = {"stats": stats, "dqkv": dqkv, "dprep": dprep, "u": u, "qk": qk_, "v": v, "qt": qt, "s": s,
                    "av": av, "ot": ot, "K": K, "m1": m1, "m2": m2, "m3": m3, "V": Vv, "pt": pt, "ov": ov, "dout": dout,
                    **later}
            for unit in PLAN:
                if unit[0] in todo:
                    todo[unit[0]](*unit[1:])

            def turn(q, v, first=False):
                pe.wait_ge(m_hg[v % 2], 32 * q + 16 * (v // 2 + 1))
                if not (first and v == 0):
                    pe.wait_ge(m_hT, 4 * q + v)
                for k in range(KD):
                    last = pe.transpose(W[0][:, 128 * k:128 * k + 128], hg[v % 2][:, 128 * k:128 * k + 128], ident)
                last.then_inc(m_T, 1)

            def gate_up(q, v):
                pe.wait_ge(m_w[v % 4], 32 * q + 32 * (v // 4 + 1))
                pe.wait_ge(m_hT, 4 * q + (v + 1))
                for k in range(KD):
                    last = mm(W[2][:, 512 * (v % 2):512 * (v % 2) + 512], hgT[v % 2][:, k, :], Wgu[v % 4][:, k, :],
                              k == 0, k == KD - 1)
                last.then_inc(m_gu, 1)

            def turn_he(q, v):
                pe.wait_ge(m_he, 4 * q + (v + 1))
                for k in range(2):
                    last = pe.transpose((SC, OD)[v % 2][:, 128 * k:128 * k + 128], he[v % 2][:, 128 * k:128 * k + 128],
                                        ident)
                last.then_inc(m_heT, 1)

            def down(q, v, first=False):
                pe.wait_ge(m_heS, 4 * q + (v + 1))
                if not (first and v == 0):
                    pe.wait_ge(m_ys, 4 * q + v)
                for a in range(2):
                    for k in range(2):
                        last = mm(W[1][:, 512 * a:512 * a + 512], heT_[v % 2][:, 128 * k:128 * k + 128],
                                  Wdn[v % 4][:, k, 512 * a:512 * a + 512], k == 0, k == 1)
                last.then_inc(m_y, 1)

            def step(q, v, first=False, last=False):
                turn_he(q, v)
                if not (last and v == 3):
                    gate_up(q, v + 1)
                if not (last and v >= 2):
                    turn(q, v + 2)
                down(q, v, first)

            pe.wait_ge(s_route, 1)
            n3 = pe.value_load(plan_t[0:1, MAXT + 1:MAXT + 2], min_val=NE // 4 - 1, max_val=MAXT // 4 - 1)
            turn(0, 0, first=True)
            gate_up(0, 0)
            turn(0, 1)
            for v in range(4):
                step(0, v, first=True)
            with pe.Fori(1, n3) as q:
                for v in range(4):
                    step(q, v)
            for v in range(4):
                step(n3, v, last=True)


def constants():
    c = np.zeros((128, C_END), np.float32)
    p = np.arange(128)
    c[:, C_ID:C_ID + 128] = np.eye(128)
    c[:, C_ONE:C_ONE + 128] = 1.0
    c[:, C_UP:C_UP + 128] = p[:, None] < p[None, :]
    c[:, C_MASK:C_MASK + 128] = np.where(p[None, :] <= p[:, None], 0.0, NEG)
    c[:, C_SUM:C_SUM + 128] = p[:, None] % 32 == p[None, :] % 32
    c[:, C_NEG:C_NEG + 64] = np.where(np.eye(8) > 0, 0.0, NEG).reshape(1, 64)
    for h in range(H):
        c[p % 32 == 2 * h, C_M0 + h] = 1.0
        c[p % 32 == 2 * h + 1, C_M1 + h] = 1.0
    c[:, C_I8:C_I8 + 8] = np.arange(8)
    c[:, C_I32:C_I32 + 32] = np.arange(32)
    c[:, C_THR:C_THR + 9] = 128.0 * np.arange(9)
    c[:, C_VAL:C_VAL + 9] = (p[:, None] + 128 * np.arange(9)) < TT
    c[:, C_TOK:C_TOK + 9] = (p[:, None] + 128 * np.arange(9)) * c[:, C_VAL:C_VAL + 9]
    c[:, C_TI:C_TI + 128] = np.arange(128)
    c[:, C_NH] = -0.5
    inv = np.float32(500000.0) ** (-np.arange(0, 16, 2, dtype=np.float32) / np.float32(16))
    pos = np.zeros((NT + 1, 128), np.float32)
    pos[:NT] = np.arange(SEQ).reshape(NT, 128)
    pos[NT] = NPAGE * PG
    ang = (pos[..., None] * inv).astype(np.float32)
    rope = np.concatenate([np.cos(ang), np.sin(ang)], -1).astype(np.float32).transpose(1, 0, 2)
    return c, np.ascontiguousarray(rope)


def pairs(a):
    return a.reshape(NP5, 2, P5, *a.shape[2:]).transpose(1, 2, 0, *range(3, a.ndim + 1)).reshape(128, NP5, *a.shape[2:])


def layout(x):
    xp, xs = x["x_prompt"][0], x["x_sample"][:, 0]
    xall = np.concatenate([xp, xs], 0)
    w_in = x["w_in"][0].reshape(KD, 128, PROJ)
    colw = np.zeros((128, 3 * KD), np.float32)
    colw[:, 0:KD] = x["ln1_g"][0].reshape(KD, 128).T
    colw[:, KD:2 * KD] = x["ln2_g"][0].reshape(KD, 128).T
    colw[:, 2 * KD] = x["subln_g"][0]
    lam = np.stack([x[f"lambda_{n}"][0] for n in ("q1", "k1", "q2", "k2")])
    consts, rope = constants()
    return {
        "consts": consts, "rope": rope, "colw": colw, "lamv": lam,
        "s5_par": np.stack([pairs(x["s5_a_re"][0]), pairs(x["s5_a_im"][0]),
                            pairs(np.repeat(x["s5_log_dt"][0][:, None], P5, 1))], 1),
        "s5_bc": np.stack([np.stack([pairs(x["s5_b_re"][0]), pairs(x["s5_b_im"][0])], 1),
                           np.stack([pairs(x["s5_c_re"][0].transpose(0, 2, 1)),
                                     pairs(x["s5_c_im"][0].transpose(0, 2, 1))], 1)], 1),
        "s5_h0": np.stack([pairs(x[f"state_s5_{n}"][0].transpose(1, 2, 0)) for n in ("re", "im")]),
        "dskip": x["s5_d"][0], "w_glu": x["w_glu"][0].reshape(4, 128, QKW).transpose(1, 0, 2),
        "b_glu": x["b_glu"][0].reshape(4, 128).T, "w_out": x["w_out"][0].reshape(KD, 128, D).transpose(1, 0, 2),
        "w_r": np.concatenate([x["w_router_group"][0],
                               x["w_router_expert"][0].transpose(1, 0, 2).reshape(D, NE)], 1)
        .reshape(KD, 128, 36).transpose(1, 0, 2),
        "b_r": np.concatenate([x["b_router_group"][0], x["b_router_expert"][0].reshape(NE)]),
        "w_gu": np.concatenate([x["w_gate"][0], x["w_up"][0]], 2).reshape(NE, KD, 128, 2 * DE).transpose(0, 2, 1, 3),
        "w_dn": x["w_down"][0].reshape(NE, 2, 128, D).transpose(0, 2, 1, 3), "ln_f_g": x["ln_f_g"],
        "x_p": x["x_prompt"].reshape(NT, 128, D), "x_s": x["x_sample"].reshape(NB, D),
        "page_table": x["page_table"].reshape(1, NB * NPAGE).astype(np.int32),
        "xT": xall.T.reshape(KD, 128, TT), "w_qkv": w_in[:, :, :3 * QKW], "w_u": w_in[:, :, 3 * QKW:],
        "cacheK": x["cache_k"][0].reshape(POOL, PG, H, 2, HD).transpose(0, 3, 4, 2, 1).reshape(POOL, 128, H * PG),
        "cacheV": x["cache_v"][0].reshape(POOL, PG, H * VD),
    }


SCRATCH = {"u_scratch": (128, CH, QKW), "h2_scratch": (TT, D), "y_scratch": (SLOTS, D)}
OUTS = {
    "y_p": (NT, 128, D), "y_s": (NB, D), "k_p": (NT, 128, QKW), "v_p": (NT, 128, QKW),
    "h_p": (2, 128, NP5), "k_s": (NB, QKW), "v_s": (NB, QKW), "h_s": (2, 128, NP5, NB),
}


def kernel(**inputs):
    from concourse import bacc
    from concourse.bass_utils import run_bass_kernel_spmd

    nc = bacc.Bacc("TRN2", target_bir_lowering=False, num_devices=1)
    arrays = {f"in_{k}": np.ascontiguousarray(v) for k, v in layout({k: np.asarray(v) for k, v in inputs.items()}).items()}
    io = {k[3:]: nc.dram_tensor(k, v.shape, mybir.dt.from_np(v.dtype), kind="ExternalInput").ap()
          for k, v in arrays.items()}
    for k, shape in OUTS.items():
        io[k] = nc.dram_tensor(f"out_{k}", shape, mybir.dt.float32, kind="ExternalOutput").ap()
    for k, shape in SCRATCH.items():
        io[k] = nc.dram_tensor(k, shape, mybir.dt.float32, kind="Internal").ap()
    hymba_step(nc, io)
    r = run_bass_kernel_spmd(nc, [arrays], core_ids=[0]).results[0]
    o = {k: np.asarray(r[f"out_{k}"]) for k in OUTS}

    def states(a):
        a = a.reshape(2, 2, P5, NP5, -1).transpose(0, 4, 3, 1, 2)
        return a.reshape(2, 1, -1, G5, P5)

    hp, hs = states(o["h_p"]), states(o["h_s"])
    return (o["y_p"].reshape(1, SEQ, D), o["y_s"].reshape(NB, 1, D),
            o["k_p"].reshape(1, 1, SEQ, 2 * H, HD), o["v_p"].reshape(1, 1, SEQ, H, VD), hp[0], hp[1],
            o["k_s"].reshape(1, NB, 1, 2 * H, HD), o["v_s"].reshape(1, NB, 1, H, VD), hs[0], hs[1])
```

```python
import numpy as np
import concourse.bass as bass
from concourse import mybir
from contextlib import ExitStack

SEQ, NB, D = 1024, 8, 1024
TT = SEQ + NB
KD = D // 128
NT = SEQ // 128
H, HD, VD = 4, 64, 128
QKW = 2 * H * HD
PROJ = 4 * QKW
NPAGE, PG = 64, 128
POOL = NB * NPAGE * 5 // 4
RING = 16
GRP = 8
TURNS = NPAGE // RING
NROT = 8
G5, W5, P5 = 32, 16, 64
NP5 = G5 // 2
CH = 8
NC = SEQ // CH
NE, EG, NG = 32, 8, 4
DE = D // 4
MAXT = 48
SLOTS = MAXT * 128
EPS = 1e-5
SETUP, SCAN, GELU, LOAD = 31.35, 13, 15.04, 9.32
NEG = -1e30
LINIT = 0.8 - 0.6
MAGIC = 12582912.0
GELU_C = float(np.sqrt(2.0 / np.pi))

C_ID, C_ONE, C_UP, C_MASK = 0, 128, 256, 384
C_SUM = 512
C_NEG = 640
C_M0, C_M1 = 704, 708
C_I8, C_I32, C_THR, C_TOK, C_VAL, C_TI = 712, 720, 752, 761, 770, 779
C_NH = C_TI + 128
C_END = C_NH + 1



def make_plan():
    dec = []
    for b in range(NB):
        dec += [(.5, ("K", b, t, g)) for t in range(TURNS) for g in range(2)]
        dec += [(0.36, ("m1", b)), (0.11, ("m2", b)), (0.25, ("m3", b)), (0.26, ("pt", b))]
        dec += [(.5, ("V", b, t, g)) for t in range(TURNS) for g in range(2)] + [(.1, ("ov", b))]
    pro = [(9.85, ("u", s)) for s in range(NT)]
    pend = None
    for i in range(NT):
        pro += [(7.5, ("qk", i, 0)), (7.5, ("qk", i, 1)), (7.5, ("v", i))]
        if pend is not None:
            pro += [(2 + .5 * i, ("av",) + pend), (.6, ("ot", i - 1))]
            pend = None
        pro += [(1.5, ("qt", i))]
        for h in range(H):
            pro += [(2 + .6 * (i + 1), ("s", i, h))]
            if pend is not None:
                pro += [(1 + .5 * (i + 1), ("av",) + pend)]
            pend = (i, h)
    pro += [(4, ("av",) + pend), (.6, ("ot", NT - 1))]
    pro += [(SETUP, ("s5a",)), (5, ("s5pt",))] + [(.5, ("s5u", n)) for n in range(8)]
    pro += [(28, ("s5k",))] + [(1.4, ("s5x", n)) for n in range(8)] + [(SCAN, ("s5h", n)) for n in range(4)]
    pro += [(3, ("s5y", n)) for n in range(8)] + [(GELU, ("s5g", n)) for n in range(3)]
    pro += [(.7, ("s5t", n)) for n in range(5)] + [(7, ("glu", n)) for n in range(4)] + [(5, ("glu", 4))]
    pro += [(LOAD, ("x1",))]
    for i in range(NT):
        pro += [(8.2, ("out", i, 0)), (8.2, ("out", i, 1))] + ([(4, ("ht", i - 1))] if i else [])
    total, wsum = sum(c for c, _ in pro), sum(w for w, _ in dec)
    plan, t, n, due = [("stats",), ("dqkv",), ("dprep",)], 0.0, 0, 0.0
    for c, x in pro:
        plan.append(x)
        t += c
        while n < len(dec) and t * wsum > due * total and not (
                x[0] in ("qk", "out") and x[2] == 0 and dec[n][1][0] == "pt"):
            plan.append(dec[n][1])
            due += dec[n][0]
            n += 1
    plan += [x for _, x in dec[n:]]
    plan += [("ht", NT - 1), ("choose", 0, NT), ("dout",), ("out", NT, 0), ("ht", NT), ("choose", NT, NT + 1), ("route",)]
    return plan


def psum_keys(unit):
    k, a = unit[0], unit[1:]
    return {
        "stats": [("ss",)], "dqkv": [("dp",)], "dprep": [("dqt",)],
        "pt": [("PT",) + a + (0,), ("PT",) + a + (1,), ("PTn",) + a],
        "u": [("u",) + a], "qk": [("qk",) + a[:1]] if a[1:] == (0,) else [], "v": [("v",) + a], "qt": [("qkT",) + a],
        "s": [("S",) + a + (0,), ("S",) + a + (1,)], "av": [("AT",) + a, ("O",) + a],
        "ot": [("oT",) + a], "dout": [("dss",)],
        "s5pt": [("pt", n) for n in range(4)], "s5k": [("k", n) for n in range(4)],
        "s5u": [("U",) + a], "s5x": [("X",) + a], "s5y": [("Y",) + a],
        "s5t": [("yT",) + a], "glu": [("z",) + a],
        "route": [("rank",), ("ids",)],
        "out": [("o",) + a[:1]] if a[1:] == (0,) else [], "ht": [("hT",) + a, ("r",) + a],
    }.get(k, [])


def hymba_step(nc, io):
    f32, i32, u32 = mybir.dt.float32, mybir.dt.int32, mybir.dt.uint32
    ALU, ACT, AX = mybir.AluOpType, mybir.ActivationFunctionType, mybir.AxisListType.X
    MUL, ADD, SUB, MAX, MIN = ALU.mult, ALU.add, ALU.subtract, ALU.max, ALU.min

    PLAN = make_plan()
    USE = {}
    for unit in PLAN:
        for key in psum_keys(unit):
            USE[key] = len(USE)
    POW = {}
    for unit in PLAN:
        if unit[0] in ("stats", "dout", "ht") or (unit[0] == "av" and unit[2] == H - 1):
            POW[unit] = len(POW)

    ctx = ExitStack()
    with ctx:
        def sb(name, shape, dt=f32):
            return ctx.enter_context(nc.sbuf_tensor(name, shape, dt))

        def sem(name):
            return ctx.enter_context(nc.semaphore(name))

        consts = sb("consts", [128, C_END])
        ident, ones = consts[:, C_ID:C_ID + 128], consts[:, C_ONE:C_ONE + 128]
        causal = consts[:, C_MASK:C_MASK + 128]
        rope = sb("rope", [128, NT + 1, 2 * NROT])
        ptab = sb("ptab", [1, NB * NPAGE], i32)
        colw = sb("colw", [128, 3 * KD])
        lamt = sb("lamt", [128, 8])
        rstd = sb("rstd", [128, 2 * NT + 1])
        xm = sb("xm", [128, KD, TT])
        ring = sb("ring", [128, RING, 512])
        dvu = sb("dvu", [NB, 2 * QKW])
        qpad = sb("qpad", [128, H, NB, 32])
        knT = sb("knT", [128, H, NB])
        sall = sb("sall", [128, TURNS, 512])
        snew = sb("snew", [128, NB])
        ptn = sb("ptn", [NB, 128])
        mrow = sb("mrow", [128, 8])
        mrep = sb("mrep", [1, 4, 32])
        wmap = sb("wmap", [128, 2, H])
        o4s = sb("o4s", [128, 512])
        aD = sb("aD", [128, H, NB])
        aD2 = sb("aD2", [128, H, NB])
        rt = sb("rt", [128, 16, NROT, 4])
        st = sb("st", [128, 32])
        arena = sb("arena", [128, 28112])
        rtf = rt[:, :, :, :].rearrange("p a b c -> p (a b c)")

        def region(base, size, pat=None, /, **kw):
            v = arena[:, base:base + size]
            return v if pat is None else v.rearrange(pat, **kw)

        w_qkv = region(0, KD * 3 * QKW, "p (k n) -> p k n", k=KD)
        w_u = region(12288, KD * QKW, "p (k n) -> p k n", k=KD)
        P = region(12288, 4096, "p (s c n) -> p s c n", s=2, c=2)
        kT = region(16384, H * SEQ, "p (h n) -> p h n", h=H)
        sq = region(16384, 2 * TT, "p (s n) -> p s n", s=2)
        V = region(20480, NT * QKW, "p (t n) -> p t n", t=NT)
        qk = region(24576, 1024)
        qT = region(25600, H * 128, "p (h n) -> p h n", h=H)
        att = region(26112, QKW)
        sumrow = region(24576, TT)[0:1]
        lamv = region(26112, 4 * HD, "p (a d) -> p a d", a=4)

        CLr = region(0, 2304, "p (j k h) -> p j k h", j=NP5, k=CH + 1)
        CLn = region(2304, 2304, "p (j k h) -> p j k h", j=NP5, k=CH + 1)
        PT5 = region(4608, 4096, "p (m j q) -> p m j q", m=2, j=NP5)
        PB = region(8704, 4096, "p (m j s h) -> p m j s h", m=2, j=NP5, s=CH)
        U = region(8704, 4608, "p (g c) -> p g c", g=G5)
        Hs = region(13312, 4640, "p (m j c) -> p m j c", m=2, j=NP5)
        Ksb = region(17952, 4096, "p (g q) -> p g q", g=G5)
        Z = region(17952, 4096, "p (g s h) -> p g s h", g=G5, s=CH)[0:2 * NB]
        Bt = region(13312, 4096, "p (m j s h) -> p m j s h", m=2, j=NP5, s=CH)
        yT = region(17952, 4 * TT, "p (k n) -> p k n", k=4)
        usb = region(22080, 4096, "p (s n) -> p s n", s=CH)
        par = region(26176, 48, "p (a j) -> p a j", a=3)
        bc = region(26224, 1024, "p (a m j h) -> p a m j h", a=2, m=2, j=NP5)
        Lp = region(27248, 288, "p (m k j) -> p m k j", m=2, k=CH + 1)
        LpR = region(27536, 256, "p (m j s) -> p m j s", m=2, j=NP5)
        sm5 = region(27792, 320, "p (a j) -> p a j", a=20)
        hs8 = rtf[:, 0:256].rearrange("p (m j b) -> p m j b", m=2, j=NP5)
        hp = rtf[:, 256:288].rearrange("p (m j) -> p m j", m=2)
        T5 = xm[:, 4:8, :].rearrange("p k n -> p (k n)")[:, 0:4096].rearrange("p (g q) -> p g q", g=G5)
        ug = T5.rearrange("p g (s h) -> p g s h", s=CH)
        tmp5 = region(4608, 4096)
        tmp5b = region(17952, 4096)
        wglu = region(0, 2048, "p (k n) -> p k n", k=4)
        x1 = region(0, (NT + 1) * D, "p (t n) -> p t n", t=NT + 1)
        wout = region(9216, KD * D, "p (k n) -> p k n", k=KD)
        h2 = region(17408, 2048, "p (s n) -> p s n", s=2)
        h2T = region(19456, 2048, "p (s k n) -> p s k n", s=2, k=KD)
        wr = sb("wr", [128, KD, 36])
        br = sb("br", [128, 36])
        logit = sb("logit", [128, NT + 1, 36])
        bglu = sb("bglu", [128, 4])
        dskip = sb("dskip", [128, QKW])
        ids = sb("ids", [128, MAXT], u32)
        idc = sb("idc", [128, 2], u32)
        rows = sb("rows", [128, 2, NT + 1], u32)
        wts = sb("wts", [128, 2, NT + 1])
        plan_t = sb("plan_t", [1, MAXT + 2], i32)
        R = [region(b, 9 * 128, "p (t n) -> p t n", t=9) for b in (21504, 22656)]
        TO = [region(b, 9 * MAXT, "p (t n) -> p t n", t=9) for b in (23808, 24240)]
        OH = [region(24672 + 288 * c, 288, "p (t e) -> p t e", t=9) for c in range(2)]
        OHs = region(25248, 320, "p (t e) -> p t e", t=10)
        xmf, ringf = xm[:, :, :].rearrange("p k n -> p (k n)"), ring[:, :, :].rearrange("p a n -> p (a n)")
        WX = [region(9216, 6144), xmf[:, 0:6144], ringf[:, 0:6144], region(21504, 6144)]
        Wgu = [w[:, 0:4096].rearrange("p (k n) -> p k n", k=KD) for w in WX]
        Wdn = [w[:, 4096:6144].rearrange("p (k n) -> p k n", k=2) for w in WX]
        hg = [ringf[:, 6144 + 1024 * s:7168 + 1024 * s] for s in range(2)]
        hgT = [xmf[:, 6144 + 1024 * s:7168 + 1024 * s].rearrange("p (k n) -> p k n", k=KD) for s in range(2)]
        yb = [region(15360 + 1024 * s, 1024) for s in range(2)]
        tg, he, heT_ = ([region(17408 + 512 * a + 256 * s, 256) for s in range(2)] for a in range(3))
        lnf = region(19456, D)
        yg = [[w[:, 2048 * s + 1024 * c:2048 * s + 1024 * c + 1024] for c in range(2)]
              for w in (WX[0], WX[3], WX[1]) for s in range(3)]

        SC = ctx.enter_context(nc.psum_tensor("SC", [128, 512], f32))
        OD = ctx.enter_context(nc.psum_tensor("OD", [128, 512], f32))
        nkP, mxT, mbP, lP, aP = OD[0:32, 0:NB], OD[0:1, 128:256], OD[:, 256:257], OD[:, 257:258], OD[:, 260:264]
        W = [ctx.enter_context(nc.psum_tensor(f"W{i}", [128, 1024], f32)) for i in range(3)]

        ps_full = [sem(f"ps_full{i}") for i in range(3)]
        ps_free = [sem(f"ps_free{i}") for i in range(3)]
        s_cst, s_lamv, s_lam = sem("s_cst"), sem("s_lamv"), sem("s_lam")
        s_wk = [sem(f"s_wk{k}") for k in range(KD)]
        s_xk = [sem(f"s_xk{k}") for k in range(KD)]
        s_pg = [sem(f"s_pg{k}") for k in range(RING // GRP)]
        s_pgfree = sem("s_pgfree")
        s_tab = sem("s_tab")
        s_sq, s_sqread, s_xg, s_rstd = sem("s_sq"), sem("s_sqread"), sem("s_xg"), sem("s_rstd")
        s_dq, s_drope, s_dst, s_qbd = sem("s_dq"), sem("s_drope"), sem("s_dst"), sem("s_qbd")
        s_u = sem("s_u")
        s_qk, s_v, s_rope, s_kst, s_qkT = sem("s_qk"), sem("s_v"), sem("s_rope"), sem("s_kst"), sem("s_qkT")
        s_vst = sem("s_vst")
        s_mx, s_exp, s_comb, s_ATs, s_att = sem("s_mx"), sem("s_exp"), sem("s_comb"), sem("s_ATs"), sem("s_att")
        s_ms, s_rs = sem("s_ms"), sem("s_rs")
        s_mix = sem("s_mix")
        s_score, s_evac, s_nk, s_m1, s_mT, s_mrep, s_mb, s_nb, s_pexp = (sem(x) for x in (
            "s_score", "s_evac", "s_nk", "s_m1", "s_mT", "s_mrep", "s_mb", "s_nb", "s_pexp"))
        s_l, s_lP, s_ptw, s_pv, s_o4, s_aP, s_ad, s_ad2, s_dmix = (sem(x) for x in (
            "s_l", "s_lP", "s_ptw", "s_pv", "s_o4", "s_aP", "s_ad", "s_ad2", "s_dmix"))
        s_ust = [sem(f"s_ust{n}") for n in range(2)]
        s_dve5, s_act5, s_ld5, s_u5, s_Td, s_Tz, s_h0 = (sem(x) for x in (
            "s_dve5", "s_act5", "s_ld5", "s_u5", "s_Td", "s_Tz", "s_h0"))
        s_z, s_pt5, s_ks, s_Us, s_Xs, s_scan = (sem(x) for x in (
            "s_z", "s_pt5", "s_ks", "s_Us", "s_Xs", "s_scan"))
        s_du, s_th, s_g5, s_yT, s_zt, s_mix2, s_wl, s_wo, s_x1 = (sem(x) for x in (
            "s_du", "s_th", "s_g5", "s_yT", "s_zt", "s_mix2", "s_wl", "s_wo", "s_x1"))
        s_xo, s_sq2, s_h2, s_h2T = (sem(x) for x in (
            "s_xo", "s_sq2", "s_h2", "s_h2T"))
        s_hst = [sem(f"s_hst{n}") for n in range(2)]
        s_fx, s_ug = sem("s_fx"), sem("s_ug")
        s_rexp, s_rex2, s_oh, s_lst, s_route = (sem(x) for x in ("s_rexp", "s_rex2", "s_oh", "s_lst", "s_route"))
        m_w = [sem(f"m_w{n}") for n in range(4)]
        m_hg = [sem(f"m_hg{n}") for n in range(2)]
        m_st = [sem(f"m_st{n}") for n in range(2)]
        m_T, m_hT, m_gu, m_th, m_he, m_heT, m_heS, m_y, m_ys = (sem(x) for x in (
            "m_T", "m_hT", "m_gu", "m_th", "m_he", "m_heT", "m_heS", "m_y", "m_ys"))
        s_stored = sem("s_stored")
        s_row, s_col = sem("s_row"), sem("s_col")
        s_zero, s_zst = sem("s_zero"), sem("s_zst")
        f_g = [sem(f"f_g{n}") for n in range(NT + 1)]
        f_gf, f_x, f_sq, f_ms, f_rs, f_out, f_st, f_sc = (sem(x) for x in (
            "f_gf", "f_x", "f_sq", "f_ms", "f_rs", "f_out", "f_st", "f_sc"))

        def slot(*key):
            return W[USE[key] % 3]

        def filled(*key):
            return ps_full[USE[key] % 3], USE[key] // 3 + 1

        def full_sem(*key):
            return ps_full[USE[key] % 3]

        def free_sem(*key):
            return ps_free[USE[key] % 3]

        def vacant(eng, *key):
            if USE[key] >= 3:
                eng.wait_ge(ps_free[USE[key] % 3], USE[key] // 3)

        block = ctx.enter_context(nc.Block())

        @block.sync
        def _(sp):
            sp.dma_start(ptab[:, :], io["page_table"]).then_inc(s_tab, 16)
            for k in range(KD):
                sp.dma_start(xm[:, k, :], io["xT"][k, :, :]).then_inc(s_xk[k], 16)
                sp.dma_start(w_qkv[:, k, :], io["w_qkv"][k, :, :]).then_inc(s_wk[k], 16)
                sp.dma_start(w_u[:, k, :], io["w_u"][k, :, :]).then_inc(s_wk[k], 16)
            sp.wait_ge(s_tab, 16)
            with sp.Fori(0, NB) as b:
                for kind, cache in enumerate((io["cacheK"], io["cacheV"])):
                    with sp.Fori(0, NPAGE // RING) as r:
                        for g in range(RING // GRP):
                            pages = [sp.value_load(ptab[0:1, bass.ds(b * NPAGE + r * RING + GRP * g + j, 1)],
                                                   min_val=0, max_val=POOL - 1) for j in range(GRP)]
                            sp.wait_ge(s_pgfree, b * (2 * NPAGE // GRP) + r * 2 + (kind * (NPAGE // GRP) + g + 1))
                            for j, page in enumerate(pages):
                                sp.dma_start(ring[:, GRP * g + j, :], cache[bass.ds(page, 1), :, :]
                                             .rearrange("a p n -> p (a n)")).then_inc(s_pg[g], 16)

            def weights(e, v):
                sp.dma_start(Wgu[v], io["w_gu"][e, :, :, :].rearrange("a p k n -> p (a k) n")).then_inc(m_w[v], 16)
                sp.dma_start(Wdn[v], io["w_dn"][e, :, :, :].rearrange("a p k n -> p (a k) n")).then_inc(m_w[v], 16)

            sp.wait_ge(*filled("o", NT))
            weights(slice(0, 1), 0)
            weights(slice(1, 2), 1)
            sp.wait_ge(s_pgfree, RING // GRP + NB * 2 * NPAGE // GRP)
            weights(slice(2, 3), 2)
            sp.wait_ge(s_route, 1)
            weights(slice(3, 4), 3)
            n4 = sp.value_load(plan_t[0:1, MAXT:MAXT + 1], min_val=NE // 4, max_val=MAXT // 4)
            with sp.Fori(1, n4) as q:
                for v in range(4):
                    e = sp.value_load(plan_t[0:1, bass.ds(4 * q + v, 1)], min_val=0, max_val=NE - 1)
                    sp.wait_ge(m_y, 4 * q + (v - 3))
                    weights(bass.ds(e, 1), v)
            for i in range(NT + 1):
                sp.wait_ge(f_out, i + 1)
                if i < NT:
                    sp.dma_start(io["y_p"][i, :, :], x1[:, i, :]).then_inc(f_st, 16)
                else:
                    sp.dma_start(io["y_s"], x1[0:NB, NT, :]).then_inc(f_st, 16)
            sp.wait_ge(f_st, 16 * (NT + 1))

        @block.gpsimd
        def _(gp):
            gp.dma_start(consts[:, :], io["consts"]).then_inc(s_cst, 16)
            gp.dma_start(colw[:, :], io["colw"]).then_inc(s_cst, 16)
            gp.dma_start(rope[:, :, :], io["rope"]).then_inc(s_cst, 16)
            gp.dma_start(dskip[:, :], io["dskip"].partition_broadcast(128)).then_inc(s_cst, 16)
            gp.dma_start(br[:, :], io["b_r"].partition_broadcast(128)).then_inc(s_cst, 16)
            gp.dma_start(wr[:, :, :], io["w_r"]).then_inc(s_cst, 16)
            gp.dma_start(bglu[:, :], io["b_glu"]).then_inc(s_cst, 16)
            gp.dma_start(lamv[:, :, :], io["lamv"].partition_broadcast(128)).then_inc(s_lamv, 16)

            def stats():
                gp.memset(qpad[:, :, :, :], 0.0).then_inc(s_qbd, 1)
                gp.wait_ge(s_cst, 112)

                gp.memset(sall[:, 0:2, :], 0.0).then_inc(s_zero, 1)
                root(rstd[:, :], ("stats",))
                gp.wait_ge(s_zero, 1)
                for t in range(NE, MAXT):
                    gp.dma_start(io["y_scratch"][128 * t:128 * t + 128, :],
                                 sall[:, 0:2, :].rearrange("p t n -> p (t n)")).then_inc(s_zst, 16)

            def root(x, key):
                gp.wait_ge(s_ms, POW[key] + 1)
                gp.tensor_tensor(x, x, consts[:, C_NH:C_NH + 1].to_broadcast(list(x.shape)), ALU.pow).then_inc(s_rs, 1)

            def av(i, h):
                if h == H - 1:
                    root(st[:, 24:28], ("av", i, h))

            def dout():
                root(aD2[:, :, :].rearrange("p h b -> p (h b)"), ("dout",))

            def dqkv():
                gp.wait_ge(s_drope, 1)
                gp.dma_start(io["v_s"], dvu[:, 0:QKW]).then_inc(s_dst, 16)
                gp.wait_ge(s_drope, 1)
                gp.dma_start(io["k_s"], qk[0:NB, QKW:2 * QKW]).then_inc(s_dst, 16)

            def u(s):
                gp.wait_ge(s_u, s + 1)
                gp.dma_start(io["u_scratch"][:, s, :], qk[:, QKW * (s % 2):QKW * (s % 2) + QKW]).then_inc(s_ust[s % 2], 16)

            def qt(i):
                gp.wait_ge(s_rope, i + 1)
                gp.dma_start(io["k_p"][i, :, :], qk[:, QKW:2 * QKW]).then_inc(s_kst, 16)
                gp.wait_ge(s_v, i + 1)
                gp.dma_start(io["v_p"][i, :, :], V[:, i, :]).then_inc(s_vst, 16)

            def s5a():
                gp.wait_ge(*filled("oT", NT - 1))
                gp.wait_ge(s_kst, 16 * NT)
                gp.wait_ge(s_vst, 16 * NT)
                for n in range(2):
                    gp.wait_ge(s_ust[n], 16 * (CH // 2))
                gp.dma_start(par, io["s5_par"]).then_inc(s_ld5, 16)
                gp.dma_start(bc, io["s5_bc"]).then_inc(s_ld5, 16)
                gp.dma_start(usb, io["u_scratch"]).then_inc(s_u5, 16)
                gp.memset(Z, 0.0).then_inc(s_z, 1)
                gp.wait_ge(s_z, 1)
                for a, s in ((0, 0), (1, CH - 1)):
                    gp.dma_start(Z[NB * a:NB * a + NB, :, s, :],
                                 dvu[:, QKW:2 * QKW].rearrange("p (g h) -> p g h", g=G5)).then_inc(s_u5, 16)

            def s5k():
                gp.wait_ge(*filled("U", 7))
                gp.memset(T5, 0.0).then_inc(s_Tz, 1)
                gp.wait_ge(*filled("k", 3))
                gp.memset(Hs[:, :, :, 0:1], 0.0).then_inc(s_Tz, 1)
                gp.wait_ge(s_ks, 4)
                gp.wait_ge(s_Tz, 2)
                for s in range(CH):
                    gp.dma_start(T5[16 * s:16 * s + 16, :, 16 * s:128], Ksb[16 * s:16 * s + 16, :, 0:128 - 16 * s])\
                        .then_inc(s_Td, 16)

            def s5x(n):
                if n == 7:
                    gp.wait_ge(s_Us, 8)
                    gp.wait_ge(s_cst, 112)
                    gp.tensor_tensor(usb, usb, dskip[:, :].unsqueeze(1).to_broadcast([128, CH, QKW]), MUL)
                    gp.tensor_tensor(dvu[:, QKW:2 * QKW], dvu[:, QKW:2 * QKW], dskip[0:NB, :], MUL)
                    gp.drain().then_inc(s_du, 1)
                    gp.wait_ge(s_Xs, 8)
                    for m in range(2):
                        gp.dma_start(Hs[:, m, :, NC + 1:NC + 1 + NB], io["s5_h0"][m, :, :, :]).then_inc(s_h0, 16)

            def s5h(n):
                if n < 3:
                    return
                gp.wait_ge(s_scan, 1)
                gp.dma_start(io["h_p"].rearrange("m p j -> p m j"), hp).then_inc(s_fx, 16)
                gp.dma_start(io["h_s"].rearrange("m p j b -> p m j b"), hs8).then_inc(s_fx, 16)

            def s5y(n):
                if n == 7:
                    gp.wait_ge(*filled("Y", 7))
                    gp.dma_start(wglu, io["w_glu"]).then_inc(s_wl, 16)
                    gp.dma_start(wout, io["w_out"]).then_inc(s_wo, 16)

            def x1_():
                gp.wait_ge(*filled("z", 4))
                gp.wait_ge(s_mix2, 5)
                for i in range(NT):
                    gp.dma_start(x1[:, i, :], io["x_p"][i, :, :]).then_inc(s_x1, 16)
                gp.dma_start(x1[0:NB, NT, :], io["x_s"]).then_inc(s_x1, 16)

            def ht(i):
                root(st[:, 28 + i % 2:29 + i % 2], ("ht", i))
                r = 128 if i < NT else NB
                gp.wait_ge(s_h2, i + 1)
                gp.dma_start(io["h2_scratch"][128 * i:128 * i + r, :], h2[0:r, i % 2, :]).then_inc(s_hst[i % 2], 16)

            later = {"s5a": s5a, "s5k": s5k, "s5x": s5x, "s5h": s5h, "s5y": s5y, "x1": x1_, "ht": ht}
            todo = {"stats": stats, "dqkv": dqkv, "qt": qt, "av": av, "dout": dout, "u": u, **later}
            for unit in PLAN:
                if unit[0] in todo:
                    todo[unit[0]](*unit[1:])

            def gather(q, v):
                gp.tensor_copy(idc[:, v % 2:v % 2 + 1], ids[:, bass.ds(4 * q + v, 1)])
                gp.drain()
                gp.indirect_dma_start(hg[v % 2], None, io["h2_scratch"],
                                      bass.IndirectOffsetOnAxis(ap=idc[:, v % 2:v % 2 + 1], axis=0))\
                    .then_inc(m_hg[v % 2], 16)

            gp.wait_ge(s_route, 1)
            gp.wait_ge(s_pgfree, RING // GRP + NB * 2 * NPAGE // GRP)
            for n in range(2):
                gp.wait_ge(s_hst[n], 16 * ((NT + 2 - n) // 2))
            gp.dma_start(lnf, io["ln_f_g"].partition_broadcast(128)).then_inc(f_gf, 16)
            for v in range(4):
                if v >= 2:
                    gp.wait_ge(m_T, v - 1)
                gather(0, v)
            n4 = gp.value_load(plan_t[0:1, MAXT:MAXT + 1], min_val=NE // 4, max_val=MAXT // 4)
            with gp.Fori(1, n4) as q:
                for v in range(4):
                    gp.wait_ge(m_T, 4 * q + (v - 1))
                    gather(q, v)

            def gather2(i):
                for c in range(2):
                    r = 128 if i < NT else NB
                    gp.indirect_dma_start(yg[i][c][0:r, :], None, io["y_scratch"],
                                          bass.IndirectOffsetOnAxis(ap=rows[0:r, c, i:i + 1], axis=0))\
                        .then_inc(f_g[i], 16)

            def gain(i):
                r = 128 if i < NT else NB
                gp.wait_ge(f_sc, i + 1)
                gp.tensor_tensor(x1[0:r, i, :], x1[0:r, i, :], lnf[0:r, :], MUL).then_inc(f_out, 1)

            gp.wait_ge(f_gf, 16)
            gp.wait_ge(s_stored, 1)
            for i in range(NT + 1):
                gather2(i)
            for i in range(NT + 1):
                gp.wait_ge(f_ms, i + 1)
                x = st[:, i:i + 1]
                gp.tensor_tensor(x, x, consts[:, C_NH:C_NH + 1], ALU.pow).then_inc(f_rs, 1)
                if i >= 1:
                    gain(i - 1)
            gain(NT)
            gp.wait_ge(s_dst, 32)
            gp.wait_ge(s_fx, 32)
            for n in range(2):
                gp.wait_ge(s_ust[n], 16 * (CH // 2))
                gp.wait_ge(s_hst[n], 16 * ((NT + 2 - n) // 2))
            gp.wait_ge(s_kst, 16 * NT)
            gp.wait_ge(s_vst, 16 * NT)

        @block.scalar
        def _(act):
            def stats():
                for k in range(KD):
                    act.wait_ge(s_xk[k], 16)
                    if k >= 2:
                        act.wait_ge(s_sqread, k - 1)
                    act.activation(sq[:, k % 2, :], xm[:, k, :], ACT.Square).then_inc(s_sq, 1)

            def dqkv():
                act.wait_ge(*filled("dp"))
                for n, out in enumerate((qk[0:NB, 0:QKW], qk[0:NB, QKW:2 * QKW], dvu[:, 0:QKW], dvu[:, QKW:2 * QKW])):
                    act.activation(out, slot("dp")[32 * n:32 * n + NB, 0:QKW], ACT.Copy)
                act.drain().then_inc(free_sem("dp"), 1)
                act.drain().then_inc(s_dq, 1)

            def u(s):
                act.wait_ge(s_rstd, 1)
                if s < 2:
                    act.wait_ge(*filled("dqt"))
                    act.wait_ge(s_dst, 32)
                else:
                    act.wait_ge(s_ust[s % 2], 16 * (s // 2))
                act.wait_ge(*filled("u", s))
                act.activation(qk[:, QKW * (s % 2):QKW * (s % 2) + QKW], slot("u", s)[:, 0:QKW], ACT.Copy,
                               scale=rstd[:, NT + s:NT + s + 1]).then_inc(s_u, 1)
                act.drain().then_inc(free_sem("u", s), 1)

            def qk_(i, n):
                if n == 0:
                    return
                if i >= 1:
                    act.wait_ge(*filled("qkT", i - 1))
                    act.wait_ge(s_kst, 16 * i)
                else:
                    for n in range(2):
                        act.wait_ge(s_ust[n], 16 * (CH // 2))
                act.wait_ge(*filled("qk", i))
                act.activation(qk, slot("qk", i)[:, :], ACT.Copy,
                               scale=rstd[:, i:i + 1]).then_inc(s_qk, 1)
                act.drain().then_inc(free_sem("qk", i), 1)

            def v(i):
                act.wait_ge(*filled("v", i))
                act.activation(V[:, i, :], slot("v", i)[:, 0:QKW], ACT.Copy,
                               scale=rstd[:, i:i + 1]).then_inc(s_v, 1)
                act.drain().then_inc(free_sem("v", i), 1)

            def qt(i):
                act.wait_ge(*filled("qkT", i))
                src = slot("qkT", i)[:, :].rearrange("p (a h n) -> p a h n", a=2, h=H)
                if i >= 1:
                    act.wait_ge(*filled("S", i - 1, H - 1, 1))
                act.activation(qT, src[:, 0, :, :], ACT.Copy)
                act.activation(kT[:, :, 128 * i:128 * i + 128], src[:, 1, :, :], ACT.Copy)
                act.drain().then_inc(free_sem("qkT", i), 1)
                act.drain().then_inc(s_qkT, 1)

            def s(i, h):
                n, w = H * i + h, 128 * (i + 1)
                if n >= 2:
                    act.wait_ge(*filled("O", (n - 2) // H, (n - 2) % H))
                for c in range(2):
                    act.wait_ge(s_mx, 2 * n + c + 1)
                    act.activation(P[:, n % 2, c, 0:w], slot("S", i, h, c)[:, 0:w], ACT.Exp,
                                   bias=st[:, 4 * (n % 2) + c:4 * (n % 2) + c + 1], scale=HD ** -0.5,
                                   accum_out=st[:, 4 * (n % 2) + 2 + c:4 * (n % 2) + 3 + c])
                    act.drain().then_inc(free_sem("S", i, h, c), 1)
                    act.drain().then_inc(s_exp, 1)

            def av(i, h):
                n, w = H * i + h, 128 * (i + 1)
                act.wait_ge(*filled("AT", i, h))
                act.activation(P[:, n % 2, 1, 0:w], slot("AT", i, h)[:, 0:w], ACT.Copy).then_inc(s_ATs, 1)
                act.drain().then_inc(free_sem("AT", i, h), 1)

            def ot(i):
                act.wait_ge(*filled("oT", i))
                for h in range(H):
                    act.activation(xm[:, h, 128 * i:128 * i + 128], slot("oT", i)[:, 128 * h:128 * h + 128],
                                   ACT.Copy, scale=colw[:, 2 * KD:2 * KD + 1])
                act.drain().then_inc(free_sem("oT", i), 1)
                act.drain().then_inc(s_mix, 1)

            def K(b, t, g):
                if t == 0 and g == 0 and b >= 1:
                    act.wait_ge(s_pv, b)
                if t == 0 and g == 0 and b == 0:
                    act.wait_ge(s_zst, 16 * (MAXT - NE))
                act.wait_ge(s_score, 2 * (TURNS * b + t) + g + 1)
                act.activation(sall[:, t, 256 * g:256 * g + 256], (SC, OD)[g][:, 0:256],
                               ACT.Copy).then_inc(s_evac, 1)

            def m3(b):
                act.wait_ge(s_nb, b + 1)
                act.activation(sall[:, :, :], sall[:, :, :], ACT.Exp, bias=mrow[:, 1:2], scale=HD ** -0.5,
                               accum_out=mrow[:, 2:3])
                act.activation(snew[:, :], snew[:, :], ACT.Exp, bias=mrow[:, 1:2], scale=HD ** -0.5,
                               accum_out=mrow[:, 3:4])
                act.drain().then_inc(s_pexp, 1)

            def pt(b):
                for n in range(2):
                    act.wait_ge(*filled("PT", b, n))
                    act.activation(sall[:, 2 * n:2 * n + 2, :].rearrange("p t n -> p (t n)"), slot("PT", b, n)[:, :],
                                   ACT.Copy)
                    act.drain().then_inc(free_sem("PT", b, n), 1)
                act.wait_ge(*filled("PTn", b))
                act.activation(ptn[:, :], slot("PTn", b)[0:NB, 0:128], ACT.Copy)
                act.drain().then_inc(free_sem("PTn", b), 1)
                act.drain().then_inc(s_ptw, 1)

            def s5a():
                act.wait_ge(s_ld5, 32)
                act.activation(sm5[:, 0, :], par[:, 2, :], ACT.Exp).then_inc(s_act5, 1)
                act.wait_ge(s_dve5, 1)
                act.activation(sm5[:, 3, :], sm5[:, 1, :], ACT.Exp).then_inc(s_act5, 1)
                act.activation(sm5[:, 6:8, :], sm5[:, 4:6, :], ACT.Sin).then_inc(s_act5, 1)

            def evac(key, n, out, src, sem_, scale=1.0):
                act.activation(out, src, ACT.Copy, scale=scale)
                act.drain().then_inc(free_sem(key, n), 1)
                act.drain().then_inc(sem_, 1)

            def s5pt():
                flat = PT5.rearrange("p m j q -> p (m j q)")
                act.wait_ge(s_u5, 48)
                act.activation(ug, usb.rearrange("p s (g h) -> p g s h", g=G5), ACT.Copy)
                act.drain().then_inc(s_ug, 1)
                for n in range(4):
                    act.wait_ge(*filled("pt", n))
                    evac("pt", n, flat[:, 1024 * n:1024 * n + 1024], slot("pt", n)[:, :], s_pt5)

            def s5k():
                act.wait_ge(*filled("U", 7))
                for n in range(4):
                    act.wait_ge(*filled("k", n))
                    evac("k", n, Ksb[:, 8 * n:8 * n + 8, :].rearrange("p (j e) q -> p e j q", e=2),
                         slot("k", n)[:, :].rearrange("p (e j q) -> p e j q", e=2, j=4), s_ks)

            def s5u(n):
                act.wait_ge(*filled("pt", 3))
                act.wait_ge(*filled("U", n))
                act.activation(U[:, 4 * n:4 * n + 4, 0:NC],
                               slot("U", n)[:, 0:512].rearrange("p (g c) -> p g c", g=4), ACT.Copy)
                evac("U", n, U[:, 4 * n:4 * n + 4, NC:NC + 16],
                     slot("U", n)[:, 512:576].rearrange("p (g c) -> p g c", g=4), s_Us)

            def s5x(n):
                act.wait_ge(*filled("X", n))
                if n == 0:
                    act.wait_ge(s_Tz, 2)
                for j in range(2):
                    act.activation(Hs[:, :, 2 * n + j, 1:145],
                                   slot("X", n)[:, 512 * j:512 * j + 288].rearrange("p (m c) -> p m c", m=2), ACT.Copy)
                act.drain().then_inc(free_sem("X", n), 1)
                act.drain().then_inc(s_Xs, 1)

            def s5g(n):
                act.wait_ge(s_th, 2 * n + 1)
                t = tmp5[0:NB, 0:512] if n == 2 else tmp5[:, 2048 * (n % 2):2048 * (n % 2) + 2048]
                act.activation(t, t, ACT.Tanh, scale=GELU_C).then_inc(s_g5, 1)

            def s5t(n):
                act.wait_ge(*filled("yT", n))
                if n == 0:
                    act.wait_ge(s_Td, 16 * CH)
                if n < 4:
                    for s in range(2):
                        act.activation(yT[:, :, 2 * n + s:SEQ:CH],
                                       slot("yT", n)[:, 512 * s:512 * s + 512].rearrange("p (k c) -> p k c", k=4),
                                       ACT.Copy, scale=0.5)
                else:
                    act.activation(yT[:, :, SEQ:TT], slot("yT", n)[:, 0:4 * NB].rearrange("p (k c) -> p k c", k=4),
                                   ACT.Copy, scale=0.5)
                act.drain().then_inc(free_sem("yT", n), 1)
                act.drain().then_inc(s_yT, 1)

            def glu(n):
                act.wait_ge(*filled("z", n))
                if n >= 2:
                    act.wait_ge(s_mix2, n - 1)
                t = tmp5[:, 1024 * (n % 2):1024 * (n % 2) + 1024]
                if n < 4:
                    act.activation(t, slot("z", n)[:, :], ACT.Tanh, bias=bglu[:, n:n + 1], scale=0.5)
                else:
                    for m in range(4):
                        act.activation(t[:, NB * m:NB * m + NB], slot("z", n)[:, NB * m:NB * m + NB], ACT.Tanh,
                                       bias=bglu[:, m:m + 1], scale=0.5)
                act.drain().then_inc(free_sem("z", n), 1)
                act.drain().then_inc(s_zt, 1)

            def ht(i):
                r = 128 if i < NT else NB
                act.wait_ge(s_xo, i + 1)
                if i >= 2:
                    act.wait_ge(s_hst[i % 2], 16 * (i // 2))
                    act.wait_ge(*filled("hT", i - 2))
                act.activation(h2[0:r, i % 2, :], x1[0:r, i, :], ACT.Square,
                               accum_out=st[0:r, 28 + i % 2:29 + i % 2]).then_inc(s_sq2, 1)

            def choose(lo, hi):
                act.wait_ge(s_rexp, 1 + lo // NT)
                act.activation(rtf[:, 5 * lo:5 * hi], rtf[:, 5 * lo:5 * hi], ACT.Exp).then_inc(s_rex2, 1)

            later = {"s5a": s5a, "s5pt": s5pt, "s5k": s5k, "s5u": s5u, "s5x": s5x, "s5g": s5g, "s5t": s5t,
                     "glu": glu, "ht": ht, "choose": choose}
            act.wait_ge(s_lam, 1)
            act.activation(lamt[:, 2:4], lamt[:, 0:2], ACT.Exp).then_inc(s_lam, 1)
            todo = {"stats": stats, "dqkv": dqkv, "u": u, "qk": qk_, "v": v, "qt": qt, "s": s, "av": av,
                    "ot": ot, "m3": m3, "K": K, "pt": pt, **later}
            for unit in PLAN:
                if unit[0] in todo:
                    todo[unit[0]](*unit[1:])

            def tanh(q, v):
                act.wait_ge(m_gu, 4 * q + (v + 1))
                act.activation(tg[v % 2], W[2][:, 512 * (v % 2):512 * (v % 2) + 256], ACT.Tanh, scale=0.5)\
                    .then_inc(m_th, 1)

            def turned(q, v):
                act.wait_ge(m_heT, 4 * q + (v + 1))
                act.activation(heT_[v % 2], (SC, OD)[v % 2][:, 0:256], ACT.Copy, scale=0.5).then_inc(m_heS, 1)

            def store(q, v, first=False):
                act.wait_ge(m_y, 4 * q + (v + 1))
                if not (first and v < 2):
                    act.wait_ge(m_st[v % 2], 32 * q + 16 * (v // 2))
                act.activation(yb[v % 2], W[1][:, :], ACT.Copy).then_inc(m_ys, 1)
                act.wait_ge(m_ys, 4 * q + (v + 1))
                act.dma_start(io["y_scratch"][bass.ds(512 * q + 128 * v, 128), :], yb[v % 2]).then_inc(m_st[v % 2], 16)

            def step(q, v, first=False, last=False):
                turned(q, v)
                if not (last and v == 3):
                    tanh(q, v + 1)
                store(q, v, first)

            act.wait_ge(s_route, 1)
            n4 = act.value_load(plan_t[0:1, MAXT:MAXT + 1], min_val=NE // 4, max_val=MAXT // 4)
            n3 = act.value_load(plan_t[0:1, MAXT + 1:MAXT + 2], min_val=NE // 4 - 1, max_val=MAXT // 4 - 1)
            tanh(0, 0)
            for v in range(4):
                step(0, v, first=True)
            with act.Fori(1, n3) as q:
                for v in range(4):
                    step(q, v)
            for v in range(4):
                step(n3, v, last=True)
            for n in range(2):
                act.wait_ge(m_st[n], 32 * n4)
            act.nop().then_inc(s_stored, 1)

            def by_rstd(i):
                r = 128 if i < NT else NB
                act.wait_ge(f_rs, i + 1)
                act.activation(x1[0:r, i, :], x1[0:r, i, :], ACT.Copy, scale=st[0:r, i:i + 1]).then_inc(f_sc, 1)

            for i in range(NT + 1):
                act.wait_ge(f_x, i + 1)
                r = 128 if i < NT else NB
                act.activation(yb[i % 2][0:r, :], x1[0:r, i, :], ACT.Square, accum_out=st[0:r, i:i + 1]).then_inc(f_sq, 1)
                if i >= 1:
                    by_rstd(i - 1)
            by_rstd(NT)

        @block.vector
        def _(dve):
            def root(key):
                dve.drain().then_inc(s_ms, 1)
                dve.wait_ge(s_rs, POW[key] + 1)

            def mean_sq(out, in_, n):
                dve.tensor_scalar(out, in_, 1.0 / n, EPS, MUL, ADD)

            def rotate(x, rows, tile):
                v = x.rearrange("p (g d) -> p g d", d=HD)
                x1, x2 = v[:, :, 0:NROT], v[:, :, NROT:2 * NROT]
                cos = rope[0:rows, tile:tile + 1, 0:NROT].to_broadcast([rows, 16, NROT])
                sin = rope[0:rows, tile:tile + 1, NROT:].to_broadcast([rows, 16, NROT])
                t = [rt[0:rows, :, :, j] for j in range(4)]
                dve.tensor_tensor(t[0], x1, cos, MUL)
                dve.tensor_tensor(t[1], x2, sin, MUL)
                dve.tensor_tensor(t[2], x2, cos, MUL)
                dve.tensor_tensor(t[3], x1, sin, MUL)
                dve.drain()
                dve.tensor_tensor(x1, t[0], t[1], SUB)
                dve.tensor_tensor(x2, t[2], t[3], ADD)
                dve.drain()

            def lam():
                dve.wait_ge(s_lamv, 16)
                dve.tensor_tensor(lamv[:, 0, :], lamv[:, 0, :], lamv[:, 1, :], MUL)
                dve.tensor_tensor(lamv[:, 2, :], lamv[:, 2, :], lamv[:, 3, :], MUL)
                dve.drain()
                dve.reduce_sum(lamt[:, 0:1], lamv[:, 0, :], AX)
                dve.reduce_sum(lamt[:, 1:2], lamv[:, 2, :], AX)
                dve.drain().then_inc(s_lam, 1)
                dve.wait_ge(s_lam, 2)
                dve.tensor_tensor(lamt[:, 4:5], lamt[:, 3:4], lamt[:, 2:3], SUB)
                dve.drain()
                dve.tensor_scalar(lamt[:, 7:8], lamt[:, 4:5], -LINIT, None, ADD)
                dve.drain()

            def stats():
                lam()
                dve.wait_ge(s_cst, 112)
                for k in range(KD):
                    dve.wait_ge(s_sq, k + 1)
                    dve.tensor_scalar(xm[:, k, :], xm[:, k, :], colw[:, k:k + 1], None, MUL).then_inc(s_xg, 1)
                dve.wait_ge(*filled("ss"))
                dve.tensor_copy(sumrow[:, 0:SEQ], slot("ss")[0:1, :])
                dve.tensor_copy(sumrow[:, SEQ:TT], SC[0:1, 0:NB])
                dve.drain().then_inc(free_sem("ss"), 1)
                dve.drain().then_inc(s_row, 1)
                dve.memset(rstd[:, 2 * NT:2 * NT + 1], 1.0)
                dve.scalar_tensor_tensor(wmap[:, 0, :], consts[:, C_M1:C_M1 + H], lamt[:, 7:8],
                                         consts[:, C_M0:C_M0 + H], MUL, ADD)
                dve.drain()
                dve.wait_ge(s_col, 1)
                mean_sq(rstd[:, 0:2 * NT], OD[:, 0:2 * NT], D)
                mean_sq(rstd[0:NB, 2 * NT:2 * NT + 1], OD[0:NB, 2 * NT:2 * NT + 1], D)
                root(("stats",))
                dve.tensor_scalar(bglu[:, :], bglu[:, :], 0.5, None, MUL)
                dve.memset(logit[:, NT, :], 0.0)
                dve.memset(st[:, :], 1.0)
                dve.tensor_scalar(colw[:, 2 * KD:2 * KD + 1], colw[:, 2 * KD:2 * KD + 1], 1.0 - LINIT, None, MUL)
                dve.drain().then_inc(s_rstd, 1)

            def dqkv():
                dve.wait_ge(s_dq, 1)
                r = rstd[0:NB, 2 * NT:2 * NT + 1]
                dve.tensor_scalar(qk[0:NB, :], qk[0:NB, :], r, None, MUL)
                dve.tensor_scalar(dvu[:, :], dvu[:, :], r, None, MUL)
                dve.drain()
                rotate(qk[0:NB, :], NB, NT)
                dve.drain().then_inc(s_drope, 1)

            def dprep():
                dve.wait_ge(s_qbd, 1)
                dve.wait_ge(*filled("dqt"))
                src = slot("dqt")[:, 0:2 * H * NB].rearrange("p (a h b) -> p a h b", a=2, h=H)
                for h in range(H):
                    for c in range(2):
                        dve.tensor_copy(qpad[64 * c:64 * c + 64, h, :, 2 * h + c], src[64 * c:64 * c + 64, 0, h, :])
                dve.tensor_copy(knT[:, :, :], src[:, 1, :, :])
                dve.drain().then_inc(free_sem("dqt"), 1)
                dve.drain().then_inc(s_qbd, 1)

            def v(i):
                dve.wait_ge(s_qk, i + 1)
                rotate(qk, 128, i)
                dve.drain().then_inc(s_rope, 1)

            def s(i, h):
                n, w = H * i + h, 128 * (i + 1)
                for c in range(2):
                    dve.wait_ge(*filled("S", i, h, c))
                    S = slot("S", i, h, c)
                    dve.tensor_tensor(S[:, 128 * i:w], S[:, 128 * i:w], causal, ADD)
                    dve.drain()
                    dve.reduce_max(st[:, 8 + c:9 + c], S[:, 0:w], AX)
                    dve.drain()
                    dve.tensor_scalar(st[:, 4 * (n % 2) + c:4 * (n % 2) + c + 1], st[:, 8 + c:9 + c],
                                      -HD ** -0.5, None, MUL)
                    dve.drain().then_inc(s_mx, 1)
                dve.wait_ge(s_exp, 2 * n + 2)
                l0, l1 = (st[:, 4 * (n % 2) + 2 + c:4 * (n % 2) + 3 + c] for c in range(2))
                r0, r1, cf = (st[:, 16 + 4 * (n % 2) + c:17 + 4 * (n % 2) + c] for c in range(3))
                dve.reciprocal(r0, l0)
                dve.reciprocal(r1, l1)
                dve.drain()
                dve.scalar_tensor_tensor(cf, l0, lamt[:, 7:8], r1, MUL, MUL)
                dve.drain()
                dve.scalar_tensor_tensor(P[:, n % 2, 0, 0:w], P[:, n % 2, 1, 0:w], cf,
                                         P[:, n % 2, 0, 0:w], MUL, ADD)
                dve.drain().then_inc(s_comb, 1)

            def av(i, h):
                n = H * i + h
                dve.wait_ge(*filled("O", i, h))
                if h == 0 and i >= 1:
                    dve.wait_ge(*filled("oT", i - 1))
                o = att[:, 128 * h:128 * h + 128]
                dve.tensor_scalar(o, slot("O", i, h)[:, 0:VD], st[:, 16 + 4 * (n % 2):17 + 4 * (n % 2)], None, MUL)
                dve.drain().then_inc(free_sem("O", i, h), 1)
                dve.tensor_tensor(rtf[:, 0:128], o, o, MUL)
                dve.drain()
                dve.reduce_sum(st[:, 24 + h:25 + h], rtf[:, 0:128], AX)
                dve.drain()
                if h == H - 1:
                    mean_sq(st[:, 24:28], st[:, 24:28], VD)
                    root(("av", i, h))
                    dve.tensor_tensor(att.rearrange("p (h d) -> p h d", h=H), att.rearrange("p (h d) -> p h d", h=H),
                                      st[:, 24:28].unsqueeze(2).to_broadcast([128, H, VD]), MUL)
                    dve.drain().then_inc(s_att, 1)

            def m1(b):
                if b >= 1:
                    dve.wait_ge(s_ptw, b)
                dve.memset(snew[:, :], NEG)
                dve.drain()
                dve.wait_ge(s_nk, b + 1)
                dve.tensor_tensor(snew[0:32, :], nkP, consts[0:32, C_NEG + 8 * b:C_NEG + 8 * b + 8], ADD)
                dve.wait_ge(s_evac, 2 * TURNS * (b + 1))
                dve.drain()
                dve.reduce_max(mrow[:, 0:1], sall[:, :, :].rearrange("p t n -> p (t n)"), AX)
                dve.reduce_max(mrow[:, 1:2], snew[:, :], AX)
                dve.drain()
                dve.tensor_tensor(mrow[:, 0:1], mrow[:, 0:1], mrow[:, 1:2], MAX)
                dve.drain().then_inc(s_m1, 1)

            def m2(b):
                dve.wait_ge(s_mT, b + 1)
                dve.reduce_max(mrep[:, 0, :], mxT.rearrange("a (j e) -> a e j", j=4), AX)
                dve.drain()
                dve.tensor_copy(mrep[:, 1:4, :], mrep[:, 0:1, :].to_broadcast([1, 3, 32]))
                dve.drain().then_inc(s_mrep, 1)

            def m3(b):
                dve.wait_ge(s_mb, b + 1)
                dve.tensor_scalar(mrow[:, 1:2], mbP, -HD ** -0.5, None, MUL)
                dve.drain().then_inc(s_nb, 1)

            def pt(b):
                dve.wait_ge(s_pexp, b + 1)
                dve.tensor_tensor(mrow[:, 2:3], mrow[:, 2:3], mrow[:, 3:4], ADD)
                dve.drain().then_inc(s_l, 1)

            def ov(b):
                dve.wait_ge(s_lP, b + 1)
                dve.wait_ge(s_pv, b + 1)
                dve.tensor_copy(o4s[:, :], SC[:, :])
                dve.reciprocal(mrow[:, 4:5], lP)
                dve.drain()
                dve.tensor_scalar(wmap[:, 1, :], wmap[:, 0, :], mrow[:, 4:5], None, MUL)
                dve.drain().then_inc(s_o4, 1)
                dve.wait_ge(s_aP, b + 1)
                dve.tensor_copy(aD[:, :, b], aP)
                dve.drain().then_inc(s_ad, 1)

            def dout():
                dve.tensor_tensor(aD2[:, :, :], aD[:, :, :], aD[:, :, :], MUL)
                dve.drain().then_inc(s_ad2, 1)
                dve.wait_ge(*filled("dss"))
                mean_sq(aD2[:, :, :], slot("dss")[:, 0:H * NB].rearrange("p (h b) -> p h b", h=H), VD)
                root(("dout",))
                dve.drain().then_inc(free_sem("dss"), 1)
                dve.tensor_tensor(aD2[:, :, :], aD2[:, :, :], aD[:, :, :], MUL)
                dve.drain()
                dve.tensor_scalar(xm[:, 0:H, SEQ:TT], aD2[:, :, :], colw[:, 2 * KD:2 * KD + 1], None, MUL)
                dve.drain().then_inc(s_dmix, 1)

            def cmul(out, a, b, t, neg_im=False):
                dve.tensor_tensor(out[0], a[0], b[0], MUL)
                dve.tensor_tensor(t[0], a[1], b[1], MUL)
                dve.tensor_tensor(out[1], a[0], b[1], MUL)
                dve.tensor_tensor(t[1], a[1], b[0], MUL)
                dve.drain()
                dve.tensor_tensor(out[0], out[0], t[0], SUB)
                if neg_im:
                    dve.scalar_tensor_tensor(out[1], out[1], -1.0, t[1], MUL, SUB)
                else:
                    dve.tensor_tensor(out[1], out[1], t[1], ADD)
                dve.drain()

            def s5a():
                dve.wait_ge(s_ld5, 32)
                dve.wait_ge(s_act5, 1)
                v = [sm5[:, a, :] for a in range(20)]
                dve.tensor_tensor(v[1], par[:, 0, :], v[0], MUL)
                dve.tensor_tensor(v[2], par[:, 1, :], v[0], MUL)
                dve.drain()
                dve.tensor_scalar(v[8], v[2], float(1 / (2 * np.pi)), None, MUL)
                dve.drain()
                dve.tensor_scalar(v[8], v[8], MAGIC, None, ADD)
                dve.drain()
                dve.tensor_scalar(v[8], v[8], MAGIC, None, SUB)
                for c in (6.28125, 0.001934051513671875, float(2 * np.pi - 6.28125 - 0.001934051513671875)):
                    dve.drain()
                    dve.scalar_tensor_tensor(v[2], v[8], -c, v[2], MUL, ADD)
                dve.drain()
                dve.tensor_scalar(v[4], v[2], 3.1415925, -3.1415925, MIN, MAX)
                dve.drain()
                dve.scalar_tensor_tensor(v[5], v[4], -1.0, v[4], MUL, MAX)
                dve.drain()
                dve.tensor_scalar(v[5], v[5], -1.0, float(np.pi / 2), MUL, ADD)
                dve.drain().then_inc(s_dve5, 1)
                dve.wait_ge(s_act5, 3)
                dve.memset(Lp[:, 0, 0, :], 1.0)
                dve.memset(Lp[:, 1, 0, :], 0.0)
                dve.tensor_tensor(Lp[:, 0, 1, :], v[3], v[7], MUL)
                dve.tensor_tensor(Lp[:, 1, 1, :], v[3], v[6], MUL)
                dve.drain()
                t = (v[16], v[17])
                L = [(Lp[:, 0, k, :], Lp[:, 1, k, :]) for k in range(CH + 1)]
                for k in range(2, CH + 1):
                    cmul(L[k], L[k - 1], L[1], t)
                for k in range(CH):
                    dve.tensor_copy(LpR[:, :, :, CH - 1 - k], Lp[:, :, k, :])
                dve.tensor_scalar(v[8], L[1][0], -1.0, None, ADD)
                dve.tensor_scalar(v[9], par[:, 1, :], -1.0, None, MUL)
                dve.tensor_tensor(v[10], par[:, 0, :], par[:, 0, :], MUL)
                dve.tensor_tensor(v[11], par[:, 1, :], par[:, 1, :], MUL)
                dve.drain()
                dve.tensor_tensor(v[10], v[10], v[11], ADD)
                dve.drain()
                dve.reciprocal(v[10], v[10])
                cmul((v[12], v[13]), (v[8], L[1][1]), (par[:, 0, :], v[9]), t)
                dve.tensor_tensor(v[12], v[12], v[10], MUL)
                dve.tensor_tensor(v[13], v[13], v[10], MUL)
                dve.drain()
                full = [128, NP5, W5]
                f = [v[12 + m].unsqueeze(2).to_broadcast(full) for m in range(2)]
                t0 = [tmp5[:, 256 * m:256 * m + 256].rearrange("p (j h) -> p j h", j=NP5) for m in range(4)]
                dve.tensor_copy(t0[2], bc[:, 0, 0, :, :])
                dve.tensor_copy(t0[3], bc[:, 0, 1, :, :])
                dve.drain()
                B = (bc[:, 0, 0, :, :], bc[:, 0, 1, :, :])
                cmul(B, (t0[2], t0[3]), f, t0[0:2])
                full = [128, NP5, CH, W5]
                t1 = [tmp5[:, 2048 * m:2048 * m + 2048].rearrange("p (j s h) -> p j s h", j=NP5, s=CH) for m in range(2)]
                cmul((PB[:, 0, :, :, :], PB[:, 1, :, :, :]),
                     [b.unsqueeze(2).to_broadcast(full) for b in B],
                     [LpR[:, m, :, :].unsqueeze(3).to_broadcast(full) for m in range(2)], t1)
                dve.drain().then_inc(s_dve5, 1)
                full = [128, NP5, CH + 1, W5]
                t2 = [region(13312 + 2304 * m, 2304, "p (j k h) -> p j k h", j=NP5, k=CH + 1) for m in range(2)]
                cmul((CLr, CLn), [bc[:, 1, m, :, :].unsqueeze(2).to_broadcast(full) for m in range(2)],
                     [Lp[:, m, :, :].rearrange("p k j -> p j k").unsqueeze(3).to_broadcast(full) for m in range(2)],
                     t2, neg_im=True)
                for m in range(2):
                    dve.tensor_copy(Bt[:, m, :, :, :], B[m].unsqueeze(2).to_broadcast([128, NP5, CH, W5]))
                dve.drain().then_inc(s_dve5, 1)

            def s5h(n):
                Q = [tmp5b[:, 128 * m:128 * m + 128].rearrange("p (k j) -> p k j", k=8) for m in range(2)]
                Hb = [Hs[:, m, :, 1:1 + NC].rearrange("p j (b k) -> p j b k", k=8) for m in range(2)]
                w = [tmp5[:, 256 * a:256 * a + 256].rearrange("p (j b) -> p j b", j=NP5) for a in range(4)]

                def step(dst, src, q, w):
                    dve.tensor_tensor(w[0], src[0], q[0], MUL)
                    dve.tensor_tensor(w[1], src[1], q[1], MUL)
                    dve.tensor_tensor(w[2], src[1], q[0], MUL)
                    dve.tensor_tensor(w[3], src[0], q[1], MUL)
                    dve.drain()
                    dve.tensor_tensor(w[0], w[0], w[1], SUB)
                    dve.tensor_tensor(w[2], w[2], w[3], ADD)
                    dve.drain()
                    dve.tensor_tensor(dst[0], dst[0], w[0], ADD)
                    dve.tensor_tensor(dst[1], dst[1], w[2], ADD)
                    dve.drain()

                if n == 0:
                    dve.wait_ge(s_Xs, 8)
                    dve.wait_ge(s_h0, 32)
                    t = [tmp5[:, 128 * a:128 * a + 128].rearrange("p (j b) -> p j b", j=NP5) for a in range(2)]
                    full = [128, NP5, NB]
                    cmul((hs8[:, 0, :, :], hs8[:, 1, :, :]), [Hs[:, m, :, NC + 1:NC + 1 + NB] for m in range(2)],
                         [Lp[:, m, 1, :].unsqueeze(2).to_broadcast(full) for m in range(2)], t)
                    for m in range(2):
                        dve.tensor_tensor(hs8[:, m, :, :], hs8[:, m, :, :], Hs[:, m, :, NC + 1 + NB:NC + 1 + 2 * NB],
                                          ADD)
                    dve.drain()
                    dve.wait_ge(s_Td, 16 * CH)
                    t = (sm5[:, 16, :], sm5[:, 17, :])
                    for m in range(2):
                        dve.tensor_copy(Q[m][:, 0, :], Lp[:, m, CH, :])
                    dve.drain()
                    for k in range(1, 8):
                        cmul([q[:, k, :] for q in Q], [q[:, k - 1, :] for q in Q], [q[:, 0, :] for q in Q], t)
                elif n == 1:
                    full = [128, NP5, 16]
                    for k in range(1, 8):
                        step([h[:, :, :, k] for h in Hb], [h[:, :, :, k - 1] for h in Hb],
                             [q[:, 0, :].unsqueeze(2).to_broadcast(full) for q in Q], w)
                elif n == 2:
                    for b in range(1, 16):
                        step([h[:, :, b, 7] for h in Hb], [h[:, :, b - 1, 7] for h in Hb], [q[:, 7, :] for q in Q],
                             [x[:, :, 0] for x in w])
                else:
                    full = [128, NP5, 15]
                    for k in range(7):
                        step([h[:, :, 1:16, k] for h in Hb], [h[:, :, 0:15, 7] for h in Hb],
                             [q[:, k, :].unsqueeze(2).to_broadcast(full) for q in Q], [x[:, :, 0:15] for x in w])
                    dve.tensor_copy(hp, Hs[:, :, :, NC])
                    dve.drain().then_inc(s_scan, 1)

            def s5y(n):
                if n == 0:
                    dve.wait_ge(s_du, 1)
                dve.wait_ge(*filled("Y", n))
                out = usb[:, :, 64 * n:64 * n + 64].rearrange("p s (g h) -> p g s h", g=4)
                for g in range(4):
                    dve.tensor_tensor(out[:, g, :, :], out[:, g, :, :],
                                      slot("Y", n)[:, 512 * (g % 2) + 128 * (g // 2):512 * (g % 2) + 128 * (g // 2) + 128]
                                      .rearrange("p (s h) -> p s h", s=CH), ADD)
                o = dvu[:, QKW + 64 * n:QKW + 64 * n + 64].rearrange("p (j e h) -> p e j h", j=2, e=2)
                dve.tensor_tensor(o, o, slot("Y", n)[0:NB, :].rearrange("p (e c) -> p e c", e=2)[:, :, 256:288]
                                  .rearrange("p e (j h) -> p e j h", j=2), ADD)
                dve.drain().then_inc(free_sem("Y", n), 1)

            def s5g(n):
                if n == 2:
                    x, t = dvu[:, QKW:2 * QKW], tmp5[0:NB, 0:512]
                    dve.wait_ge(s_th, 2)
                else:
                    x = usb[:, 4 * n:4 * n + 4, :].rearrange("p s n -> p (s n)")
                    t = tmp5[:, 2048 * n:2048 * n + 2048]
                dve.tensor_tensor(t, x, x, MUL)
                dve.drain()
                dve.tensor_scalar(t, t, 0.044715, 1.0, MUL, ADD)
                dve.drain()
                dve.tensor_tensor(t, t, x, MUL)
                dve.drain().then_inc(s_th, 1)
                dve.wait_ge(s_g5, n + 1)
                dve.scalar_tensor_tensor(x, t, 1.0, x, ADD, MUL)
                dve.drain().then_inc(s_th, 1)

            def glu(n):
                if n == 0:
                    dve.wait_ge(*filled("Y", 7))
                dve.wait_ge(s_zt, n + 1)
                t = tmp5[:, 1024 * (n % 2):1024 * (n % 2) + 1024]
                if n < 4:
                    out, y = xm[:, 4 + n, 0:SEQ], yT[:, n, 0:SEQ]
                else:
                    t = t[:, 0:4 * NB]
                    out, y = xm[:, 4:8, SEQ:TT], yT[:, :, SEQ:TT]
                dve.tensor_scalar(t, t, 0.5, 0.5, MUL, ADD)
                dve.drain()
                dve.tensor_tensor(out, t if n < 4 else t.rearrange("p (k b) -> p k b", k=4), y, MUL)
                dve.drain().then_inc(s_mix2, 1)

            def out_(i, a):
                if i < NT and a == 0:
                    return
                r = 128 if i < NT else NB
                dve.wait_ge(s_x1, 16 * (NT + 1))
                dve.wait_ge(*filled("o", i))
                if i < NT:
                    dve.tensor_tensor(x1[0:r, i, :], x1[0:r, i, :], slot("o", i)[0:r, :], ADD)
                else:
                    for c in range(4):
                        q = x1[0:NB, NT, 256 * c:256 * c + 256]
                        dve.tensor_tensor(q, q, slot("o", i)[32 * c:32 * c + NB, 0:256], ADD)
                dve.drain().then_inc(free_sem("o", i), 1)
                dve.drain().then_inc(s_xo, 1)

            def ht(i):
                r = 128 if i < NT else NB
                dve.wait_ge(s_sq2, i + 1)
                mean_sq(st[:, 28 + i % 2:29 + i % 2], st[:, 28 + i % 2:29 + i % 2], D)
                root(("ht", i))
                dve.tensor_scalar(h2[0:r, i % 2, :], x1[0:r, i, :], st[0:r, 28 + i % 2:29 + i % 2], None, MUL)
                dve.drain().then_inc(s_h2, 1)
                dve.wait_ge(*filled("hT", i))
                if i >= 2:
                    dve.wait_ge(*filled("r", i - 2))
                dve.tensor_tensor(h2T[:, i % 2, :, 0:r], slot("hT", i)[:, :].rearrange("p (k n) -> p k n", k=KD)[:, :, 0:r],
                                  colw[:, KD:2 * KD].unsqueeze(2).to_broadcast([128, KD, r]), MUL)
                dve.drain().then_inc(free_sem("hT", i), 1)
                dve.drain().then_inc(s_h2T, 1)
                dve.wait_ge(*filled("r", i))
                dve.tensor_tensor(logit[0:r, i, :], slot("r", i)[0:r, 0:36], br[0:r, :], ADD)
                dve.drain().then_inc(free_sem("r", i), 1)

            used = [26368]

            def small(*shape):
                n = int(np.prod(shape))
                v = region(used[0], n)
                used[0] += n
                return v if len(shape) == 1 else v.rearrange("p (a b) -> p a b", a=shape[0])

            T9, EQ = NT + 1, ALU.is_equal
            ex = rtf[:, 0:5 * T9].rearrange("p (t n) -> p t n", t=T9)
            over, incl, B, zero = (rtf[:, 64 + 32 * a:96 + 32 * a] for a in range(4))
            big, cmp_ = region(25568, 288), region(25856, 512)
            f9, gtop, gsum, t1, t2 = (small(T9) for _ in range(5))
            v4, ghot = small(T9, NG), small(T9, NG)
            el, v8, hot1, hot2 = (small(T9, EG) for _ in range(4))

            def wide(x, n, t=T9):
                return x.unsqueeze(2).to_broadcast([128, t, n])

            def row(c, n, t=T9):
                return consts[:, c:c + n].unsqueeze(1).to_broadcast([128, t, n])

            def choose(lo, hi):
                if lo == 0:
                    dve.wait_ge(s_fx, 32)
                dve.drain()
                t, m = slice(lo, hi), hi - lo

                def first_max(x, n, top, v, hot):
                    dve.reduce_max(top, x, AX)
                    dve.drain()
                    dve.tensor_tensor(v, x, wide(top, n, m), EQ)
                    dve.drain()
                    dve.scalar_tensor_tensor(v, v, -8.0, row(C_I8, n, m), MUL, ADD)
                    dve.drain()
                    dve.tensor_reduce(f9[:, t], v, AX, MIN)
                    dve.drain()
                    dve.tensor_tensor(hot, v, wide(f9[:, t], n, m), EQ)
                    dve.drain()

                gl, els = logit[:, t, 0:NG], logit[:, t, NG:].rearrange("p t (g e) -> p t g e", g=NG)
                first_max(gl, NG, gtop[:, t], v4[:, t, :], ghot[:, t, :])
                dve.tensor_tensor(ex[:, t, 0:NG], gl, wide(gtop[:, t], NG, m), SUB)
                b4 = big[:, 32 * lo:32 * hi].rearrange("p (t g e) -> p t g e", t=m, g=NG)
                gh4 = ghot[:, t, :].unsqueeze(3).to_broadcast([128, m, NG, EG])
                dve.tensor_tensor(b4, els, gh4, MUL)
                dve.drain()
                dve.reduce_sum(el[:, t, :], b4.rearrange("p t g e -> p t e g"), AX)
                dve.drain()
                first_max(el[:, t, :], EG, t1[:, t], v8[:, t, :], hot1[:, t, :])
                dve.scalar_tensor_tensor(el[:, t, :], hot1[:, t, :], NEG, el[:, t, :], MUL, ADD)
                dve.drain()
                first_max(el[:, t, :], EG, t2[:, t], v8[:, t, :], hot2[:, t, :])
                dve.tensor_tensor(ex[:, t, NG], t2[:, t], t1[:, t], SUB)
                dve.drain().then_inc(s_rexp, 1)
                for hot in (hot1, hot2):
                    dve.tensor_tensor(hot[:, t, :], hot[:, t, :], wide(consts[:, C_VAL + lo:C_VAL + hi], EG, m), MUL)
                dve.memset(OHs[:, T9, :], 0.0)
                dve.drain()
                for c, hot in enumerate((hot1, hot2)):
                    dve.tensor_tensor(OH[c][:, t, :].rearrange("p t (g e) -> p t g e", g=NG), gh4,
                                      hot[:, t, :].unsqueeze(2).to_broadcast([128, m, NG, EG]), MUL)
                dve.drain()
                dve.tensor_tensor(OHs[:, t, :], OH[0][:, t, :], OH[1][:, t, :], ADD)
                dve.drain().then_inc(s_oh, 1)
                dve.wait_ge(s_rex2, 1 + lo // NT)
                dve.reduce_sum(gsum[:, t], ex[:, t, 0:NG], AX)
                dve.tensor_scalar(t1[:, t], ex[:, t, NG], 1.0, None, ADD)
                dve.drain()
                dve.tensor_tensor(gsum[:, t], gsum[:, t], t1[:, t], MUL)
                dve.drain()
                dve.reciprocal(wts[:, 0, t], gsum[:, t])
                dve.drain()
                dve.tensor_tensor(wts[:, 1, t], wts[:, 0, t], ex[:, t, NG], MUL)

            def route():
                dve.memset(zero, 0.0)
                dve.wait_ge(*filled("rank"))
                rank = slot("rank")[:, 0:288].rearrange("p (t e) -> p t e", t=T9)
                total = slot("rank")[:, 288:320]
                c8 = big[:, 0:256].rearrange("p (e m) -> p e m", m=EG)
                thr = consts[:, C_THR + 1:C_THR + 9].unsqueeze(1)
                dve.tensor_tensor(c8, total.unsqueeze(2).to_broadcast([128, NE, EG]), thr.to_broadcast([128, NE, EG]),
                                  ALU.is_gt)
                dve.drain()
                dve.reduce_sum(over, c8, AX)
                dve.drain()
                dve.tensor_tensor_scan(incl, zero, over, 0.0, ADD, ADD)
                dve.drain()
                dve.scalar_tensor_tensor(B, incl, float(NE - 1), over, ADD, SUB)
                dve.drain()
                dve.tensor_tensor(B, B, consts[:, C_I32:C_I32 + NE], SUB)
                dve.drain()
                r9, q9, e9, b9, g9 = f9, gtop, gsum, t1, t2
                c9 = v8
                big3 = big.rearrange("p (t e) -> p t e", t=T9)
                for c in range(2):
                    for src, out in ((rank, r9), (row(C_I32, NE), e9), (B.unsqueeze(1).to_broadcast([128, T9, NE]), b9)):
                        dve.tensor_tensor(big3, OH[c], src, MUL)
                        dve.drain()
                        dve.reduce_sum(out, big3, AX)
                        dve.drain()
                    dve.tensor_tensor(c9, wide(r9, EG), thr.to_broadcast([128, T9, EG]), ALU.is_ge)
                    dve.drain()
                    dve.reduce_sum(q9, c9, AX)
                    dve.drain()
                    dve.scalar_tensor_tensor(r9, q9, -128.0, r9, MUL, ADD)
                    dve.tensor_scalar(g9, q9, 0.0, None, ALU.is_gt)
                    dve.tensor_tensor(e9, e9, q9, ADD)
                    dve.drain()
                    dve.tensor_tensor(g9, g9, b9, MUL)
                    dve.drain()
                    dve.tensor_tensor(e9, e9, g9, ADD)
                    dve.drain()
                    dve.scalar_tensor_tensor(g9, e9, 128.0, r9, MUL, ADD)
                    dve.tensor_tensor(TO[c], row(C_TI, MAXT), wide(e9, MAXT), EQ)
                    dve.drain()
                    dve.tensor_copy(rows[:, c, :], g9)
                    dve.tensor_tensor(TO[c], TO[c], wide(consts[:, C_TOK:C_TOK + T9], MAXT), MUL)
                    if c == 1:
                        dve.tensor_tensor(R[1], row(C_TI, 128), wide(r9, 128), EQ)
                        dve.tensor_tensor(R[0], row(C_TI, 128), wide(v4[:, :, 0], 128), EQ)
                    else:
                        dve.tensor_copy(v4[:, :, 0], r9)
                    dve.drain()
                dve.drain().then_inc(s_lst, 1)
                dve.drain().then_inc(free_sem("rank"), 1)
                k16 = consts[0:1, C_TI:C_TI + 16].unsqueeze(2).to_broadcast([1, 16, NE])
                cm = cmp_.rearrange("p (k e) -> p k e", k=16)[0:1]
                te = rtf[0:1, 256:256 + MAXT + 2]
                dve.tensor_tensor(cm, incl[0:1, :].unsqueeze(1).to_broadcast([1, 16, NE]), k16, ALU.is_le)
                dve.tensor_copy(te[:, 0:NE], consts[0:1, C_I32:C_I32 + NE])
                dve.tensor_scalar(zero[0:1, 0:4], consts[0:1, C_I8:C_I8 + 4], 4.0, None, MUL)
                dve.drain()
                dve.reduce_sum(te[:, NE:MAXT], cm, AX)
                dve.tensor_tensor(zero[0:1, 4:8], incl[0:1, NE - 1:NE].to_broadcast([1, 4]), zero[0:1, 0:4], ALU.is_gt)
                dve.drain()
                dve.tensor_scalar(te[:, NE:MAXT], te[:, NE:MAXT], float(NE - 1), None, MIN)
                dve.reduce_sum(te[:, MAXT:MAXT + 1], zero[0:1, 4:8], AX)
                dve.drain()
                dve.tensor_scalar(te[:, MAXT + 1:], te[:, MAXT:MAXT + 1], float(NE // 4 - 1), None, ADD)
                dve.tensor_scalar(te[:, MAXT:MAXT + 1], te[:, MAXT:MAXT + 1], float(NE // 4), None, ADD)
                dve.drain()
                dve.tensor_copy(plan_t[:, :], te)
                dve.wait_ge(*filled("ids"))
                dve.tensor_copy(ids[:, :], slot("ids")[:, 0:MAXT])
                dve.drain().then_inc(free_sem("ids"), 1)
                dve.drain().then_inc(s_route, 1)

            later = {"s5a": s5a, "s5h": s5h, "s5y": s5y, "s5g": s5g, "glu": glu, "out": out_, "ht": ht,
                     "route": route, "choose": choose}
            todo = {"stats": stats, "dqkv": dqkv, "dprep": dprep, "v": v, "s": s, "av": av,
                    "m1": m1, "m2": m2, "m3": m3, "pt": pt, "ov": ov, "dout": dout, **later}
            for unit in PLAN:
                if unit[0] in todo:
                    todo[unit[0]](*unit[1:])

            def scale(q, v):
                dve.wait_ge(m_T, 4 * q + (v + 1))
                dve.tensor_tensor(hgT[v % 2], W[0][:, :].rearrange("p (k n) -> p k n", k=KD),
                                  colw[:, KD:2 * KD].unsqueeze(2).to_broadcast([128, KD, 128]), MUL).then_inc(m_hT, 1)

            def silu(q, v):
                gu = W[2][:, 512 * (v % 2):512 * (v % 2) + 512]
                dve.wait_ge(m_th, 4 * q + (v + 1))
                dve.scalar_tensor_tensor(he[v % 2], tg[v % 2], 1.0, gu[:, 0:DE], ADD, MUL)
                dve.drain()
                dve.tensor_tensor(he[v % 2], he[v % 2], gu[:, DE:], MUL).then_inc(m_he, 1)

            for n in range(2):
                dve.wait_ge(s_hst[n], 16 * ((NT + 2 - n) // 2))
            n3 = dve.value_load(plan_t[0:1, MAXT + 1:MAXT + 2], min_val=NE // 4 - 1, max_val=MAXT // 4 - 1)
            scale(0, 0)
            for v in range(4):
                silu(0, v)
                scale(0, v + 1)
            with dve.Fori(1, n3) as q:
                for v in range(4):
                    silu(q, v)
                    scale(q, v + 1)
            for v in range(4):
                silu(n3, v)
                if v < 3:
                    scale(n3, v + 1)

            def combine(i):
                r = 128 if i < NT else NB
                dve.wait_ge(f_g[i], 32)
                for c in range(2):
                    dve.scalar_tensor_tensor(x1[0:r, i, :], yg[i][c][0:r, :], wts[0:r, c, i:i + 1],
                                             x1[0:r, i, :], MUL, ADD)
                    dve.drain()
                dve.drain().then_inc(f_x, 1)

            def mean(i):
                dve.wait_ge(f_sq, i + 1)
                mean_sq(st[:, i:i + 1], st[:, i:i + 1], D)
                dve.drain().then_inc(f_ms, 1)

            for i in range(NT + 1):
                combine(i)
                if i >= 1:
                    mean(i - 1)
            mean(NT)

        @block.tensor
        def _(pe):
            def mm(out, lhsT, rhs, first=True, last=True, **kw):
                return pe.matmul(out, lhsT, rhs, start=first, stop=last, **kw)

            def stats():
                pe.nop().then_inc(s_pgfree, RING // GRP)
                pe.wait_ge(s_cst, 112)
                for k in range(KD):
                    pe.wait_ge(s_sq, k + 1)
                    for out, c0, c1 in ((slot("ss")[0:32, 0:512], 0, 512), (slot("ss")[0:32, 512:SEQ], 512, SEQ),
                                        (SC[0:32, 0:NB], SEQ, TT)):
                        last = mm(out, ones[:, 0:32], sq[:, k % 2, c0:c1], k == 0, k == KD - 1)
                    last.then_inc(s_sqread, 1)
                pe.wait_ge(s_sqread, KD)
                pe.nop().then_inc(full_sem("ss"), 1)
                pe.wait_ge(s_row, 1)
                for t in range(2 * NT + 1):
                    cols = (sumrow[:, 128 * t:128 * t + 128] if t < NT else
                            sumrow[:, t - NT:SEQ:CH] if t < 2 * NT else sumrow[:, SEQ:TT])
                    last = mm(OD[0:(NB if t == 2 * NT else 128), t:t + 1], cols, ones[0:1, 0:1], True, True,
                              skip_group_check=True)
                last.then_inc(s_col, 1)

            def dqkv():
                pe.wait_ge(s_xg, KD)
                vacant(pe, "dp")
                for k in range(KD):
                    pe.wait_ge(s_wk[k], 32)
                    for n in range(4):
                        w = w_qkv[:, k, 512 * n:512 * n + 512] if n < 3 else w_u[:, k, :]
                        last = mm(slot("dp")[32 * n:32 * n + NB, 0:512], xm[:, k, SEQ:TT], w, k == 0, k == KD - 1)
                last.then_inc(full_sem("dp"), 1)

            def dprep():
                pe.wait_ge(s_drope, 1)
                vacant(pe, "dqt")
                for j in range(2 * H):
                    last = pe.transpose(slot("dqt")[:, NB * j:NB * j + NB], qk[0:NB, 128 * j:128 * j + 128],
                                        ident[0:NB, 0:NB])
                last.then_inc(full_sem("dqt"), 1)

            def u(s):
                vacant(pe, "u", s)
                for k in range(KD):
                    last = mm(slot("u", s)[:, 0:QKW], xm[:, k, s:SEQ:CH], w_u[:, k, :], k == 0, k == KD - 1)
                last.then_inc(full_sem("u", s), 1)

            def product(out, i, n):
                for k in range(KD):
                    last = mm(out, xm[:, k, 128 * i:128 * i + 128], w_qkv[:, k, 512 * n:512 * n + 512],
                              k == 0, k == KD - 1)
                return last

            def qk_(i, n):
                if n == 0:
                    vacant(pe, "qk", i)
                last = product(slot("qk", i)[:, 512 * n:512 * n + 512], i, n)
                if n == 1:
                    last.then_inc(full_sem("qk", i), 1)

            def v(i):
                vacant(pe, "v", i)
                product(slot("v", i)[:, 0:512], i, 2).then_inc(full_sem("v", i), 1)

            def qt(i):
                pe.wait_ge(s_rope, i + 1)
                vacant(pe, "qkT", i)
                for j in range(2 * H):
                    last = pe.transpose(slot("qkT", i)[:, 128 * j:128 * j + 128], qk[:, 128 * j:128 * j + 128], ident)
                last.then_inc(full_sem("qkT", i), 1)

            def s(i, h):
                w = 128 * (i + 1)
                pe.wait_ge(s_qkT, i + 1)
                for c in range(2):
                    vacant(pe, "S", i, h, c)
                    for a in range(0, w, 512):
                        b = min(w, a + 512)
                        last = mm(slot("S", i, h, c)[:, a:b], qT[64 * c:64 * c + 64, h, :],
                                  kT[64 * c:64 * c + 64, h, a:b])
                    last.then_inc(full_sem("S", i, h, c), 1)

            def av(i, h):
                n = H * i + h
                pe.wait_ge(s_comb, n + 1)
                vacant(pe, "AT", i, h)
                for j in range(i + 1):
                    last = pe.transpose(slot("AT", i, h)[:, 128 * j:128 * j + 128],
                                        P[:, n % 2, 0, 128 * j:128 * j + 128], ident)
                last.then_inc(full_sem("AT", i, h), 1)
                vacant(pe, "O", i, h)
                pe.wait_ge(s_ATs, n + 1)
                pe.wait_ge(s_v, i + 1)
                for j in range(i + 1):
                    last = mm(slot("O", i, h)[:, 0:VD], P[:, n % 2, 1, 128 * j:128 * j + 128],
                              V[:, j, VD * h:VD * h + VD], j == 0, j == i)
                last.then_inc(full_sem("O", i, h), 1)

            def ot(i):
                pe.wait_ge(s_att, i + 1)
                vacant(pe, "oT", i)
                for h in range(H):
                    last = pe.transpose(slot("oT", i)[:, 128 * h:128 * h + 128], att[:, 128 * h:128 * h + 128], ident)
                last.then_inc(full_sem("oT", i), 1)

            def K(b, t, g):
                if t == 0 and g == 0:
                    pe.wait_ge(s_qbd, 2)
                    pe.wait_ge(s_rstd, 1)
                    if b >= 1:
                        pe.wait_ge(s_ad, b)
                pe.wait_ge(s_pg[g], 16 * GRP * (2 * TURNS * b + t + 1))
                if t:
                    pe.wait_ge(s_evac, 2 * (TURNS * b + t) + g - 1)
                for h in range(H):
                    for c in range(4):
                        last = mm((SC, OD)[g][32 * c:32 * c + 32, 0:256], qpad[:, h, b, :],
                                  ring[:, GRP * g + 2 * c:GRP * g + 2 * c + 2, 128 * h:128 * h + 128],
                                  h == 0, h == H - 1, skip_group_check=True)
                last.then_inc(s_score, 1)
                pe.wait_ge(s_score, 2 * (TURNS * b + t) + g + 1)
                pe.nop().then_inc(s_pgfree, 1)

            def m1(b):
                pe.wait_ge(s_evac, 2 * TURNS * (b + 1))
                for h in range(H):
                    last = mm(nkP, qpad[:, h, b, :], knT[:, h, :], h == 0, h == H - 1)
                last.then_inc(s_nk, 1)

            def m2(b):
                pe.wait_ge(s_m1, b + 1)
                pe.transpose(mxT, mrow[:, 0:1], ident).then_inc(s_mT, 1)

            def m3(b):
                pe.wait_ge(s_mrep, b + 1)
                mm(mbP, mrep[:, :, :].rearrange("a j e -> a (j e)"), ones[0:1, 0:1]).then_inc(s_mb, 1)

            def pt(b):
                pe.wait_ge(s_pexp, b + 1)
                for n in range(2):
                    vacant(pe, "PT", b, n)
                    for j in range(8):
                        last = pe.transpose(slot("PT", b, n)[:, 128 * j:128 * j + 128],
                                            sall[:, 2 * n + j // 4, 128 * (j % 4):128 * (j % 4) + 128], ident)
                    last.then_inc(full_sem("PT", b, n), 1)
                vacant(pe, "PTn", b)
                pe.transpose(slot("PTn", b)[0:NB, 0:128], snew[:, :], ident).then_inc(full_sem("PTn", b), 1)
                pe.wait_ge(s_l, b + 1)
                mm(lP, consts[:, C_SUM:C_SUM + 128], mrow[:, 2:3]).then_inc(s_lP, 1)

            def Vv(b, r, g):
                if r == 0 and g == 0:
                    pe.wait_ge(s_ptw, b + 1)
                pe.wait_ge(s_pg[g], 16 * GRP * (2 * TURNS * b + TURNS + r + 1))
                for j in range(GRP):
                    t, q, c = j // 2, j % 2, j % 4
                    blk = sall[:, r, 256 * g + 128 * q:256 * g + 128 * q + 128]
                    last = mm(SC[32 * c:32 * c + 32, :], blk[:, 32 * t:32 * t + 32], ring[:, GRP * g + j, :],
                              r == 0 and g == 0 and j < 4, r == TURNS - 1 and g == 1 and j >= 4 and c > 0,
                              skip_group_check=True)
                last.then_inc(s_pgfree, 1)
                if r == TURNS - 1 and g == 1:
                    mm(SC[0:32, :], ptn[:, 0:32], dvu[:, 0:QKW], False, True, skip_group_check=True).then_inc(s_pv, 1)

            def ov(b):
                pe.wait_ge(s_o4, b + 1)
                for h in range(H):
                    last = mm(aP[:, h:h + 1], o4s[:, 128 * h:128 * h + 128], wmap[:, 1, h:h + 1])
                last.then_inc(s_aP, 1)

            def dout():
                pe.wait_ge(s_ad2, 1)
                vacant(pe, "dss")
                mm(slot("dss")[:, 0:H * NB], ones, aD2[:, :, :].rearrange("p h b -> p (h b)"))\
                    .then_inc(full_sem("dss"), 1)

            def s5pt():
                pe.wait_ge(s_dve5, 2)
                for n in range(4):
                    vacant(pe, "pt", n)
                    for q in range(8):
                        m, j = divmod(8 * n + q, NP5)
                        last = pe.transpose(slot("pt", n)[:, 128 * q:128 * q + 128],
                                            PB[:, m, j, :, :].rearrange("p s h -> p (s h)"), ident)
                    last.then_inc(full_sem("pt", n), 1)

            def s5k():
                pe.wait_ge(s_dve5, 3)
                for n in range(4):
                    vacant(pe, "k", n)
                    for q in range(8):
                        j, e = divmod(8 * n + q, 2)
                        p = slice(64 * e, 64 * e + 64)
                        for m, C in enumerate((CLr, CLn)):
                            c = 512 * e + 128 * (q // 2)
                            last = mm(slot("k", n)[:, c:c + 128],
                                      Bt[p, m, j, :, :].rearrange("p s h -> p (s h)"),
                                      C[p, j, 0:CH, :].rearrange("p s h -> p (s h)"), m == 0, m == 1)
                    last.then_inc(full_sem("k", n), 1)

            def s5u(n):
                if n == 0:
                    pe.wait_ge(s_ug, 1)
                vacant(pe, "U", n)
                for q in range(4):
                    g = 4 * n + q
                    pe.transpose(slot("U", n)[:, 128 * q:128 * q + 128], ug[:, g, :, :].rearrange("p s h -> p (s h)"), ident)
                    last = pe.transpose(slot("U", n)[:, 512 + 16 * q:512 + 16 * q + 16],
                                        Z[:, g, :, :].rearrange("p s h -> p (s h)"), ident[0:16, 0:16])
                last.then_inc(full_sem("U", n), 1)

            def s5x(n):
                pe.wait_ge(s_pt5, 4)
                pe.wait_ge(s_Us, min(n + 1, 8))
                vacant(pe, "X", n)
                for q in range(2):
                    j = 2 * n + q
                    for m in range(2):
                        for e in range(2):
                            last = mm(slot("X", n)[64 * e:64 * e + 64, 512 * q + 144 * m:512 * q + 144 * m + 144],
                                      PT5[:, m, j, 64 * e:64 * e + 64], U[:, 2 * j + e, :], skip_group_check=True)
                last.then_inc(full_sem("X", n), 1)

            def s5y(n):
                if n == 0:
                    pe.wait_ge(s_scan, 1)
                    pe.wait_ge(s_Td, 16 * CH)
                vacant(pe, "Y", n)
                for q in range(4):
                    g = 4 * n + q
                    j, e = divmod(g, 2)
                    p = slice(64 * e, 64 * e + 64)
                    o, o2 = 512 * e + 128 * (q // 2), 512 * e + 256 + 16 * (q // 2)
                    for out, c0, c1, k0, k1 in ((slot("Y", n)[:, o:o + 128], 0, NC, 0, CH),
                                                (slot("Y", n)[0:NB, o2:o2 + 16], NC + 1, NC + 1 + NB, 0, 1)):
                        Uc = U[:, g, 0:NC] if c0 == 0 else U[:, g, NC:NC + NB]
                        mm(out, Uc, T5[:, g, 16 * k0:16 * k1], True, False, skip_group_check=True)
                        mm(out, Hs[p, 0, j, c0:c1], CLr[p, j, k0 + 1:k1 + 1, :].rearrange("p s h -> p (s h)"),
                           False, False, skip_group_check=True)
                        last = mm(out, Hs[p, 1, j, c0:c1], CLn[p, j, k0 + 1:k1 + 1, :].rearrange("p s h -> p (s h)"),
                                  False, True, skip_group_check=True)
                last.then_inc(full_sem("Y", n), 1)

            def s5t(n):
                pe.wait_ge(s_th, 2 * (n // 2 + 1))
                vacant(pe, "yT", n)
                if n < 4:
                    for q in range(8):
                        s, k = 2 * n + q // 4, q % 4
                        last = pe.transpose(slot("yT", n)[:, 128 * q:128 * q + 128], usb[:, s, 128 * k:128 * k + 128],
                                            ident)
                else:
                    for k in range(4):
                        last = pe.transpose(slot("yT", n)[:, NB * k:NB * k + NB],
                                            dvu[:, QKW + 128 * k:QKW + 128 * k + 128], ident[0:NB, 0:NB])
                last.then_inc(full_sem("yT", n), 1)

            def glu(n):
                pe.wait_ge(s_yT, 5)
                pe.wait_ge(s_wl, 16)
                vacant(pe, "z", n)
                if n < 4:
                    for a in range(2):
                        for k in range(4):
                            last = mm(slot("z", n)[:, 512 * a:512 * a + 512], wglu[:, k, 128 * n:128 * n + 128],
                                      yT[:, k, 512 * a:512 * a + 512], k == 0, k == 3)
                else:
                    for m in range(4):
                        for k in range(4):
                            last = mm(slot("z", n)[:, NB * m:NB * m + NB], wglu[:, k, 128 * m:128 * m + 128],
                                      yT[:, k, SEQ:TT], k == 0, k == 3)
                last.then_inc(full_sem("z", n), 1)

            def out_(i, a):
                if a == 0:
                    pe.wait_ge(s_wo, 16)
                    pe.wait_ge(s_mix, NT)
                    pe.wait_ge(s_mix2, 5)
                    if i == NT:
                        pe.wait_ge(s_dmix, 1)
                    vacant(pe, "o", i)
                for k in range(KD):
                    if i < NT:
                        last = mm(slot("o", i)[:, 512 * a:512 * a + 512], xm[:, k, 128 * i:128 * i + 128],
                                  wout[:, k, 512 * a:512 * a + 512], k == 0, k == KD - 1)
                    elif a == 0:
                        for c in range(4):
                            last = mm(slot("o", i)[32 * c:32 * c + NB, 0:256], xm[:, k, SEQ:TT],
                                      wout[:, k, 256 * c:256 * c + 256], k == 0, k == KD - 1)
                if i == NT and a == 0 or i < NT and a == 1:
                    last.then_inc(full_sem("o", i), 1)

            def ht(i):
                r = 128 if i < NT else NB
                pe.wait_ge(s_h2, i + 1)
                vacant(pe, "hT", i)
                for k in range(KD):
                    last = pe.transpose(slot("hT", i)[:, 128 * k:128 * k + r], h2[0:r, i % 2, 128 * k:128 * k + 128],
                                        ident[0:r, 0:r])
                last.then_inc(full_sem("hT", i), 1)
                pe.wait_ge(s_h2T, i + 1)
                vacant(pe, "r", i)
                for k in range(KD):
                    last = mm(slot("r", i)[0:r, 0:36], h2T[:, i % 2, k, 0:r], wr[:, k, :], k == 0, k == KD - 1)
                last.then_inc(full_sem("r", i), 1)

            def route():
                pe.wait_ge(s_oh, 2)
                vacant(pe, "rank")
                rank = slot("rank")[:, 0:320]
                mm(rank, consts[:, C_UP:C_UP + 128], OHs.rearrange("p t e -> p (t e)"), True, False,
                   skip_group_check=True)
                for i in range(NT + 1):
                    n = NT + 1 - i
                    last = mm(rank[:, 32 * (i + 1):320], ones, OHs[:, i:i + 1, :].to_broadcast([128, n, NE]),
                              False, i == NT, skip_group_check=True)
                last.then_inc(full_sem("rank"), 1)
                pe.wait_ge(s_lst, 1)
                vacant(pe, "ids")
                for c in range(2):
                    for i in range(NT + 1):
                        last = mm(slot("ids")[:, 0:MAXT], R[c][:, i, :], TO[c][:, i, :], c + i == 0,
                                  c == 1 and i == NT)
                last.then_inc(full_sem("ids"), 1)

            later = {"s5pt": s5pt, "s5k": s5k, "s5u": s5u, "s5x": s5x, "s5y": s5y, "s5t": s5t, "glu": glu,
                     "out": out_, "ht": ht, "route": route}
            todo = {"stats": stats, "dqkv": dqkv, "dprep": dprep, "u": u, "qk": qk_, "v": v, "qt": qt, "s": s,
                    "av": av, "ot": ot, "K": K, "m1": m1, "m2": m2, "m3": m3, "V": Vv, "pt": pt, "ov": ov, "dout": dout,
                    **later}
            for unit in PLAN:
                if unit[0] in todo:
                    todo[unit[0]](*unit[1:])

            def turn(q, v, first=False):
                pe.wait_ge(m_hg[v % 2], 32 * q + 16 * (v // 2 + 1))
                if not (first and v == 0):
                    pe.wait_ge(m_hT, 4 * q + v)
                for k in range(KD):
                    last = pe.transpose(W[0][:, 128 * k:128 * k + 128], hg[v % 2][:, 128 * k:128 * k + 128], ident)
                last.then_inc(m_T, 1)

            def gate_up(q, v):
                pe.wait_ge(m_w[v % 4], 32 * q + 32 * (v // 4 + 1))
                pe.wait_ge(m_hT, 4 * q + (v + 1))
                for k in range(KD):
                    last = mm(W[2][:, 512 * (v % 2):512 * (v % 2) + 512], hgT[v % 2][:, k, :], Wgu[v % 4][:, k, :],
                              k == 0, k == KD - 1)
                last.then_inc(m_gu, 1)

            def turn_he(q, v):
                pe.wait_ge(m_he, 4 * q + (v + 1))
                for k in range(2):
                    last = pe.transpose((SC, OD)[v % 2][:, 128 * k:128 * k + 128], he[v % 2][:, 128 * k:128 * k + 128],
                                        ident)
                last.then_inc(m_heT, 1)

            def down(q, v, first=False):
                pe.wait_ge(m_heS, 4 * q + (v + 1))
                if not (first and v == 0):
                    pe.wait_ge(m_ys, 4 * q + v)
                for a in range(2):
                    for k in range(2):
                        last = mm(W[1][:, 512 * a:512 * a + 512], heT_[v % 2][:, 128 * k:128 * k + 128],
                                  Wdn[v % 4][:, k, 512 * a:512 * a + 512], k == 0, k == 1)
                last.then_inc(m_y, 1)

            def step(q, v, first=False, last=False):
                turn_he(q, v)
                if not (last and v == 3):
                    gate_up(q, v + 1)
                if not (last and v >= 2):
                    turn(q, v + 2)
                down(q, v, first)

            pe.wait_ge(s_route, 1)
            n3 = pe.value_load(plan_t[0:1, MAXT + 1:MAXT + 2], min_val=NE // 4 - 1, max_val=MAXT // 4 - 1)
            turn(0, 0, first=True)
            gate_up(0, 0)
            turn(0, 1)
            for v in range(4):
                step(0, v, first=True)
            with pe.Fori(1, n3) as q:
                for v in range(4):
                    step(q, v)
            for v in range(4):
                step(n3, v, last=True)


def constants():
    c = np.zeros((128, C_END), np.float32)
    p = np.arange(128)
    c[:, C_ID:C_ID + 128] = np.eye(128)
    c[:, C_ONE:C_ONE + 128] = 1.0
    c[:, C_UP:C_UP + 128] = p[:, None] < p[None, :]
    c[:, C_MASK:C_MASK + 128] = np.where(p[None, :] <= p[:, None], 0.0, NEG)
    c[:, C_SUM:C_SUM + 128] = p[:, None] % 32 == p[None, :] % 32
    c[:, C_NEG:C_NEG + 64] = np.where(np.eye(8) > 0, 0.0, NEG).reshape(1, 64)
    for h in range(H):
        c[p % 32 == 2 * h, C_M0 + h] = 1.0
        c[p % 32 == 2 * h + 1, C_M1 + h] = 1.0
    c[:, C_I8:C_I8 + 8] = np.arange(8)
    c[:, C_I32:C_I32 + 32] = np.arange(32)
    c[:, C_THR:C_THR + 9] = 128.0 * np.arange(9)
    c[:, C_VAL:C_VAL + 9] = (p[:, None] + 128 * np.arange(9)) < TT
    c[:, C_TOK:C_TOK + 9] = (p[:, None] + 128 * np.arange(9)) * c[:, C_VAL:C_VAL + 9]
    c[:, C_TI:C_TI + 128] = np.arange(128)
    c[:, C_NH] = -0.5
    inv = np.float32(500000.0) ** (-np.arange(0, 16, 2, dtype=np.float32) / np.float32(16))
    pos = np.zeros((NT + 1, 128), np.float32)
    pos[:NT] = np.arange(SEQ).reshape(NT, 128)
    pos[NT] = NPAGE * PG
    ang = (pos[..., None] * inv).astype(np.float32)
    rope = np.concatenate([np.cos(ang), np.sin(ang)], -1).astype(np.float32).transpose(1, 0, 2)
    return c, np.ascontiguousarray(rope)


def pairs(a):
    return a.reshape(NP5, 2, P5, *a.shape[2:]).transpose(1, 2, 0, *range(3, a.ndim + 1)).reshape(128, NP5, *a.shape[2:])


def layout(x):
    xp, xs = x["x_prompt"][0], x["x_sample"][:, 0]
    xall = np.concatenate([xp, xs], 0)
    w_in = x["w_in"][0].reshape(KD, 128, PROJ)
    colw = np.zeros((128, 3 * KD), np.float32)
    colw[:, 0:KD] = x["ln1_g"][0].reshape(KD, 128).T
    colw[:, KD:2 * KD] = x["ln2_g"][0].reshape(KD, 128).T
    colw[:, 2 * KD] = x["subln_g"][0]
    lam = np.stack([x[f"lambda_{n}"][0] for n in ("q1", "k1", "q2", "k2")])
    consts, rope = constants()
    return {
        "consts": consts, "rope": rope, "colw": colw, "lamv": lam,
        "s5_par": np.stack([pairs(x["s5_a_re"][0]), pairs(x["s5_a_im"][0]),
                            pairs(np.repeat(x["s5_log_dt"][0][:, None], P5, 1))], 1),
        "s5_bc": np.stack([np.stack([pairs(x["s5_b_re"][0]), pairs(x["s5_b_im"][0])], 1),
                           np.stack([pairs(x["s5_c_re"][0].transpose(0, 2, 1)),
                                     pairs(x["s5_c_im"][0].transpose(0, 2, 1))], 1)], 1),
        "s5_h0": np.stack([pairs(x[f"state_s5_{n}"][0].transpose(1, 2, 0)) for n in ("re", "im")]),
        "dskip": x["s5_d"][0], "w_glu": x["w_glu"][0].reshape(4, 128, QKW).transpose(1, 0, 2),
        "b_glu": x["b_glu"][0].reshape(4, 128).T, "w_out": x["w_out"][0].reshape(KD, 128, D).transpose(1, 0, 2),
        "w_r": np.concatenate([x["w_router_group"][0],
                               x["w_router_expert"][0].transpose(1, 0, 2).reshape(D, NE)], 1)
        .reshape(KD, 128, 36).transpose(1, 0, 2),
        "b_r": np.concatenate([x["b_router_group"][0], x["b_router_expert"][0].reshape(NE)]),
        "w_gu": np.concatenate([x["w_gate"][0], x["w_up"][0]], 2).reshape(NE, KD, 128, 2 * DE).transpose(0, 2, 1, 3),
        "w_dn": x["w_down"][0].reshape(NE, 2, 128, D).transpose(0, 2, 1, 3), "ln_f_g": x["ln_f_g"],
        "x_p": x["x_prompt"].reshape(NT, 128, D), "x_s": x["x_sample"].reshape(NB, D),
        "page_table": x["page_table"].reshape(1, NB * NPAGE).astype(np.int32),
        "xT": xall.T.reshape(KD, 128, TT), "w_qkv": w_in[:, :, :3 * QKW], "w_u": w_in[:, :, 3 * QKW:],
        "cacheK": x["cache_k"][0].reshape(POOL, PG, H, 2, HD).transpose(0, 3, 4, 2, 1).reshape(POOL, 128, H * PG),
        "cacheV": x["cache_v"][0].reshape(POOL, PG, H * VD),
    }


SCRATCH = {"u_scratch": (128, CH, QKW), "h2_scratch": (TT, D), "y_scratch": (SLOTS, D)}
OUTS = {
    "y_p": (NT, 128, D), "y_s": (NB, D), "k_p": (NT, 128, QKW), "v_p": (NT, 128, QKW),
    "h_p": (2, 128, NP5), "k_s": (NB, QKW), "v_s": (NB, QKW), "h_s": (2, 128, NP5, NB),
}


def kernel(**inputs):
    from concourse import bacc
    from concourse.bass_utils import run_bass_kernel_spmd

    nc = bacc.Bacc("TRN2", target_bir_lowering=False, num_devices=1)
    arrays = {f"in_{k}": np.ascontiguousarray(v) for k, v in layout({k: np.asarray(v) for k, v in inputs.items()}).items()}
    io = {k[3:]: nc.dram_tensor(k, v.shape, mybir.dt.from_np(v.dtype), kind="ExternalInput").ap()
          for k, v in arrays.items()}
    for k, shape in OUTS.items():
        io[k] = nc.dram_tensor(f"out_{k}", shape, mybir.dt.float32, kind="ExternalOutput").ap()
    for k, shape in SCRATCH.items():
        io[k] = nc.dram_tensor(k, shape, mybir.dt.float32, kind="Internal").ap()
    hymba_step(nc, io)
    r = run_bass_kernel_spmd(nc, [arrays], core_ids=[0]).results[0]
    o = {k: np.asarray(r[f"out_{k}"]) for k in OUTS}

    def states(a):
        a = a.reshape(2, 2, P5, NP5, -1).transpose(0, 4, 3, 1, 2)
        return a.reshape(2, 1, -1, G5, P5)

    hp, hs = states(o["h_p"]), states(o["h_s"])
    return (o["y_p"].reshape(1, SEQ, D), o["y_s"].reshape(NB, 1, D),
            o["k_p"].reshape(1, 1, SEQ, 2 * H, HD), o["v_p"].reshape(1, 1, SEQ, H, VD), hp[0], hp[1],
            o["k_s"].reshape(1, NB, 1, 2 * H, HD), o["v_s"].reshape(1, NB, 1, H, VD), hs[0], hs[1])
```
